# Optimizing a Trainium2 kernel written in Bass

```python
import jax, jax.numpy as jnp
from jax import lax
import numpy as np
import math

D_MODEL = 1024
BATCH = 1
SEQ = 256
DEPTH = 2

HEAD_DIM = 64
N_HEADS = D_MODEL // HEAD_DIM
N_HEADS_A = N_HEADS // 2
N_KV_A = N_HEADS_A // 4
N_HEADS_B = N_HEADS - N_HEADS_A
D_FF = 4 * D_MODEL
GRID_W = 64
AXIAL_THETA = 10000.0
ROPE_THETA = 500000.0
ROPE_DIM = HEAD_DIM // 4
BLOCK_Q = 128
DILATED_PATTERNS = ((128, 1), (512, 4), (2048, 16))
NORM_EPS = 1e-6
NEG_INF = -1e30

QA_W = N_HEADS_A * HEAD_DIM
KVA_W = N_KV_A * HEAD_DIM
QB_W = N_HEADS_B * HEAD_DIM
IN_W = QA_W + 2 * KVA_W + 3 * QB_W
MIX_W = QA_W + QB_W


def rmsnorm(x, g):
    xf = x.astype(jnp.float32)
    y = xf * lax.rsqrt(jnp.mean(xf * xf, axis=-1, keepdims=True) + NORM_EPS)
    return (y * g.astype(jnp.float32)).astype(x.dtype)

def rope(x, pos, theta):
    half = x.shape[-1] // 2
    freqs = theta ** (-jnp.arange(half, dtype=jnp.float32) / half)
    ang = pos.astype(jnp.float32)[:, None] * freqs[None, :]
    cos = jnp.cos(ang)[:, None, :]
    sin = jnp.sin(ang)[:, None, :]
    xf = x.astype(jnp.float32)
    x1, x2 = xf[..., :half], xf[..., half:]
    return jnp.concatenate([x1 * cos - x2 * sin, x2 * cos + x1 * sin], axis=-1).astype(x.dtype)

def axial_rope(x, row_ids, col_ids):
    h = x.shape[-1] // 2
    return jnp.concatenate([rope(x[..., :h], row_ids, AXIAL_THETA),
                            rope(x[..., h:], col_ids, AXIAL_THETA)], axis=-1)

def partial_rope(x, pos):
    return jnp.concatenate([rope(x[..., :ROPE_DIM], pos, ROPE_THETA), x[..., ROPE_DIM:]], axis=-1)

def global_gqa(q, k, v):
    B, S, HA, hd = q.shape
    HKV = k.shape[2]
    G = HA // HKV
    nb = S // BLOCK_Q
    scale = hd ** -0.5
    qb = q.reshape(B, nb, BLOCK_Q, HKV, G, hd).transpose(1, 0, 2, 3, 4, 5)

    def one(qblk):
        s = jnp.einsum('bqkgd,bskd->bkgqs', qblk, k).astype(jnp.float32) * scale
        p = jax.nn.softmax(s, axis=-1).astype(v.dtype)
        return jnp.einsum('bkgqs,bskd->bqkgd', p, v)

    o = lax.map(one, qb)
    return o.transpose(1, 0, 2, 3, 4, 5).reshape(B, S, HA * hd)

def dilated_window_attention(q, k, v):
    B, S, H, hd = q.shape
    nb = S // BLOCK_Q
    scale = hd ** -0.5
    qb = q.reshape(B, nb, BLOCK_Q, H, hd).transpose(1, 0, 2, 3, 4)
    starts = jnp.arange(nb, dtype=jnp.int32) * BLOCK_Q

    def one(args):
        qblk, start = args
        pos = start + jnp.arange(BLOCK_Q, dtype=jnp.int32)
        outs, lses = [], []
        for window, dil in DILATED_PATTERNS:
            n_side = window // (2 * dil)
            offs = jnp.arange(-n_side, n_side + 1, dtype=jnp.int32) * dil
            idx = pos[:, None] + offs[None, :]
            valid = (idx >= 0) & (idx < S)
            idxc = jnp.clip(idx, 0, S - 1)
            kg = k[:, idxc]
            vg = v[:, idxc]
            s = jnp.einsum('bqhd,bqjhd->bhqj', qblk, kg).astype(jnp.float32) * scale
            s = jnp.where(valid[None, None], s, NEG_INF)
            lse = jax.nn.logsumexp(s, axis=-1, keepdims=True)
            p = jnp.exp(s - lse).astype(v.dtype)
            outs.append(jnp.einsum('bhqj,bqjhd->bqhd', p, vg).astype(jnp.float32))
            lses.append(lse[..., 0])
        wts = jax.nn.softmax(jnp.stack(lses, axis=0), axis=0)
        o = jnp.einsum('pbhq,pbqhd->bqhd', wts, jnp.stack(outs, axis=0))
        return o.astype(v.dtype)

    o = lax.map(one, (qb, starts))
    return o.transpose(1, 0, 2, 3, 4).reshape(B, S, H * hd)

def hybrid_layer(x, n1, w_in, q_norm, k_norm, out_norm_a, out_norm_b, w_out,
                 n2, w_mlp_in, w_mlp_out, row_ids, col_ids, pos):
    B, S, _ = x.shape
    h = rmsnorm(x, n1)
    proj = h @ w_in
    cuts = np.cumsum([QA_W, KVA_W, KVA_W, QB_W, QB_W]).tolist()
    qa, ka, va, qb, kb, vb = jnp.split(proj, cuts, axis=-1)

    qa = qa.reshape(B, S, N_HEADS_A, HEAD_DIM)
    ka = ka.reshape(B, S, N_KV_A, HEAD_DIM)
    va = va.reshape(B, S, N_KV_A, HEAD_DIM)
    qa = axial_rope(rmsnorm(qa, q_norm), row_ids, col_ids)
    ka = axial_rope(rmsnorm(ka, k_norm), row_ids, col_ids)
    ya = global_gqa(qa, ka, va)

    qb = partial_rope(qb.reshape(B, S, N_HEADS_B, HEAD_DIM), pos)
    kb = partial_rope(kb.reshape(B, S, N_HEADS_B, HEAD_DIM), pos)
    vb = vb.reshape(B, S, N_HEADS_B, HEAD_DIM)
    yb = dilated_window_attention(qb, kb, vb)

    y = jnp.concatenate([rmsnorm(ya, out_norm_a), rmsnorm(yb, out_norm_b)], axis=-1)
    x = x + y @ w_out

    u = rmsnorm(x, n2) @ w_mlp_in
    u = jnp.square(jax.nn.relu(u))
    return x + u @ w_mlp_out

def first_inputs(seed: int = 0) -> dict:
    key = jax.random.key(seed)
    ks = jax.random.split(key, 13)
    f32 = jnp.float32

    def gain(k, shape):
        return 1.0 + 0.02 * jax.random.normal(k, shape, f32)

    return {
        "x": jax.random.normal(ks[0], (BATCH, SEQ, D_MODEL), f32),
        "norm1": gain(ks[1], (DEPTH, D_MODEL)),
        "w_in": jax.random.normal(ks[2], (DEPTH, D_MODEL, IN_W), f32) * D_MODEL ** -0.5,
        "q_norm": gain(ks[3], (DEPTH, HEAD_DIM)),
        "k_norm": gain(ks[4], (DEPTH, HEAD_DIM)),
        "out_norm_a": gain(ks[5], (DEPTH, QA_W)),
        "out_norm_b": gain(ks[6], (DEPTH, QB_W)),
        "w_out": jax.random.normal(ks[7], (DEPTH, MIX_W, D_MODEL), f32) * MIX_W ** -0.5,
        "norm2": gain(ks[8], (DEPTH, D_MODEL)),
        "w_mlp_in": jax.random.normal(ks[9], (DEPTH, D_MODEL, D_FF), f32) * D_MODEL ** -0.5,
        "w_mlp_out": jax.random.normal(ks[10], (DEPTH, D_FF, D_MODEL), f32) * D_FF ** -0.5,
        "final_norm": gain(ks[11], (D_MODEL,)),
    }

def first_block(x, norm1, w_in, q_norm, k_norm, out_norm_a, out_norm_b, w_out,
              norm2, w_mlp_in, w_mlp_out, final_norm):
    S = x.shape[1]
    rows = S // GRID_W
    row_ids = jnp.repeat(jnp.arange(rows, dtype=jnp.int32), GRID_W)
    col_ids = jnp.tile(jnp.arange(GRID_W, dtype=jnp.int32), rows)
    pos = jnp.arange(S, dtype=jnp.int32)
    for l in range(DEPTH):
        x = hybrid_layer(x, norm1[l], w_in[l], q_norm[l], k_norm[l],
                         out_norm_a[l], out_norm_b[l], w_out[l], norm2[l],
                         w_mlp_in[l], w_mlp_out[l], row_ids, col_ids, pos)
    return rmsnorm(x, final_norm)


D_MIX = D_MODEL
A_HEADS = (3 * D_MIX) // (8 * HEAD_DIM)
A_WIDTH = A_HEADS * HEAD_DIM
IDX_HEADS = 4
IDX_DIM = HEAD_DIM
DSA_TOPK_MAX = 256
B_HEADS = D_MIX // (4 * HEAD_DIM)
B_QK_DIM = HEAD_DIM // 2
B_WIDTH = B_HEADS * HEAD_DIM
SUBLN_EPS = 1e-5
C_HEADS = A_HEADS
C_WIDTH = C_HEADS * HEAD_DIM
MOBA_BLOCK = 256
MOBA_TOPK = 3
ROPE_FRACTION = 4
MAX_POS_OFFSET = 1024
Q_BLOCK = 128
MOBA_Q_BLOCK = 32
D_FF_2 = 2816
N_EXPERTS = 8
TOP_K_EXPERTS = 2
D_FF_EXPERT = 2816
EPS = 1e-6
IN_COLS = (A_WIDTH, HEAD_DIM, HEAD_DIM, IDX_HEADS * IDX_DIM, IDX_DIM, IDX_HEADS,
           2 * B_HEADS * B_QK_DIM, 2 * B_HEADS * B_QK_DIM, B_WIDTH,
           C_WIDTH, C_WIDTH, C_WIDTH)
D_IN = sum(IN_COLS)


F32 = jnp.float32

def _split_points():
    pts, acc = [], 0
    for w in IN_COLS[:-1]:
        acc += w
        pts.append(acc)
    return pts

def rms_norm(x, g, eps=EPS):
    xf = x.astype(F32)
    y = xf * lax.rsqrt(jnp.mean(xf * xf, axis=-1, keepdims=True) + eps)
    return (y * g.astype(F32)).astype(x.dtype)

def rope_tables(positions, dim):
    rot = dim // ROPE_FRACTION
    inv = 1.0 / (ROPE_THETA ** (np.arange(0, rot, 2, dtype=np.float32) / rot))
    ang = positions.astype(F32)[..., None] * jnp.asarray(inv, F32)
    return jnp.cos(ang), jnp.sin(ang)

def partial_rope_2(x, cos, sin):
    half = cos.shape[-1]
    xf = x.astype(F32)
    x1, x2, xp = xf[..., :half], xf[..., half:2 * half], xf[..., 2 * half:]
    c, s = cos[:, :, None, :], sin[:, :, None, :]
    return jnp.concatenate([x1 * c - x2 * s, x2 * c + x1 * s, xp], axis=-1).astype(x.dtype)

def dsa_attention(q, k, v, q_idx, k_idx, w_idx):
    B, S, H, dh = q.shape
    k_top = min(DSA_TOPK_MAX, S // 4)
    key_pos = jnp.arange(S)
    kf_idx = k_idx.astype(F32)
    gather = jax.vmap(lambda zz, ii: zz[ii])

    def one_block(i):
        t0 = i * Q_BLOCK
        t = t0 + jnp.arange(Q_BLOCK)
        qb = lax.dynamic_slice_in_dim(q, t0, Q_BLOCK, axis=1).astype(F32)
        qib = lax.dynamic_slice_in_dim(q_idx, t0, Q_BLOCK, axis=1).astype(F32)
        wb = lax.dynamic_slice_in_dim(w_idx, t0, Q_BLOCK, axis=1).astype(F32) * IDX_HEADS ** -0.5
        rel = jax.nn.relu(jnp.einsum('bqhd,bsd->bqhs', qib, kf_idx) * IDX_DIM ** -0.5)
        score_idx = jnp.einsum('bqh,bqhs->bqs', wb, rel)
        causal = key_pos[None, :] <= t[:, None]
        score_idx = jnp.where(causal[None], score_idx, -jnp.inf)
        _, sel = lax.top_k(score_idx, k_top)
        valid = sel <= t[None, :, None]
        kg = gather(k, sel).astype(F32)
        vg = gather(v, sel).astype(F32)
        s = jnp.einsum('bqhd,bqkd->bqhk', qb, kg) * dh ** -0.5
        s = jnp.where(valid[:, :, None, :], s, -jnp.inf)
        p = jax.nn.softmax(s, axis=-1)
        return jnp.einsum('bqhk,bqkd->bqhd', p, vg).astype(q.dtype)

    out = lax.map(one_block, jnp.arange(S // Q_BLOCK))
    return jnp.moveaxis(out, 0, 1).reshape(B, S, H * dh)

def diff_attention(q, k, v, lam, g_sub, lam_init):
    B, S, H, _, dq = q.shape
    dv = v.shape[-1]
    key_pos = jnp.arange(S)
    kf = k.astype(F32)
    vf = v.astype(F32)

    def one_block(i):
        t0 = i * Q_BLOCK
        t = t0 + jnp.arange(Q_BLOCK)
        qb = lax.dynamic_slice_in_dim(q, t0, Q_BLOCK, axis=1).astype(F32)
        s = jnp.einsum('bqhcd,bshcd->bhcqs', qb, kf) * dq ** -0.5
        causal = key_pos[None, :] <= t[:, None]
        p = jax.nn.softmax(jnp.where(causal, s, -jnp.inf), axis=-1)
        a = p[:, :, 0] - lam * p[:, :, 1]
        return jnp.einsum('bhqs,bshd->bqhd', a, vf)

    o = lax.map(one_block, jnp.arange(S // Q_BLOCK))
    o = jnp.moveaxis(o, 0, 1).reshape(B, S, H, dv)
    o = rms_norm(o, g_sub, SUBLN_EPS) * (1.0 - lam_init)
    return o.reshape(B, S, H * dv).astype(v.dtype)

def moba_attention(q, k, v):
    B, S, H, dh = q.shape
    nb = -(-S // MOBA_BLOCK)
    n_sel = min(MOBA_TOPK, nb - 1)
    pad = nb * MOBA_BLOCK - S

    def to_blocks(z):
        z = jnp.pad(z, ((0, 0), (0, pad), (0, 0), (0, 0)))
        return z.reshape(B, nb, MOBA_BLOCK, H, dh).transpose(0, 3, 1, 2, 4)

    kb = to_blocks(k)
    vb = to_blocks(v)
    k_mean = jnp.mean(kb.astype(F32), axis=3)
    qh = q.transpose(0, 2, 1, 3)
    scale = dh ** -0.5
    in_block = jnp.arange(MOBA_BLOCK)
    gather = jax.vmap(jax.vmap(lambda zz, ii: zz[ii]))

    def one_block(i):
        t0 = i * MOBA_Q_BLOCK
        t = t0 + jnp.arange(MOBA_Q_BLOCK)
        own = t0 // MOBA_BLOCK
        qb = lax.dynamic_slice_in_dim(qh, t0, MOBA_Q_BLOCK, axis=2).astype(F32)
        k_own = lax.dynamic_index_in_dim(kb, own, axis=2, keepdims=False).astype(F32)
        v_own = lax.dynamic_index_in_dim(vb, own, axis=2, keepdims=False).astype(F32)
        s_own = jnp.einsum('bhqd,bhkd->bhqk', qb, k_own) * scale
        s_own = jnp.where((own * MOBA_BLOCK + in_block)[None, :] <= t[:, None], s_own, -jnp.inf)
        if n_sel == 0:
            p_own = jax.nn.softmax(s_own, axis=-1)
            return jnp.einsum('bhqk,bhkd->bhqd', p_own, v_own).astype(q.dtype)
        n_past = t // MOBA_BLOCK
        gate = jnp.einsum('bhqd,bhnd->bhqn', qb, k_mean)
        gate = jnp.where(jnp.arange(nb)[None, :] < n_past[:, None], gate, -jnp.inf)
        _, sel = lax.top_k(gate, n_sel)
        kg = gather(kb, sel).astype(F32)
        vg = gather(vb, sel).astype(F32)
        s_sel = jnp.einsum('bhqd,bhqnkd->bhqnk', qb, kg) * scale
        sel_ok = jnp.arange(n_sel)[None, :] < n_past[:, None]
        s_sel = jnp.where(sel_ok[None, None, :, :, None], s_sel, -jnp.inf)
        n_keys = n_sel * MOBA_BLOCK
        s_all = jnp.concatenate([s_sel.reshape(B, H, MOBA_Q_BLOCK, n_keys), s_own], axis=-1)
        p = jax.nn.softmax(s_all, axis=-1)
        p_sel = p[..., :n_keys].reshape(B, H, MOBA_Q_BLOCK, n_sel, MOBA_BLOCK)
        p_own = p[..., n_keys:]
        o = jnp.einsum('bhqnk,bhqnkd->bhqd', p_sel, vg) + jnp.einsum('bhqk,bhkd->bhqd', p_own, v_own)
        return o.astype(q.dtype)

    out = lax.map(one_block, jnp.arange(S // MOBA_Q_BLOCK))
    return out.transpose(1, 0, 3, 2, 4).reshape(B, S, H * dh)

def hybrid_mixer(h, cos64, sin64, cos32, sin32, w_in, w_out, lam_vec, g_sub, lam_init):
    B, S, _ = h.shape
    proj = jnp.einsum('bsd,dn->bsn', h, w_in)
    (q_a, k_a, v_a, q_i, k_i, w_i, q_b, k_b, v_b, q_c, k_c, v_c) = jnp.split(proj, _split_points(), axis=-1)
    q_a = partial_rope_2(q_a.reshape(B, S, A_HEADS, HEAD_DIM), cos64, sin64)
    k_a = partial_rope_2(k_a.reshape(B, S, 1, HEAD_DIM), cos64, sin64)[:, :, 0]
    q_i = partial_rope_2(q_i.reshape(B, S, IDX_HEADS, IDX_DIM), cos64, sin64)
    k_i = partial_rope_2(k_i.reshape(B, S, 1, IDX_DIM), cos64, sin64)[:, :, 0]
    y_a = dsa_attention(q_a, k_a, v_a, q_i, k_i, w_i)
    q_b = partial_rope_2(q_b.reshape(B, S, 2 * B_HEADS, B_QK_DIM), cos32, sin32).reshape(B, S, B_HEADS, 2, B_QK_DIM)
    k_b = partial_rope_2(k_b.reshape(B, S, 2 * B_HEADS, B_QK_DIM), cos32, sin32).reshape(B, S, B_HEADS, 2, B_QK_DIM)
    v_b = v_b.reshape(B, S, B_HEADS, HEAD_DIM)
    lf = lam_vec.astype(F32)
    lam = jnp.exp(jnp.sum(lf[0] * lf[1])) - jnp.exp(jnp.sum(lf[2] * lf[3])) + lam_init
    y_b = diff_attention(q_b, k_b, v_b, lam, g_sub, lam_init)
    q_c = partial_rope_2(q_c.reshape(B, S, C_HEADS, HEAD_DIM), cos64, sin64)
    k_c = partial_rope_2(k_c.reshape(B, S, C_HEADS, HEAD_DIM), cos64, sin64)
    y_c = moba_attention(q_c, k_c, v_c.reshape(B, S, C_HEADS, HEAD_DIM))
    y = jnp.concatenate([y_a, y_b, y_c], axis=-1)
    return jnp.einsum('bsm,md->bsd', y, w_out)

def swiglu(h, w_gate, w_up, w_down):
    a = jnp.einsum('bsd,df->bsf', h, w_gate)
    u = jnp.einsum('bsd,df->bsf', h, w_up)
    return jnp.einsum('bsf,fd->bsd', jax.nn.silu(a) * u, w_down)

def moe_swiglu(h, w_router, w_gate, w_up, w_down):
    logits = jnp.einsum('bsd,de->bse', h.astype(F32), w_router.astype(F32))
    top_val, top_idx = lax.top_k(logits, TOP_K_EXPERTS)
    top_w = jax.nn.softmax(top_val, axis=-1)
    combine = jnp.sum(jax.nn.one_hot(top_idx, N_EXPERTS, dtype=F32) * top_w[..., None], axis=-2)
    out = jnp.zeros_like(h)
    for e in range(N_EXPERTS):
        out = out + combine[..., e:e + 1].astype(h.dtype) * swiglu(h, w_gate[e], w_up[e], w_down[e])
    return out

def second_inputs(seed: int = 0) -> dict:
    key = jax.random.key(seed)
    ks = jax.random.split(key, 20)
    n_dense = (DEPTH + 1) // 2
    n_moe = DEPTH // 2

    def nrm(k, shape, scale):
        return jax.random.normal(k, shape, F32) * scale

    x = nrm(ks[0], (BATCH, SEQ, D_MODEL), 1.0)
    c = nrm(ks[1], (BATCH, D_MODEL), 1.0)
    offset = jax.random.randint(ks[2], (BATCH, 1), 0, MAX_POS_OFFSET, dtype=jnp.int32)
    positions = offset + jnp.arange(SEQ, dtype=jnp.int32)[None, :]
    w_in = nrm(ks[3], (DEPTH, D_MODEL, D_IN), D_MODEL ** -0.5)
    w_out = nrm(ks[4], (DEPTH, D_MIX, D_MODEL), D_MIX ** -0.5)
    diff_lambda = nrm(ks[5], (DEPTH, 4, B_QK_DIM), 0.1)
    diff_subln = 1.0 + nrm(ks[6], (DEPTH, HEAD_DIM), 0.01)
    w_ada = nrm(ks[7], (DEPTH, D_MODEL, 6 * D_MODEL), 0.5 * D_MODEL ** -0.5)
    b_ada = nrm(ks[8], (DEPTH, 6 * D_MODEL), 0.01)
    g_attn = 1.0 + nrm(ks[9], (DEPTH, D_MODEL), 0.01)
    g_ffn = 1.0 + nrm(ks[10], (DEPTH, D_MODEL), 0.01)
    w_ff_gate = nrm(ks[11], (n_dense, D_MODEL, D_FF_2), D_MODEL ** -0.5)
    w_ff_up = nrm(ks[12], (n_dense, D_MODEL, D_FF_2), D_MODEL ** -0.5)
    w_ff_down = nrm(ks[13], (n_dense, D_FF_2, D_MODEL), D_FF_2 ** -0.5)
    w_router = nrm(ks[14], (n_moe, D_MODEL, N_EXPERTS), D_MODEL ** -0.5)
    w_exp_gate = nrm(ks[15], (n_moe, N_EXPERTS, D_MODEL, D_FF_EXPERT), D_MODEL ** -0.5)
    w_exp_up = nrm(ks[16], (n_moe, N_EXPERTS, D_MODEL, D_FF_EXPERT), D_MODEL ** -0.5)
    w_exp_down = nrm(ks[17], (n_moe, N_EXPERTS, D_FF_EXPERT, D_MODEL), D_FF_EXPERT ** -0.5)
    g_final = 1.0 + nrm(ks[18], (D_MODEL,), 0.01)
    return {'x': x, 'c': c, 'positions': positions, 'w_in': w_in, 'w_out': w_out,
            'diff_lambda': diff_lambda, 'diff_subln': diff_subln, 'w_ada': w_ada, 'b_ada': b_ada,
            'g_attn': g_attn, 'g_ffn': g_ffn, 'w_ff_gate': w_ff_gate, 'w_ff_up': w_ff_up,
            'w_ff_down': w_ff_down, 'w_router': w_router, 'w_exp_gate': w_exp_gate,
            'w_exp_up': w_exp_up, 'w_exp_down': w_exp_down, 'g_final': g_final}

def second_block(x, c, positions, w_in, w_out, diff_lambda, diff_subln, w_ada, b_ada,
              g_attn, g_ffn, w_ff_gate, w_ff_up, w_ff_down, w_router, w_exp_gate,
              w_exp_up, w_exp_down, g_final):
    cos64, sin64 = rope_tables(positions, HEAD_DIM)
    cos32, sin32 = rope_tables(positions, B_QK_DIM)
    c_act = jax.nn.silu(c)
    for layer in range(DEPTH):
        mod = jnp.einsum('bd,dn->bn', c_act, w_ada[layer]) + b_ada[layer]
        sh1, sc1, gt1, sh2, sc2, gt2 = [m[:, None, :] for m in jnp.split(mod, 6, axis=-1)]
        lam_init = 0.8 - 0.6 * math.exp(-0.3 * layer)
        h = rms_norm(x, g_attn[layer]) * (1.0 + sc1) + sh1
        y = hybrid_mixer(h, cos64, sin64, cos32, sin32, w_in[layer], w_out[layer],
                         diff_lambda[layer], diff_subln[layer], lam_init)
        x = x + gt1 * y
        h = rms_norm(x, g_ffn[layer]) * (1.0 + sc2) + sh2
        j = layer // 2
        if layer % 2 == 0:
            f = swiglu(h, w_ff_gate[j], w_ff_up[j], w_ff_down[j])
        else:
            f = moe_swiglu(h, w_router[j], w_exp_gate[j], w_exp_up[j], w_exp_down[j])
        x = x + gt2 * f
    return rms_norm(x, g_final)


def setup_inputs(seed=0):
    out = dict(first_inputs(seed))
    for name, value in second_inputs(seed + 1).items():
        if name != "x":
            out[name + "_2"] = value
    return out


def reference(
    x, norm1, w_in, q_norm, k_norm, out_norm_a, out_norm_b, w_out, norm2, w_mlp_in, w_mlp_out,
    final_norm, c_2, positions_2, w_in_2, w_out_2, diff_lambda_2, diff_subln_2, w_ada_2,
    b_ada_2, g_attn_2, g_ffn_2, w_ff_gate_2, w_ff_up_2, w_ff_down_2, w_router_2, w_exp_gate_2,
    w_exp_up_2, w_exp_down_2, g_final_2,
):
    x = first_block(
        x, norm1, w_in, q_norm, k_norm, out_norm_a, out_norm_b, w_out, norm2, w_mlp_in,
        w_mlp_out, final_norm,
    )
    return second_block(
        x, c_2, positions_2, w_in_2, w_out_2, diff_lambda_2, diff_subln_2, w_ada_2, b_ada_2,
        g_attn_2, g_ffn_2, w_ff_gate_2, w_ff_up_2, w_ff_down_2, w_router_2, w_exp_gate_2,
        w_exp_up_2, w_exp_down_2, g_final_2,
    )


_drawn_inputs = setup_inputs


def setup_inputs(seed=0):
    import zlib

    import numpy as np

    out = dict(_drawn_inputs(seed))
    spreads = {}
    factors = {'q_norm': 4.516,
     'k_norm': 4.526,
     'out_norm_a': 2.868,
     'out_norm_b': 3.338,
     'diff_lambda_2': 8.0,
     'diff_subln_2': 8.0,
     'b_ada_2': 2.916,
     'g_attn_2': 8.0,
     'g_ffn_2': 7.713,
     'g_final_2': 5.496}
    for name, (base, spread) in spreads.items():
        noise = np.random.default_rng([zlib.crc32(name.encode()), seed]).standard_normal(out[name].shape)
        drawn = base * np.exp(spread * noise) if base else spread * noise
        out[name] = __import__('jax').numpy.asarray(drawn.astype(out[name].dtype))
    for name, factor in factors.items():
        out[name] = (out[name] * factor).astype(out[name].dtype)
    return out
```

```python
from contextlib import ExitStack

import numpy as np

import concourse.bass as bass
from concourse import mybir

F32 = mybir.dt.float32
F32R = mybir.dt.float32r
I32 = mybir.dt.int32
ALU = mybir.AluOpType
ACT = mybir.ActivationFunctionType
AX = mybir.AxisListType

P = 128
D = 1024
SEQ = 256
TT = SEQ // P
KC = D // P
DEPTH = 2
HD = 64
HA, KVA, HB = 8, 2, 8
QA1, KA1, VA1 = 0, HA * HD, (HA + KVA) * HD
QB1 = VA1 + KVA * HD
KB1, VB1 = QB1 + HB * HD, QB1 + 2 * HB * HD
IN1 = VB1 + HB * HD
FF1 = 4 * D
A2, I2, B2, C2 = 6, 4, 4, 6
QA2 = 0
KA2 = QA2 + A2 * HD
VA2 = KA2 + HD
QI2 = VA2 + HD
KI2 = QI2 + I2 * HD
WI2 = KI2 + HD
QB2 = WI2 + I2
KB2 = QB2 + B2 * HD
VB2 = KB2 + B2 * HD
QC2 = VB2 + B2 * HD
KC2 = QC2 + C2 * HD
VC2 = KC2 + C2 * HD
IN2 = VC2 + C2 * HD
FF2 = 2816
NE = 8
TOPK = SEQ // 4
ADA = 6 * D
EPS, SUB_EPS = 1e-6, 1e-5
MASKED, TAKEN = -1e30, -3e38

TILE = 2048
RAW = 4
MORE_RAW = 6
FREE_RAW, FREE_SPLIT, FREE_BANKS = 6, 4, 4
OVERFLOW = True
V_LOADS = 4 * DEPTH + 2
R_LOADS = 4 + 2 * DEPTH + 1
SPLIT = 4
COL = 512
PIECE = 2048
NPIECE = ADA // PIECE
F_UP = 512
F_GATED = 256

_at = {}
_n = 0
for _name, _w in (("ident", P), ("ones", P), ("before", P), ("iota", P), ("dilated", TT * SEQ), ("causal", TT * SEQ),
                  ("ax_cos", TT * HD), ("ax_sin", TT * HD), ("pr_cos", TT * 16), ("pr_sin", TT * 16),
                  ("inv64", 8), ("inv32", 4), ("earlier", NE * NE)):
    _at[_name] = (_n, _w)
    _n += _w
CONST_W = _n

G_NORM1, G_NORM2, G_OUT, G_ATTN, G_FFN, G_C = 0, 16, 32, 48, 64, 80
NG = 88

S_RAW = RAW * TILE
X_QKT = 0
X_SM, X_P, X_PT = 4352, 5376, 6400
X_SELW = 7424
X_HTF = 6144
X_ADA, X_ACT, X_ACT2 = 0, 6144, 7168
X_MACT, X_MACT2, X_G, X_GW, X_GT, X_YE, X_HGF = 4096, 4352, 4608, 4864, 5120, 5376, 6400
SCRATCH = 8192
X_LAM, X_ANG, X_WR, X_POS, X_LAMS = 512, 1024, 1280, 1408, 1424
C_RT = TT * IN2


def constants():
    f = np.float32
    out = np.zeros((P, CONST_W), f)

    def put(name, a):
        o, w = _at[name]
        out[:, o:o + w] = np.asarray(a, f).reshape(-1, w) if np.ndim(a) > 1 else np.asarray(a, f)[None, :]

    def by_token(a):
        return a.reshape(TT, P, -1).transpose(1, 0, 2).reshape(P, -1)

    put("ident", np.eye(P))
    put("ones", np.ones((P, P)))
    put("before", np.triu(np.ones((P, P)), 1))
    put("iota", np.arange(P))
    q, k = np.arange(SEQ)[:, None], np.arange(SEQ)[None, :]
    off = np.abs(q - k)
    times = np.zeros((SEQ, SEQ))
    for window, dil in ((128, 1), (512, 4), (2048, 16)):
        times += (off % dil == 0) & (off // dil <= window // (2 * dil))
    bias = np.where(times > 0, np.log(np.maximum(times, 1)) * HD ** 0.5, MASKED)
    put("dilated", by_token(bias))
    put("causal", by_token(np.where(k <= q, 0.0, MASKED)))

    def rope(pos, half, theta):
        freqs = (f(theta) ** (-np.arange(half, dtype=f) / f(half))).astype(f)
        ang = pos.astype(f)[:, None] * freqs[None, :]
        c, s = np.cos(ang), np.sin(ang)
        return np.concatenate([c, c], 1), np.concatenate([-s, s], 1)

    pos = np.arange(SEQ)
    rc, rs = rope(pos // 64, 16, 10000.0)
    cc, cs = rope(pos % 64, 16, 10000.0)
    put("ax_cos", by_token(np.concatenate([rc, cc], 1)))
    put("ax_sin", by_token(np.concatenate([rs, cs], 1)))
    pc, ps = rope(pos, 8, 500000.0)
    put("pr_cos", by_token(pc))
    put("pr_sin", by_token(ps))
    put("inv64", 1.0 / (500000.0 ** (np.arange(0, 16, 2, dtype=f) / 16)))
    put("inv32", 1.0 / (500000.0 ** (np.arange(0, 8, 2, dtype=f) / 8)))
    put("earlier", (np.arange(NE)[None, :] < np.arange(NE)[:, None]).reshape(-1))
    return out


class Tiles:

    def __init__(self):
        self.t, self.i, self.start = 0, 0, 0
        self.loads = [0] * MORE_RAW
        self.raw, self.split = RAW, SPLIT

    def stage(self, raw=RAW, split=SPLIT):
        self.i, self.raw, self.split, self.start = 0, raw, split, self.t

    def next(self):
        s = self.i % self.raw
        self.loads[s] = self.loads[s] + 1
        got = (self.t, s, self.i % self.split, self.loads[s])
        self.t = self.t + 1
        self.i += 1
        return got

    def enter(self, it, n):
        per = [sum((self.i + k) % self.raw == s for k in range(n)) for s in range(MORE_RAW)]
        self.kept = (self.t, self.i, list(self.loads), n, per)
        self.t = self.t + it * n
        self.loads = [c + it * m if m else c for c, m in zip(self.loads, per)]

    def leave(self, steps):
        t, i, loads, n, per = self.kept
        self.t, self.i = t + steps * n, i + steps * n
        self.loads = [c + steps * m for c, m in zip(loads, per)]


def build(nc, A, out, stop=None):
    ctx = ExitStack()
    with ctx:
        def sb(name, shape, dt=F32):
            return ctx.enter_context(nc.sbuf_tensor(name, shape, dt))

        def sem(name):
            return ctx.enter_context(nc.semaphore(name))

        x = sb("x", [P, TT, D])
        h = sb("h", [P, TT, D])
        hT_hi = sb("hT_hi", [P, KC, SEQ], F32R)
        hT_lo = sb("hT_lo", [P, KC, SEQ], F32R)
        big = sb("big", [P, ADA])
        slab = sb("slab", [P, S_RAW + SCRATCH])
        w_hi = sb("w_hi", [P, SPLIT, TILE], F32R)
        w_lo = sb("w_lo", [P, SPLIT, TILE], F32R)
        hid_hi = sb("hid_hi", [P, 4, SEQ], F32R)
        hid_lo = sb("hid_lo", [P, 4, SEQ], F32R)
        const = sb("const", [P, CONST_W])
        rowg = sb("rowg", [P, D])
        gcol = sb("gcol", [P, NG])
        modcol = sb("modcol", [P, DEPTH, 48])
        modg = sb("modg", [P, DEPTH, 2, KC])
        qkg = sb("qkg", [P, DEPTH, 2, HD])
        subg = sb("subg", [P, DEPTH, HD])
        nlam = sb("nlam", [P, DEPTH])
        posi = sb("posi", [P, TT], I32)
        rope64 = sb("rope64", [P, 2, TT, 16])
        rope32 = sb("rope32", [P, 2, TT, 8])
        wr_hi = sb("wr_hi", [P, KC, NE], F32R)
        wr_lo = sb("wr_lo", [P, KC, NE], F32R)
        stat = sb("stat", [P, 3, 20])
        att = sb("att", [P, 4, 20, TT])
        half = sb("half", [P, 1])
        flag = sb("flag", [1, 1], I32)

        def k_(name, *shape):
            o, w = _at[name]
            a = const[:, o:o + w]
            if len(shape) == 2:
                a = a.rearrange("p (a b) -> p a b", a=shape[0])
            return a

        ident, ones, before, iota = k_("ident"), k_("ones"), k_("before"), k_("iota")

        def scr(o, n, *shape):
            a = slab[:, S_RAW + o:S_RAW + o + n]
            if len(shape) == 2:
                a = a.rearrange("p (a b) -> p a b", a=shape[0])
            if len(shape) == 3:
                a = a.rearrange("p (a b c) -> p a b c", a=shape[0], b=shape[1])
            return a

        def raw(s):
            return slab[:, s * TILE:(s + 1) * TILE]

        csilu = sb("csilu", [P, KC])
        lam = scr(X_LAM, DEPTH * 4 * 32, DEPTH, 4 * 32)
        ang = scr(X_ANG, 4 * TT * 12, 4, TT * 12)
        posf = scr(X_POS, TT)
        lams = scr(X_LAMS, 4 * DEPTH)
        wr = scr(X_WR, KC * NE, KC, NE)
        rt = big[:, C_RT:C_RT + 14 * TT * NE].rearrange("p (i t e) -> p i t e", i=14, t=TT)
        prj = big[:, 0:TT * IN2].rearrange("p (t n) -> p t n", t=TT)
        htf = scr(X_HTF, KC * SEQ, KC, SEQ)
        qkT = scr(X_QKT, 17 * SEQ, 17, SEQ)
        bank = [ctx.enter_context(nc.psum_tensor(f"bank{i}", [P, COL], F32)) for i in range(8)]
        gates = nc.dram_tensor("gates", (DEPTH, P, 2, D), F32, kind="Internal").ap()

        w_loaded = [sem(f"w_loaded{i}") for i in range(6)]
        hi_done, lo_done = sem("hi_done"), sem("lo_done")
        w_used = sem("w_used")
        c_in, r_in, v_in, rout_in = sem("c_in"), sem("r_in"), sem("v_in"), sem("rout_in")
        x_in = sem("x_in")
        row_in, row_used = sem("row_in"), sem("row_used")
        gc_t, gc_d = sem("gc_t"), sem("gc_d")
        silu_c = sem("silu_c")
        sin_a, sin_d, sin_h = sem("sin_a"), sem("sin_d"), sem("sin_h")
        lam_s, lam_e, lam_d = sem("lam_s"), sem("lam_e"), sem("lam_d")
        half_d = sem("half_d")
        ss_done, ms_done, rstd_done, xn_done = sem("ss_done"), sem("ms_done"), sem("rstd_done"), sem("xn_done")
        tp_done, tpe_done, hh_done, hl_done = sem("tp_done"), sem("tpe_done"), sem("hh_done"), sem("hl_done")
        pge_done = sem("pge_done")
        xu_done = sem("xu_done")
        rope_v, rope_p = sem("rope_v"), sem("rope_p")
        qt_done, qte_done = sem("qt_done"), sem("qte_done")
        sc_done, nm_done, ex_done, pt_done = sem("sc_done"), sem("nm_done"), sem("ex_done"), sem("pt_done")
        pte_done, av_done, y_done = sem("pte_done"), sem("av_done"), sem("y_done")
        ix_done, ixe_done = sem("ix_done"), sem("ixe_done")
        dve_chain, pool_chain, act_chain = sem("dve_chain"), sem("pool_chain"), sem("act_chain")
        act_done, sq_done = sem("act_done"), sem("sq_done")
        ht_done, hidh_done, hidl_done = sem("ht_done"), sem("hidh_done"), sem("hidl_done")
        ada_in = [sem(f"ada_in{i}") for i in range(NPIECE)]
        ada_used, ada_t, ada_e, gate_out = sem("ada_used"), sem("ada_t"), sem("ada_e"), sem("gate_out")
        lg_done, rex_done, sel_done, cnt_done = sem("lg_done"), sem("rex_done"), sem("sel_done"), sem("cnt_done")
        g_done, gt_t, gt_e, ga_done = sem("g_done"), sem("gt_t"), sem("gt_e"), sem("ga_done")
        gf_done, gh_done, gl_done = sem("gf_done"), sem("gh_done"), sem("gl_done")
        ye_done, st_done, ma_done = sem("ye_done"), sem("st_done"), sem("ma_done")
        moved = sem("moved")
        flag_done, out_ready, out_done = sem("flag_done"), sem("out_ready"), sem("out_done")

        LAYERS = range(2 * DEPTH)
        if stop is not None:
            LAYERS = range(stop)

        def width(l):
            return IN1 if l < DEPTH else IN2

        def groups(n):
            return [min(COL, n - c) for c in range(0, n, COL)]

        GROUPS0 = {}
        n = 0
        for l in LAYERS:
            for which in (0, 1):
                GROUPS0[l, which] = n
                n += len(groups(width(l))) if which == 0 else D // COL
        def pairs(l):
            if l < DEPTH:
                return ([("big", QA1 + P * i) for i in range(4)] + [("dup", 0), ("dup", P)]
                        + [("big", QB1 + P * i) for i in range(8)])
            return ([("big", QA2 + P * i) for i in range(3)] + [("dup", 0)] + [("big", QI2 + P * i) for i in range(2)]
                    + [("dup", P)] + [("big", QB2 + P * i) for i in range(4)] + [("big", QC2 + P * i) for i in range(6)])

        PAIRS0 = {l: sum(len(pairs(m)) for m in LAYERS if m < l) for l in LAYERS}
        BANKS0 = {l: sum((len(pairs(m)) + 1) // 2 for m in LAYERS if m < l) for l in LAYERS}

        def jobs(l):
            full = HD ** -0.5
            if l < DEPTH:
                a = [(i // 2, 4 + i // 4, HD * (i % 2), HD, VA1 + HD * (i // 4), None, full, HD * i, 0) for i in range(HA)]
                b = [(6 + i // 2, 10 + i // 2, HD * (i % 2), HD, VB1 + HD * i, "dilated", full, HA * HD + HD * i, 0)
                     for i in range(HB)]
                return a + b
            c = [(11 + i // 2, 14 + i // 2, HD * (i % 2), HD, VC2 + HD * i, "causal", full, (A2 + B2 + i) * HD, 0)
                 for i in range(C2)]
            b = [(7 + i // 4, 9 + i // 4, 32 * (i % 4), 32, VB2 + HD * (i // 2), "causal", 32 ** -0.5,
                  A2 * HD + HD * (i // 2), 1 + i % 2) for i in range(2 * B2)]
            a = [(i // 2, 3, HD * (i % 2), HD, VA2, "chosen", full, HD * i, 0) for i in range(A2)]
            return c + b + a

        JOBS0 = {l: sum(len(jobs(m)) for m in LAYERS if m < l) for l in LAYERS}

        def steps(l):
            return FF1 // F_UP if l < DEPTH else FF2 // F_GATED

        STEPS0 = {l: sum(steps(m) for m in LAYERS if m < l) for l in LAYERS}
        MOE = 2 * DEPTH - 1
        MJ = FF2 // F_GATED
        MT = 3 * MJ

        def w_in_of(l):
            return (A["w_in"] if l < DEPTH else A["w_in_2"])[l % DEPTH].rearrange("(k p) n -> p k n", p=P)

        def w_out_of(l):
            return (A["w_out"] if l < DEPTH else A["w_out_2"])[l % DEPTH].rearrange("(k p) n -> p k n", p=P)



        def proj_evac(l):
            return FREE_BANKS + TT * sum(len(groups(width(i))) for i in LAYERS if i <= l)

        def expert_ring(ring, e, t0, loads0):
            per = [sum(i % MORE_RAW == s for i in range(MT)) for s in range(MORE_RAW)]
            ring.t, ring.i, ring.raw = t0 + e * MT, 0, MORE_RAW
            ring.loads = [c + e * m for c, m in zip(loads0, per)]

        def expert_after(t0, loads0):
            per = [sum(i % MORE_RAW == s for i in range(MT)) for s in range(MORE_RAW)]
            return t0 + NE * MT, [c + NE * m for c, m in zip(loads0, per)]

        def silu_col(k):
            return csilu[:, k:k + 1] if isinstance(k, int) else csilu[:, bass.ds(k, 1)]

        def gate_mul(dve, at, ntt, src, dst, banks):
            for t in range(ntt):
                dve.wait_ge(act_done, at + t + 1)
                dve.tensor_tensor(scr(dst + t * F_GATED, F_GATED), scr(src + t * F_GATED, F_GATED),
                                  banks[t][:, F_GATED:2 * F_GATED], ALU.mult).then_inc(sq_done, 1)

        def rope_steps(eng, link, v, heads, half_, cos, sin, tmp):
            n = 2 * half_
            a, b = scr(tmp, heads * n, heads, n), scr(tmp + 320, heads * n, heads, n)
            link(eng.tensor_tensor(a, v[:, :, 0:n], cos.unsqueeze(1).broadcast_to([P, heads, n]), ALU.mult))
            for o, i in ((0, half_), (half_, 0)):
                s = sin[:, o:o + half_].unsqueeze(1).broadcast_to([P, heads, half_])
                link(eng.tensor_tensor(b[:, :, o:o + half_], v[:, :, i:i + half_], s, ALU.mult))
            link(eng.tensor_tensor(v[:, :, 0:n], a, b, ALU.add))

        block = ctx.enter_context(nc.Block())

        def group_loop(eng, ring, widths, first, body):
            full = widths.count(COL) // 2
            done = 0
            if full > 1:
                with eng.Fori(0, full) as it:
                    ring.enter(it, 4)
                    body(2 * it, COL, 0)
                    body(2 * it + 1, COL, 1)
                ring.leave(full)
                done = 2 * full
            for c in range(done, len(widths)):
                body(c, widths[c], c % 2)

        @block.sync
        def _(sp):
            ring = Tiles()

            def stage(raw_slots=RAW):
                ring.stage(raw_slots)
                if ring.t:
                    sp.wait_ge(lo_done, FREE_RAW + ring.t)

            def tile(parts, back=None):
                t, s, _, _ = ring.next()
                sp.wait_ge(lo_done, FREE_RAW + t - (back or ring.raw) + 1)
                for dst, src in parts(raw(s)):
                    sp.dma_start(dst, src).then_inc(w_loaded[s], 16)

            def cols(w, c, n):
                for a in range(2):
                    def parts(r, a=a):
                        d = r[:, 0:4 * n].rearrange("p (k n) -> p k n", k=4)
                        for b in range(2):
                            k = 4 * a + 2 * b
                            yield d[:, 2 * b:2 * b + 2, :], w[:, k:k + 2, bass.ds(c, n)]
                    tile(parts)

            def gated(wg, wu, c, backs=(None, None)):
                for a in range(2):
                    def parts(r, a=a):
                        d = r.rearrange("p (k b n) -> p k b n", k=4, b=2)
                        for b, w in enumerate((wg, wu)):
                            yield d[:, :, b, :], w[:, 4 * a:4 * a + 4, bass.ds(c, F_GATED)]
                    tile(parts, backs[a])

            def rows(w, r0, n, back=None):
                for b in range(n):
                    def parts(r, b=b):
                        d = r.rearrange("p (i n) -> p i n", i=2)
                        for i in range(2):
                            yield d[:, i:i + 1, :], w[:, bass.ds(r0 + 2 * b + i, 1), :]
                    tile(parts, back)

            def project(w, widths):
                stage()
                group_loop(sp, ring, widths, 0, lambda c, n, g: cols(w, c * COL, n))

            def ada_piece(l, k, n):
                to = scr(X_ADA + n * PIECE, PIECE)
                at = NPIECE * (9 * l + k) + n
                if not isinstance(at, int) or at >= NPIECE:
                    sp.wait_ge(ada_used, at - NPIECE + 1)
                if isinstance(k, int) and k == KC:
                    sp.dma_start(to[0:1, :], A["b_ada_2"][l:l + 1, n * PIECE:(n + 1) * PIECE]).then_inc(ada_in[n], 16)
                else:
                    src = A["w_ada_2"][l].rearrange("(k p) n -> p k n", p=P)
                    sp.dma_start(to.unsqueeze(1), src[:, bass.ds(k, 1), n * PIECE:(n + 1) * PIECE]).then_inc(ada_in[n], 16)

            def row(src, n):
                if n:
                    sp.wait_ge(row_used, n)
                sp.dma_start(rowg[:, :], src).then_inc(row_in, 16)

            sp.dma_start(const[:, :], A["consts"]).then_inc(c_in, 16)
            sp.dma_start(x[:, :, :], A["x"][0].rearrange("(t p) d -> p t d", p=P)).then_inc(x_in, 16)
            g = slab[:, S_RAW:S_RAW + P]
            for at, src in ((G_NORM1, A["norm1"]), (G_NORM2, A["norm2"]), (G_ATTN, A["g_attn_2"]),
                            (G_FFN, A["g_ffn_2"])):
                sp.dma_start(g[at:at + 16, :], src.rearrange("l (k n) -> (l k) n", n=P)).then_inc(r_in, 16)
            for l in range(DEPTH):
                for i, src in enumerate((A["out_norm_a"], A["out_norm_b"])):
                    at = G_OUT + KC * l + 4 * i
                    sp.dma_start(g[at:at + 4, :], src[l].rearrange("(k n) -> k n", n=P)).then_inc(r_in, 16)
            sp.dma_start(g[G_C:G_C + KC, :], A["c_2"][0].rearrange("(k n) -> k n", n=P)).then_inc(r_in, 16)
            for l in range(DEPTH):
                sp.dma_start(qkg[:, l, 0, :], A["q_norm"][l:l + 1, :].broadcast_to([P, HD])).then_inc(v_in, 16)
                sp.dma_start(qkg[:, l, 1, :], A["k_norm"][l:l + 1, :].broadcast_to([P, HD])).then_inc(v_in, 16)
                sp.dma_start(subg[:, l, :], A["diff_subln_2"][l:l + 1, :].broadcast_to([P, HD])).then_inc(v_in, 16)
                sp.dma_start(lam[:, l, :], A["diff_lambda_2"][l:l + 1].rearrange("a b c -> a (b c)").broadcast_to([P, 4 * 32])
                             ).then_inc(v_in, 16)
            with nc.allow_non_contiguous_dma(reason="256 positions"):
                sp.dma_start(posi[:, :].unsqueeze(2), A["positions_2"].rearrange("a (t p) -> p t a", p=P)).then_inc(v_in, 16)
            sp.dma_start(wr[:, :, :], A["w_router_2"][0].rearrange("(k p) e -> p k e", p=P)).then_inc(v_in, 16)

            nrow = 0
            for l in LAYERS:
                m = l % DEPTH
                project(w_in_of(l), groups(width(l)))
                if l >= DEPTH:
                    if l == DEPTH:
                        sp.wait_ge(gate_out, 16 * DEPTH)
                    row(gates[m, :, 0, :], nrow)
                    nrow += 1
                project(w_out_of(l), groups(D))
                if l < DEPTH:
                    w1 = A["w_mlp_in"][l].rearrange("(k p) n -> p k n", p=P)
                    w2 = A["w_mlp_out"][l].rearrange("(r p) n -> p r n", p=P)
                    J = steps(l)
                    stage()
                    cols(w1, 0, F_UP)
                    sp.wait_ge(hl_done, 2 * (3 * l + 1) + 2)
                    for n in range(NPIECE):
                        ada_piece(l, 0, n)
                    with sp.Fori(0, J - 1) as j:
                        ring.enter(j, 4)
                        cols(w1, j * F_UP + F_UP, F_UP)
                        rows(w2, j * 4, 2)
                        for n in range(NPIECE):
                            ada_piece(l, j + 1, n)
                    ring.leave(J - 1)
                    rows(w2, 4 * (J - 1), 2)
                    for n in range(NPIECE):
                        ada_piece(l, KC, n)
                    if l == DEPTH - 1:
                        row(A["final_norm"].rearrange("(a n) -> a n", a=1).broadcast_to([P, D]), nrow)
                        nrow += 1
                elif l < MOE:
                    wg = A["w_ff_gate_2"][0].rearrange("(k p) n -> p k n", p=P)
                    wu = A["w_ff_up_2"][0].rearrange("(k p) n -> p k n", p=P)
                    wd = A["w_ff_down_2"][0].rearrange("(r p) n -> p r n", p=P)
                    J = steps(l)
                    stage(3)
                    gated(wg, wu, 0)
                    with sp.Fori(0, J - 1) as j:
                        ring.enter(j, 3)
                        gated(wg, wu, j * F_GATED + F_GATED)
                        rows(wd, j * 2, 1)
                    ring.leave(J - 1)
                    rows(wd, 2 * (J - 1), 1)
                    row(gates[m, :, 1, :], nrow)
                    nrow += 1
                else:
                    row(gates[m, :, 1, :], nrow)
                    nrow += 1
                    sp.wait_ge(hl_done, 2 * (3 * l + 2) + 2)
                    stage(MORE_RAW)

                    def expert_loads(t0, loads0):
                        with sp.Fori(0, NE) as e:
                            expert_ring(ring, e, t0, loads0)
                            wg = A["w_exp_gate_2"][0, bass.ds(e, 1)].rearrange("a (k p) n -> p (a k) n", p=P)
                            wu = A["w_exp_up_2"][0, bass.ds(e, 1)].rearrange("a (k p) n -> p (a k) n", p=P)
                            wd = A["w_exp_down_2"][0, bass.ds(e, 1)].rearrange("a (r p) n -> p (a r) n", p=P)
                            gated(wg, wu, 0, (3, 2))
                            with sp.Fori(0, MJ // 2) as jj:
                                ring.enter(jj, 6)
                                for b in range(2):
                                    gated(wg, wu, jj * 2 * F_GATED + (b + 1) * F_GATED)
                                    rows(wd, jj * 4 + 2 * b, 1)
                            ring.leave(MJ // 2)
                            rows(wd, 2 * (MJ - 1), 1)

                    t0, loads0 = ring.t, list(ring.loads)
                    expert_loads(t0, loads0)
                    if OVERFLOW:
                        sp.wait_ge(flag_done, 1)
                        full = sp.value_load(flag[0:1, 0:1], min_val=0, max_val=SEQ)
                        with sp.If(full > P):
                            expert_loads(*expert_after(t0, loads0))
            row(A["g_final_2"].rearrange("(a n) -> a n", a=1).broadcast_to([P, D]), nrow)
            sp.wait_ge(out_ready, 1)
            sp.dma_start(out[0].rearrange("(t p) d -> p t d", p=P), h[:, :, :]).then_inc(out_done, 16)
            sp.wait_ge(out_done, 16)

        @block.gpsimd
        def _(pool):
            n_chain = [0]

            def link(ins):
                n_chain[0] += 1
                ins.then_inc(pool_chain, 1)
                pool.wait_ge(pool_chain, n_chain[0])

            roots = [0]

            def root(n):
                roots[0] += 1
                pool.wait_ge(ms_done, roots[0])
                pool.tensor_tensor(stat[:, 2, 0:n], stat[:, 1, 0:n], half[:, 0:1].broadcast_to([P, n]), ALU.pow).then_inc(rstd_done, 1)

            def rope(src, heads, d, half_, cos, sin):
                for t in range(TT):
                    v = prj[:, t, src:src + heads * d].rearrange("p (h d) -> p h d", h=heads)
                    rope_steps(pool, link, v, heads, half_, cos[:, t, :], sin[:, t, :], X_PT)

            pool.wait_ge(half_d, 1)
            for l in LAYERS:
                root(TT)
                pool.wait_ge(pge_done, proj_evac(l))
                if l < DEPTH:
                    root((HA + KVA) * TT)
                    rope(QB1, 2 * HB, HD, 8, k_("pr_cos", TT, 16), k_("pr_sin", TT, 16))
                else:
                    if l == DEPTH:
                        pool.wait_ge(sin_d, 1)
                    rope(QB2, 4 * B2, 32, 4, rope32[:, 0], rope32[:, 1])
                    rope(QC2, 2 * C2, HD, 8, rope64[:, 0], rope64[:, 1])
                pool.nop().then_inc(rope_p, 1)
                if l >= DEPTH:
                    root(TT * B2)
                if l < DEPTH:
                    root(2 * TT)
                root(TT)
                if l < DEPTH:
                    ub = 2 * STEPS0[l]

                    def square(j):
                        for t in range(TT):
                            pool.wait_ge(act_done, ub + j * TT + t + 1)
                            a = scr(X_ACT + t * F_UP, F_UP)
                            pool.tensor_tensor(scr(X_ACT2 + t * F_UP, F_UP), a, a, ALU.mult).then_inc(sq_done, 1)

                    with pool.Fori(0, steps(l)) as j:
                        square(j)
                if l == DEPTH - 1:
                    root(TT)
            root(TT)

        @block.vector
        def _(dve):
            ring = Tiles()
            n_chain = [0]

            def mark(ins):
                n_chain[0] += 1
                ins.then_inc(dve_chain, 1)
                return n_chain[0]

            def link(ins):
                dve.wait_ge(dve_chain, mark(ins))

            def lo():
                t, s, q, _ = ring.next()
                dve.wait_ge(hi_done, t + 1)
                dve.tensor_tensor(w_lo[:, q, :], raw(s), w_hi[:, q, :].bitcast(F32), ALU.subtract).then_inc(lo_done, 1)

            def norm():
                xns[0] += TT
                dve.wait_ge(ss_done, sums[0] + TT)
                sums[0] += TT
                dve.tensor_scalar(stat[:, 1, 0:TT], stat[:, 0, 0:TT], 1.0 / D, EPS, ALU.mult, ALU.add).then_inc(ms_done, 1)
                roots[0] += 1
                dve.wait_ge(rstd_done, roots[0])
                for t in range(TT):
                    dve.tensor_scalar(h[:, t, :], x[:, t, :], stat[:, 2, t:t + 1], None, ALU.mult).then_inc(xn_done, 1)

            sums, roots, turned, xns = [0], [0], [0], [0]

            def turn(gain, shift):
                m = turned[0]
                turned[0] += 1
                for k in range(KC):
                    src = bank[k // 2][:, (k % 2) * SEQ:(k % 2 + 1) * SEQ]
                    dve.wait_ge(tp_done, KC * m + k - k % 2 + 2)
                    if gain is None:
                        dve.tensor_copy(htf[:, k, :], src).then_inc(tpe_done, 1)
                    elif shift is None:
                        dve.tensor_scalar(htf[:, k, :], src, gain(k), None, ALU.mult).then_inc(tpe_done, 1)
                    else:
                        dve.tensor_scalar(htf[:, k, :], src, gain(k), shift(k), ALU.mult, ALU.add).then_inc(tpe_done, 1)
                for b in range(2):
                    ks = slice(4 * b, 4 * b + 4)
                    dve.wait_ge(hh_done, 2 * m + b + 1)
                    dve.tensor_tensor(hT_lo[:, ks, :], htf[:, ks, :], hT_hi[:, ks, :].bitcast(F32), ALU.subtract
                                      ).then_inc(hl_done, 1)

            def gain_of(at):
                return lambda k: gcol[:, at + k:at + k + 1]

            def gated_gain(l, which):
                return lambda k: modg[:, l, which, k:k + 1]

            def shift_of(l, v):
                return lambda k: modcol[:, l, KC * v + k:KC * v + k + 1]

            def split_tiles(widths):
                def body(c, n, g):
                    if isinstance(c, int) and c == len(widths) - 1:
                        return
                    lo()
                    lo()
                group_loop(dve, ring, widths, 2, body)

            def x_update(c, gated_, src, wait):
                wait()
                for t in range(TT):
                    at = x[:, t, c * COL:(c + 1) * COL]
                    if gated_:
                        tmp = scr(X_SM + t * COL, COL)
                        link(dve.tensor_tensor(tmp, src(t), rowg[:, c * COL:(c + 1) * COL], ALU.mult))
                        mark(dve.tensor_tensor(at, tmp, at, ALU.add))
                    else:
                        mark(dve.tensor_tensor(at, src(t), at, ALU.add))

            mark(dve.memset(half[:, :], -0.5))
            dve.memset(stat[:, :, :], 0.0).then_inc(lo_done, FREE_RAW)
            dve.memset(ang[:, :, :], 0.0).then_inc(w_used, FREE_SPLIT)
            dve.wait_ge(lo_done, FREE_RAW)
            dve.wait_ge(w_used, FREE_SPLIT)
            dve.wait_ge(dve_chain, 1)
            dve.nop().then_inc(half_d, 1)
            dve.nop().then_inc(pge_done, FREE_BANKS)
            dve.wait_ge(gc_t, 1)
            dve.tensor_copy(gcol[:, :], bank[7][:, 0:NG]).then_inc(gc_d, 1)
            dve.wait_ge(v_in, 16 * V_LOADS)
            link(dve.tensor_copy(posf[:, :], posi[:, :]))
            dve.wait_ge(c_in, 16)
            inv = const[:, _at["inv64"][0]:_at["inv64"][0] + 12]
            for t in range(TT):
                mark(dve.tensor_scalar(ang[:, 0, 12 * t:12 * t + 12], inv, posf[:, t:t + 1], None, ALU.mult))
            dve.wait_ge(dve_chain, n_chain[0])
            big_f = 12582912.0
            link(dve.tensor_scalar(ang[:, 1], ang[:, 0], float(1 / (2 * np.pi)), None, ALU.mult))
            link(dve.tensor_scalar(ang[:, 1], ang[:, 1], big_f, None, ALU.add))
            link(dve.tensor_scalar(ang[:, 1], ang[:, 1], big_f, None, ALU.subtract))
            p1 = 6.28125
            p2 = float(np.float32(round((2 * np.pi - p1) * 2 ** 21) / 2 ** 21))
            p3 = float(2 * np.pi - p1 - p2)
            for part in (p1, p2, p3):
                link(dve.scalar_tensor_tensor(ang[:, 0], ang[:, 1], -part, ang[:, 0], ALU.mult, ALU.add))
            pi = float(np.float32(3.1415925))
            link(dve.tensor_scalar(ang[:, 0], ang[:, 0], pi, -pi, ALU.min, ALU.max))
            dve.tensor_scalar(ang[:, 1], ang[:, 0], 0.5, None, ALU.mult).then_inc(sin_a, 1)
            dve.wait_ge(sin_h, 2)
            link(dve.tensor_tensor(ang[:, 3], ang[:, 3], ang[:, 3], ALU.mult))
            link(dve.tensor_scalar(ang[:, 3], ang[:, 3], -2.0, 1.0, ALU.mult, ALU.add))
            for tab, o, n in ((rope64, 0, 8), (rope32, 8, 4)):
                for t in range(TT):
                    a = 12 * t + o
                    mark(dve.tensor_copy(tab[:, 0, t, 0:n], ang[:, 3, a:a + n]))
                    mark(dve.tensor_copy(tab[:, 0, t, n:2 * n], ang[:, 3, a:a + n]))
                    mark(dve.tensor_scalar(tab[:, 1, t, 0:n], ang[:, 2, a:a + n], -1.0, None, ALU.mult))
                    mark(dve.tensor_copy(tab[:, 1, t, n:2 * n], ang[:, 2, a:a + n]))
            dve.wait_ge(dve_chain, n_chain[0])
            dve.nop().then_inc(sin_d, 1)
            for l in range(DEPTH):
                v = lam[:, l, :].rearrange("p (a b n) -> p a b n", a=2, b=2)
                link(dve.tensor_tensor(v[:, :, 0, :], v[:, :, 0, :], v[:, :, 1, :], ALU.mult))
                r = dve.tensor_reduce(lams[:, 2 * l:2 * l + 2], v[:, :, 0, :], AX.X, ALU.add)
                r.then_inc(lam_s, 1)
            dve.wait_ge(lam_e, 1)
            for l in range(DEPTH):
                start = 0.8 - 0.6 * float(np.exp(-0.3 * l))
                link(dve.tensor_tensor(nlam[:, l:l + 1], lams[:, 5 + 2 * l:6 + 2 * l], lams[:, 4 + 2 * l:5 + 2 * l], ALU.subtract))
                link(dve.tensor_scalar(nlam[:, l:l + 1], nlam[:, l:l + 1], start, None, ALU.subtract))
                link(dve.tensor_scalar(subg[:, l, :], subg[:, l, :], 1.0 - start, None, ALU.mult))
            link(dve.tensor_copy(wr_hi[:, :, :], wr[:, :, :]))
            link(dve.tensor_tensor(wr_lo[:, :, :], wr[:, :, :], wr_hi[:, :, :].bitcast(F32), ALU.subtract))
            dve.wait_ge(x_in, 16)

            jobs_done = [0]
            idx_done = [0]
            rows_used = [0]
            ub = 0
            for l in LAYERS:
                m = l % DEPTH
                widths = groups(width(l))
                if l == DEPTH:
                    dve.wait_ge(ada_e, 5 * DEPTH)
                    for d in range(DEPTH):
                        for which, v, at in ((0, 1, G_ATTN), (1, 4, G_FFN)):
                            mark(dve.scalar_tensor_tensor(modg[:, d, which, :], modcol[:, d, KC * v:KC * v + KC], 1.0,
                                                          gcol[:, at + KC * d:at + KC * d + KC], ALU.add, ALU.mult))
                    dve.wait_ge(dve_chain, n_chain[0])
                norm()
                ring.stage()
                lo()
                lo()
                if l < DEPTH:
                    turn(gain_of(G_NORM1 + KC * m), None)
                else:
                    turn(gated_gain(m, 0), shift_of(m, 0))
                split_tiles(widths)

                dve.wait_ge(pge_done, proj_evac(l))
                t1, t2 = X_SM, X_SM + 640
                if l < DEPTH:
                    nh = HA + KVA
                    v = prj[:, :, 0:nh * HD]
                    vh = v.rearrange("p t (h d) -> p t h d", h=nh)
                    sq = scr(X_SM, TT * nh * HD, TT, nh * HD)
                    link(dve.tensor_tensor(sq, v, v, ALU.mult))
                    link(dve.tensor_reduce(stat[:, 0, 0:TT * nh], scr(X_SM, TT * nh * HD, TT * nh, HD), AX.X, ALU.add))
                    dve.tensor_scalar(stat[:, 1, 0:TT * nh], stat[:, 0, 0:TT * nh], 1.0 / HD, EPS, ALU.mult, ALU.add
                                      ).then_inc(ms_done, 1)
                    roots[0] += 1
                    dve.wait_ge(rstd_done, roots[0])
                    r = stat[:, 2, 0:TT * nh].rearrange("p (t h) -> p t h", t=TT).unsqueeze(3).broadcast_to([P, TT, nh, HD])
                    link(dve.tensor_tensor(vh, vh, r, ALU.mult))
                    for i, (a, b) in enumerate(((0, HA), (HA, nh))):
                        for t in range(TT):
                            g = qkg[:, m, i, :].unsqueeze(1).broadcast_to([P, b - a, HD])
                            mark(dve.tensor_tensor(vh[:, t, a:b, :], vh[:, t, a:b, :], g, ALU.mult))
                    dve.wait_ge(dve_chain, n_chain[0])
                    for t in range(TT):
                        cos, sin = k_("ax_cos", TT, HD)[:, t, :], k_("ax_sin", TT, HD)[:, t, :]
                        a1 = scr(t1, nh * HD, nh, HD)
                        a2 = scr(t2, nh * HD, nh, 2, HD // 2)
                        v4 = vh[:, t].rearrange("p h (b d) -> p h b d", b=2)
                        s4 = sin.rearrange("p (b d) -> p b d", b=2)
                        mark(dve.tensor_tensor(a1, vh[:, t], cos.unsqueeze(1).broadcast_to([P, nh, HD]), ALU.mult))
                        for o, i in ((0, 16), (16, 0)):
                            s = s4[:, :, o:o + 16].unsqueeze(1).broadcast_to([P, nh, 2, 16])
                            mark(dve.tensor_tensor(a2[:, :, :, o:o + 16], v4[:, :, :, i:i + 16], s, ALU.mult))
                        dve.wait_ge(dve_chain, n_chain[0])
                        b2 = scr(t2, nh * HD, nh, HD)
                        mark(dve.tensor_tensor(vh[:, t, 0:HA], a1[:, 0:HA], b2[:, 0:HA], ALU.add))
                        for i in range(KVA):
                            for d in range(2):
                                o = P * i + HD * d
                                mark(dve.tensor_tensor(h[:, t, o:o + HD], a1[:, HA + i], b2[:, HA + i], ALU.add))
                        dve.wait_ge(dve_chain, n_chain[0])
                    dve.nop().then_inc(rope_v, 1)
                else:
                    def rope(src, heads):
                        for t in range(TT):
                            v = prj[:, t, src:src + heads * HD].rearrange("p (h d) -> p h d", h=heads)
                            rope_steps(dve, link, v, heads, 8, rope64[:, 0, t, :], rope64[:, 1, t, :], X_SM)

                    rope(QA2, A2 + 1)
                    rope(QI2, I2 + 1)
                    for t in range(TT):
                        for i, src in enumerate((KA2, KI2)):
                            for d in range(2):
                                o = P * i + HD * d
                                mark(dve.tensor_copy(h[:, t, o:o + HD], prj[:, t, src:src + HD]))
                    wi = prj[:, :, WI2:WI2 + I2]
                    mark(dve.tensor_scalar(wi, wi, I2 ** -0.5, None, ALU.mult))
                    dve.wait_ge(dve_chain, n_chain[0])
                    dve.nop().then_inc(rope_v, 1)

                picks = []
                if l >= DEPTH:
                    selw = selm = scr(X_SELW, TT * SEQ, TT, SEQ)
                    for i in range(I2):
                        n = idx_done[0] = idx_done[0] + 1
                        r = scr(X_SM, TT * SEQ, TT, SEQ)
                        dve.wait_ge(ix_done, n)
                        last = dve.tensor_scalar(r, bank[6 + i % 2][:, :].rearrange("p (t n) -> p t n", t=TT),
                                                 HD ** -0.5, 0.0, ALU.mult, ALU.max)
                        last.then_inc(ixe_done, 1)
                        dve.wait_ge(ixe_done, n)
                        for t in range(TT):
                            w = prj[:, t, WI2 + i:WI2 + i + 1]
                            if i == 0:
                                mark(dve.tensor_scalar(selw[:, t], r[:, t], w, None, ALU.mult))
                            else:
                                mark(dve.scalar_tensor_tensor(selw[:, t], r[:, t], w, selw[:, t], ALU.mult, ALU.add))
                        dve.wait_ge(dve_chain, n_chain[0])
                    link(dve.tensor_tensor(selw, selw, k_("causal", TT, SEQ), ALU.add))

                    def pick(t):
                        m8 = rt[:, 12 + t, :, :].rearrange("p a b -> p (a b)")[:, 0:8]
                        last = [None, None]

                        def find():
                            if waits[t]:
                                dve.wait_ge(dve_chain, waits[t])
                            waits[t] = mark(dve.max(m8, selw[:, t]))

                        def strike():
                            dve.wait_ge(dve_chain, waits[t])
                            waits[t] = mark(dve.match_replace(selw[:, t], m8, selw[:, t], TAKEN))
                        return find, strike

                    waits = [0, 0]
                    fs = [pick(t) for t in range(TT)]
                    for _ in range(TOPK // 8):
                        for phase in range(2):
                            picks += [fs[t][phase] for t in range(TT)]

                def finish_picks():
                    dve.wait_ge(dve_chain, n_chain[0])
                    link(dve.tensor_scalar(selm, selw, TAKEN / 2, MASKED, ALU.is_gt, ALU.mult))
                    link(dve.tensor_tensor(selm, selm, k_("causal", TT, SEQ), ALU.add))

                js = jobs(l)
                j0 = jobs_done[0]
                ring.stage()
                ywait = {}
                for n in range(len(js) + 2):
                    if n < len(js):
                        _, _, _, _, _, mask, scale, _, _ = js[n]
                        b = (j0 + n) % 2
                        if mask == "chosen" and js[n - 1][5] != "chosen":
                            finish_picks()
                        sm = scr(X_SM + b * COL, COL, TT, SEQ)
                        dve.wait_ge(sc_done, j0 + n + 1)
                        if n >= 2:
                            dve.wait_ge(ex_done, TT * (j0 + n - 1))
                        else:
                            dve.wait_ge(dve_chain, n_chain[0])
                        mx = att[:, 0, n, :]
                        ps = bank[b][:, :].rearrange("p (t n) -> p t n", t=TT)
                        for t in range(TT):
                            if mask is None:
                                mark(dve.tensor_scalar(sm[:, t], ps[:, t], scale, TAKEN, ALU.mult, ALU.max, accum_out=mx[:, t:t + 1]))
                            else:
                                mk = selm if mask == "chosen" else k_(mask, TT, SEQ)
                                mark(dve.tensor_tensor_reduce(sm[:, t], ps[:, t], mk[:, t], scale, TAKEN,
                                                              ALU.add, ALU.max, mx[:, t:t + 1]))
                        dve.wait_ge(dve_chain, n_chain[0])
                        dve.tensor_scalar(att[:, 1, n, :], mx, -1.0, None, ALU.mult).then_inc(nm_done, 1)
                    for _ in range(4):
                        if picks and n >= 1:
                            picks.pop(0)()
                    if n in (2, 4, 6, 8):
                        lo()
                    if n >= 2:
                        i = n - 2
                        _, _, _, _, _, _, _, yc, part = js[i]
                        b = (j0 + i) % 2
                        dve.wait_ge(ex_done, TT * (j0 + i + 1))
                        link(dve.reciprocal(att[:, 3, i, :], att[:, 2, i, :]))
                        if part == 2:
                            link(dve.tensor_scalar(att[:, 3, i, :], att[:, 3, i, :], nlam[:, m:m + 1], None, ALU.mult))
                        dve.wait_ge(av_done, j0 + i + 1)
                        for t in range(TT):
                            o = bank[4 + b][:, t * HD:(t + 1) * HD]
                            y = h[:, t, yc:yc + HD]
                            w = att[:, 3, i, t:t + 1]
                            if part == 2:
                                dve.wait_ge(y_done, TT * (j0 + i))
                                ins = dve.scalar_tensor_tensor(y, o, w, y, ALU.mult, ALU.add)
                            else:
                                ins = dve.tensor_scalar(y, o, w, None, ALU.mult)
                            ins.then_inc(y_done, 1)
                jobs_done[0] += len(js)
                dve.wait_ge(y_done, TT * jobs_done[0])
                sm = scr(X_SM, TT * B2 * HD, TT, B2 * HD)
                if l < DEPTH:
                    dve.wait_ge(ss_done, sums[0] + 2 * TT)
                    sums[0] += 2 * TT
                    dve.tensor_scalar(stat[:, 1, 0:2 * TT], stat[:, 0, 0:2 * TT], 1.0 / (HA * HD), EPS, ALU.mult, ALU.add
                                      ).then_inc(ms_done, 1)
                    roots[0] += 1
                    dve.wait_ge(rstd_done, roots[0])
                    for t in range(TT):
                        for i in range(2):
                            y = h[:, t, i * HA * HD:(i + 1) * HA * HD]
                            c = stat[:, 2, 2 * t + i:2 * t + i + 1]
                            ins = dve.tensor_scalar(y, y, c, None, ALU.mult)
                            if i:
                                ins.then_inc(xn_done, 1)
                    turn(gain_of(G_OUT + KC * m), None)
                else:
                    y = h[:, :, A2 * HD:(A2 + B2) * HD]
                    link(dve.tensor_tensor(sm, y, y, ALU.mult))
                    link(dve.tensor_reduce(stat[:, 0, 0:TT * B2], scr(X_SM, TT * B2 * HD, TT * B2, HD), AX.X, ALU.add))
                    dve.tensor_scalar(stat[:, 1, 0:TT * B2], stat[:, 0, 0:TT * B2], 1.0 / HD, SUB_EPS, ALU.mult, ALU.add
                                      ).then_inc(ms_done, 1)
                    roots[0] += 1
                    dve.wait_ge(rstd_done, roots[0])
                    yh = y.rearrange("p t (h d) -> p t h d", h=B2)
                    r = stat[:, 2, 0:TT * B2].rearrange("p (t h) -> p t h", t=TT).unsqueeze(3).broadcast_to([P, TT, B2, HD])
                    link(dve.tensor_tensor(yh, yh, r, ALU.mult))
                    for t in range(TT):
                        g = subg[:, m, :].unsqueeze(1).broadcast_to([P, B2, HD])
                        dve.tensor_tensor(yh[:, t], yh[:, t], g, ALU.mult).then_inc(xn_done, 1)
                    turn(None, None)

                xns[0] += TT
                if l >= DEPTH:
                    rows_used[0] += 1
                    dve.wait_ge(row_in, 16 * rows_used[0])
                for c in range(D // COL):
                    used = ring.start + 2 * c + 2
                    x_update(c, l >= DEPTH, lambda t: bank[4 + 2 * (c % 2) + t][:, :],
                             lambda: dve.wait_ge(w_used, FREE_SPLIT + used))
                dve.wait_ge(dve_chain, n_chain[0])
                dve.nop().then_inc(xu_done, 1)
                if l >= DEPTH:
                    dve.nop().then_inc(row_used, 1)

                norm()
                J = steps(l)
                if l < MOE:
                    ring.stage(RAW if l < DEPTH else 3, SPLIT if l < DEPTH else 3)
                    lo()
                    lo()
                if l < DEPTH:
                    turn(gain_of(G_NORM2 + KC * m), None)
                else:
                    turn(gated_gain(m, 1), shift_of(m, 3))

                def hid_lo_part(at, t, n, b):
                    dve.wait_ge(hidh_done, at + t + 1)
                    src = b[:, 0:n * P].rearrange("p (f n) -> p f n", f=n)
                    o = slice(t * P, (t + 1) * P)
                    dve.tensor_tensor(hid_lo[:, 0:n, o], src, hid_hi[:, 0:n, o].bitcast(F32), ALU.subtract
                                      ).then_inc(hidl_done, 1)

                if l < DEPTH:
                    def ada(k, n):
                        acc = big[:, n * PIECE:(n + 1) * PIECE]
                        w = scr(X_ADA + n * PIECE, PIECE)
                        c = None if isinstance(k, int) and k == KC else silu_col(k)
                        at = 9 * l + k
                        dve.wait_ge(ada_in[n], 16 * (at + 1))
                        if isinstance(k, int) and k == 0:
                            ins = dve.tensor_scalar(acc, w, c, None, ALU.mult)
                        else:
                            dve.wait_ge(ada_used, NPIECE * (at - 1) + n + 1)
                            if isinstance(k, int) and k == KC:
                                ins = dve.tensor_tensor(acc[0:1, :], w[0:1, :], acc[0:1, :], ALU.add)
                            else:
                                ins = dve.scalar_tensor_tensor(acc, w, c, acc, ALU.mult, ALU.add)
                        ins.then_inc(ada_used, 1)

                    def step(j, more):
                        if more:
                            lo()
                        ada(j, 0)
                        if more:
                            lo()
                        ada(j, 1)
                        lo()
                        ada(j, 2)
                        lo()
                        for t in range(TT):
                            hid_lo_part(ub + j * TT, t, 4, bank[2 + t])

                    step(0, True)
                    with dve.Fori(0, J - 2) as j:
                        ring.enter(j, 4)
                        step(j + 1, True)
                    ring.leave(J - 2)
                    step(J - 1, False)
                    for n in range(NPIECE):
                        ada(KC, n)
                    ub += J * TT
                elif l < MOE:
                    def step(j, more):
                        if more:
                            lo()
                        gate_mul(dve, ub + j * TT, TT, X_ACT, X_ACT2, [bank[0], bank[1]])
                        if more:
                            lo()
                        lo()
                        for t in range(TT):
                            hid_lo_part(ub + j * TT, t, 2, bank[2 + t])

                    with dve.Fori(0, J - 1) as j:
                        ring.enter(j, 3)
                        step(j, True)
                    ring.leave(J - 1)
                    step(J - 1, False)
                    ub += J * TT
                if l < MOE:
                    if l >= DEPTH:
                        rows_used[0] += 1
                        dve.wait_ge(row_in, 16 * rows_used[0])
                    for c in range(2):
                        x_update(c, l >= DEPTH, lambda t: bank[4 + 2 * t + c][:, :],
                                 lambda: dve.wait_ge(w_used, FREE_SPLIT + ring.t))
                    dve.wait_ge(dve_chain, n_chain[0])
                    dve.nop().then_inc(xu_done, 1)
                    if l >= DEPTH:
                        dve.nop().then_inc(row_used, 1)
                    if l == DEPTH - 1:
                        norm()
                        rows_used[0] += 1
                        dve.wait_ge(row_in, 16 * rows_used[0])
                        dve.wait_ge(xn_done, xns[0])
                        for t in range(TT):
                            mark(dve.tensor_tensor(x[:, t, :], h[:, t, :], rowg[:, :], ALU.mult))
                        dve.wait_ge(dve_chain, n_chain[0])
                        dve.nop().then_inc(xu_done, 1)
                        dve.nop().then_inc(row_used, 1)
                    continue

                lg, m8, nm, ex, gt, sel, den, wts, pos, tot = (rt[:, i] for i in range(10))
                dve.wait_ge(lg_done, 1)
                link(dve.tensor_copy(lg, bank[4][:, 0:TT * NE].rearrange("p (t e) -> p t e", t=TT)))
                for t in range(TT):
                    mark(dve.max(m8[:, t, :], lg[:, t, :]))
                dve.wait_ge(dve_chain, n_chain[0])
                dve.tensor_scalar(nm[:, :, 0:1], m8[:, :, 0:1], -1.0, None, ALU.mult).then_inc(sel_done, 1)
                cmp = scr(X_MACT, 2 * NE * NE, 2, NE, NE)
                for t in range(TT):
                    mine = lg[:, t, :].unsqueeze(2).broadcast_to([P, NE, NE])
                    other = lg[:, t, :].unsqueeze(1).broadcast_to([P, NE, NE])
                    mark(dve.tensor_tensor(cmp[:, 0], other, mine, ALU.is_gt))
                    link(dve.tensor_tensor(cmp[:, 1], other, mine, ALU.is_equal))
                    link(dve.tensor_tensor(cmp[:, 1], cmp[:, 1], k_("earlier", NE, NE), ALU.mult))
                    link(dve.tensor_tensor(cmp[:, 0], cmp[:, 0], cmp[:, 1], ALU.add))
                    link(dve.tensor_reduce(gt[:, t, :], cmp[:, 0], AX.X, ALU.add))
                dve.tensor_scalar(sel, gt, 2.0, None, ALU.is_lt).then_inc(sel_done, 1)
                dve.wait_ge(sel_done, 2)
                dve.wait_ge(rex_done, TT)
                link(dve.tensor_tensor(ex, ex, sel, ALU.mult))
                link(dve.tensor_reduce(den[:, :, 0:1], ex, AX.X, ALU.add))
                link(dve.reciprocal(den[:, :, 0:1], den[:, :, 0:1]))
                for t in range(TT):
                    mark(dve.tensor_scalar(wts[:, t, :], ex[:, t, :], den[:, t, 0:1], None, ALU.mult))
                dve.wait_ge(cnt_done, 1)
                cnt = bank[5][:, 0:3 * NE].rearrange("p (t e) -> p t e", t=3)
                link(dve.tensor_scalar(pos, cnt[:, 0:2, :], 1.0, None, ALU.add))
                link(dve.tensor_tensor(pos, pos, sel, ALU.mult))
                link(dve.tensor_scalar(pos, pos, -1.0, None, ALU.add))
                link(dve.tensor_reduce(tot[0:1, 0, 0:1], cnt[0:1, 2, :], AX.X, ALU.max))
                dve.tensor_copy(flag[0:1, 0:1], tot[0:1, 0, 0:1]).then_inc(flag_done, 1)
                acc = big[:, 0:TT * D].rearrange("p (t n) -> p t n", t=TT)
                link(dve.memset(big[:, 0:TT * D], 0.0))
                dve.nop().then_inc(ma_done, 1)

                def expert(e, n, t0):
                    ring.t, ring.i, ring.raw, ring.split = t0, 0, MORE_RAW, 3
                    dve.wait_ge(st_done, n + 1)
                    pe_ = pos[:, :, bass.ds(e, 1)]
                    we = wts[:, :, bass.ds(e, 1)]
                    for t in range(TT):
                        dve.tensor_scalar(scr(X_G + t * P, P), iota, pe_[:, t], None, ALU.is_equal).then_inc(g_done, 1)
                        dve.tensor_scalar(scr(X_GW + t * P, P), iota, pe_[:, t], we[:, t], ALU.is_equal, ALU.mult
                                          ).then_inc(g_done, 1)
                    lo()
                    lo()
                    dve.wait_ge(ga_done, n + 1)
                    for k in range(KC):
                        dve.tensor_scalar(scr(X_HGF + k * P, P), bank[2 + k // 4][:, (k % 4) * P:(k % 4 + 1) * P],
                                          modg[:, m, 1, k:k + 1], modcol[:, m, KC * 3 + k:KC * 3 + k + 1], ALU.mult, ALU.add
                                          ).then_inc(gf_done, 1)
                    dve.wait_ge(gh_done, n + 1)
                    dve.tensor_tensor(hT_lo[:, 0:KC // 2, :], scr(X_HGF, KC * P, KC // 2, SEQ),
                                      hT_hi[:, 0:KC // 2, :].bitcast(F32), ALU.subtract).then_inc(gl_done, 1)

                    def step(j, more):
                        if more:
                            lo()
                        gate_mul(dve, ub + n * MJ + j, 1, X_MACT, X_MACT2, [bank[0]])
                        if more:
                            lo()
                        lo()
                        hid_lo_part(ub + n * MJ + j, 0, 2, bank[1])

                    with dve.Fori(0, MJ // 2) as jj:
                        ring.enter(jj, 6)
                        step(2 * jj, True)
                        step(2 * jj + 1, True)
                    ring.leave(MJ // 2)
                    step(MJ - 1, False)
                    dve.wait_ge(st_done, n + 2)
                    for t in range(TT):
                        for c in range(2):
                            at = acc[:, t, c * COL:(c + 1) * COL]
                            dve.tensor_tensor(at, bank[4 + 2 * t + c][:, :], at, ALU.add).then_inc(ma_done, 1)

                t0 = ring.t
                with dve.Fori(0, NE) as e:
                    expert(e, e, t0 + e * MT)
                if OVERFLOW:
                    full = dve.value_load(flag[0:1, 0:1], min_val=0, max_val=SEQ)
                    dve.wait_ge(ma_done, 1 + 4 * NE)
                    with dve.If(full > P):
                        dve.tensor_scalar(pos, pos, -float(P), None, ALU.add).then_inc(moved, 1)
                        dve.wait_ge(moved, 1)
                        with dve.Fori(0, NE) as e:
                            expert(e, e + NE, t0 + NE * MT + e * MT)
                        dve.wait_ge(ma_done, 1 + 8 * NE)
                rows_used[0] += 1
                dve.wait_ge(row_in, 16 * rows_used[0])
                for t in range(TT):
                    mark(dve.tensor_tensor(acc[:, t, :], acc[:, t, :], rowg[:, :], ALU.mult))
                dve.wait_ge(dve_chain, n_chain[0])
                dve.nop().then_inc(row_used, 1)
                for t in range(TT):
                    mark(dve.tensor_tensor(x[:, t, :], acc[:, t, :], x[:, t, :], ALU.add))
                dve.wait_ge(dve_chain, n_chain[0])
                dve.nop().then_inc(xu_done, 1)
            norm()
            rows_used[0] += 1
            dve.wait_ge(row_in, 16 * rows_used[0])
            dve.wait_ge(xn_done, xns[0])
            for t in range(TT):
                mark(dve.tensor_tensor(h[:, t, :], h[:, t, :], rowg[:, :], ALU.mult))
            dve.wait_ge(dve_chain, n_chain[0])
            dve.nop().then_inc(out_ready, 1)

        @block.scalar
        def _(act):
            ring = Tiles()

            def stage(raw_slots=RAW, split=SPLIT):
                ring.stage(raw_slots, split)
                act.wait_ge(w_used, FREE_SPLIT + ring.t)

            def hi():
                t, s, q, n = ring.next()
                act.wait_ge(w_loaded[s], 32 * n)
                act.wait_ge(w_used, FREE_SPLIT + t - ring.split + 1)
                act.activation(w_hi[:, q, :], raw(s), ACT.Copy).then_inc(hi_done, 1)

            updates = [0]

            def squares():
                if updates[0]:
                    act.wait_ge(xu_done, updates[0])
                else:
                    act.wait_ge(x_in, 16)
                    act.wait_ge(lo_done, FREE_RAW)
                updates[0] += 1
                for t in range(TT):
                    act.activation(h[:, t, :], x[:, t, :], ACT.Square, accum_out=stat[:, 0, t:t + 1]).then_inc(ss_done, 1)

            turned = [0]

            def turn():
                m = turned[0]
                turned[0] += 1
                for b in range(2):
                    ks = slice(4 * b, 4 * b + 4)
                    act.wait_ge(tpe_done, KC * m + 4 * (b + 1))
                    act.activation(hT_hi[:, ks, :], htf[:, ks, :], ACT.Copy).then_inc(hh_done, 1)

            act.wait_ge(gc_d, 1)
            act.activation(csilu[:, :], gcol[:, G_C:G_C + KC], ACT.Silu).then_inc(silu_c, 1)
            act.wait_ge(sin_a, 1)
            act.activation(ang[:, 2], ang[:, 0], ACT.Sin).then_inc(sin_h, 1)
            act.activation(ang[:, 3], ang[:, 1], ACT.Sin).then_inc(sin_h, 1)
            act.wait_ge(lam_s, DEPTH)
            act.activation(lams[:, 4:8], lams[:, 0:4], ACT.Exp).then_inc(lam_e, 1)

            jobs_done = [0]
            ub = 0
            for l in LAYERS:
                m = l % DEPTH
                widths = groups(width(l))
                squares()
                stage()
                hi()
                hi()
                turn()

                def project(c, n, g):
                    if not (isinstance(c, int) and c == len(widths) - 1):
                        hi()
                        hi()
                    act.wait_ge(w_used, FREE_SPLIT + ring.start + 2 * c + 2)
                    for t in range(TT):
                        act.activation(prj[:, t, bass.ds(c * COL, n)], bank[4 + 2 * g + t][:, 0:n], ACT.Copy).then_inc(pge_done, 1)

                group_loop(act, ring, widths, 2, project)

                nb = (len(pairs(l)) + 1) // 2
                if 0 < l <= DEPTH:
                    act.wait_ge(gate_out, 16 * l)
                for i in range(nb):
                    w = min(2, len(pairs(l)) - 2 * i)
                    act.wait_ge(qt_done, BANKS0[l] + i + 1)
                    act.activation(qkT[:, 2 * i:2 * i + w, :], bank[i % 4][:, 0:w * SEQ].rearrange("p (a n) -> p a n", a=w),
                                   ACT.Copy).then_inc(qte_done, 1)

                js = jobs(l)
                j0 = jobs_done[0]
                stage()
                for n in range(len(js) + 1):
                    if n < len(js):
                        b = (j0 + n) % 2
                        act.wait_ge(nm_done, j0 + n + 1)
                        if n >= 2:
                            act.wait_ge(pt_done, j0 + n - 1)
                        for t in range(TT):
                            act.activation(scr(X_P + b * COL + t * SEQ, SEQ), scr(X_SM + b * COL + t * SEQ, SEQ), ACT.Exp,
                                           bias=att[:, 1, n, t:t + 1], accum_out=att[:, 2, n, t:t + 1]).then_inc(ex_done, 1)
                    if n >= 1:
                        b = (j0 + n - 1) % 2
                        act.wait_ge(pt_done, j0 + n)
                        if n >= 3:
                            act.wait_ge(av_done, j0 + n - 2)
                        act.activation(scr(X_PT + b * COL, COL), bank[2 + b][:, :], ACT.Copy).then_inc(pte_done, 1)
                    if n in (1, 3, 5, 7):
                        hi()
                jobs_done[0] += len(js)
                if l < DEPTH:
                    act.wait_ge(y_done, TT * jobs_done[0])
                    for t in range(TT):
                        for i in range(2):
                            w = HA * HD
                            act.activation(scr(X_SM + (2 * t + i) * w, w), h[:, t, i * w:(i + 1) * w], ACT.Square,
                                           accum_out=stat[:, 0, 2 * t + i:2 * t + i + 1]).then_inc(ss_done, 1)
                turn()
                squares()
                J = steps(l)
                if l < MOE:
                    stage(RAW if l < DEPTH else 3, SPLIT if l < DEPTH else 3)
                    hi()
                    hi()
                turn()

                def hid_high_part(at, t, n, b):
                    act.wait_ge(ht_done, at + t + 1)
                    src = b[:, 0:n * P].rearrange("p (f n) -> p f n", f=n)
                    act.activation(hid_hi[:, 0:n, t * P:(t + 1) * P], src, ACT.Copy).then_inc(hidh_done, 1)

                if l < DEPTH:
                    def step(j, more):
                        up = 2 if isinstance(j, int) and j == 0 else 4 * j
                        if more:
                            hi()
                        act.wait_ge(w_used, FREE_SPLIT + ring.start + up)
                        for t in range(TT):
                            act.activation(scr(X_ACT + t * F_UP, F_UP), bank[t][:, :], ACT.Relu).then_inc(act_done, 1)
                        if more:
                            hi()
                        hi()
                        hi()
                        for t in range(TT):
                            hid_high_part(ub + j * TT, t, 4, bank[2 + t])

                    step(0, True)
                    with act.Fori(0, J - 2) as j:
                        ring.enter(j, 4)
                        step(j + 1, True)
                    ring.leave(J - 2)
                    step(J - 1, False)
                    ub += J * TT
                    act.wait_ge(ada_t, 5 * l + 1)
                    act.activation(modcol[:, l, :], bank[0][:, 0:48], ACT.Copy).then_inc(ada_e, 1)
                    for i in range(4):
                        act.wait_ge(ada_t, 5 * l + 2 + i)
                        act.activation(scr(X_ADA + i * COL, COL), bank[1 + i % 3][:, :], ACT.Copy).then_inc(ada_e, 1)
                    act.wait_ge(ada_e, 5 * (l + 1))
                    act.dma_start(gates[l].rearrange("p a n -> p (a n)"), scr(X_ADA, 2 * D)).then_inc(gate_out, 16)
                elif l < MOE:
                    def step(j, more):
                        up = 2 if isinstance(j, int) and j == 0 else 3 * j + 1
                        if more:
                            hi()
                        act.wait_ge(w_used, FREE_SPLIT + ring.start + up)
                        for t in range(TT):
                            act.activation(scr(X_ACT + t * F_GATED, F_GATED), bank[t][:, 0:F_GATED], ACT.Silu).then_inc(act_done, 1)
                        if more:
                            hi()
                        hi()
                        for t in range(TT):
                            hid_high_part(ub + j * TT, t, 2, bank[2 + t])

                    step(0, True)
                    with act.Fori(0, J - 2) as j:
                        ring.enter(j, 3)
                        step(j + 1, True)
                    ring.leave(J - 2)
                    step(J - 1, False)
                    ub += J * TT
                else:
                    lg, nm, ex = rt[:, 0], rt[:, 2], rt[:, 3]
                    act.wait_ge(sel_done, 1)
                    for t in range(TT):
                        act.activation(ex[:, t, :], lg[:, t, :], ACT.Exp, bias=nm[:, t, 0:1]).then_inc(rex_done, 1)
                    stage(MORE_RAW, 3)

                    def expert(e, n, t0, loads0):
                        expert_ring(ring, e, t0, loads0)
                        ring.split = 3
                        hi()
                        hi()
                        act.wait_ge(gt_t, n + 1)
                        act.activation(scr(X_GT, TT * P), bank[1][:, 0:TT * P], ACT.Copy).then_inc(gt_e, 1)
                        act.wait_ge(gf_done, KC * (n + 1))
                        act.activation(hT_hi[:, 0:KC // 2, :], scr(X_HGF, KC * P, KC // 2, SEQ), ACT.Copy).then_inc(gh_done, 1)

                        def step(j, more, up):
                            if more:
                                hi()
                            act.wait_ge(w_used, FREE_SPLIT + up)
                            act.activation(scr(X_MACT, F_GATED), bank[0][:, 0:F_GATED], ACT.Silu).then_inc(act_done, 1)
                            if more:
                                hi()
                            hi()
                            hid_high_part(ub + n * MJ + j, 0, 2, bank[1])

                        t0e = t0 + e * MT
                        step(0, True, t0e + 2)
                        step(1, True, t0e + 4)
                        with act.Fori(0, MJ // 2 - 1) as jj:
                            ring.enter(jj, 6)
                            step(2 * jj + 2, True, t0e + 7 + 6 * jj)
                            step(2 * jj + 3, True, t0e + 10 + 6 * jj)
                        ring.leave(MJ // 2 - 1)
                        step(MJ - 1, False, t0e + 3 * (MJ - 1) + 1)
                        act.wait_ge(w_used, FREE_SPLIT + t0e + MT)
                        act.wait_ge(st_done, n + 1)
                        for c in range(2):
                            act.activation(scr(X_YE + c * COL, COL), bank[2 + c][:, :], ACT.Copy).then_inc(ye_done, 1)

                    t0, loads0 = ring.t, list(ring.loads)
                    with act.Fori(0, NE) as e:
                        expert(e, e, t0, loads0)
                    if OVERFLOW:
                        act.wait_ge(flag_done, 1)
                        full = act.value_load(flag[0:1, 0:1], min_val=0, max_val=SEQ)
                        with act.If(full > P):
                            with act.Fori(0, NE) as e:
                                expert(e, e + NE, *expert_after(t0, loads0))
                if l == DEPTH - 1:
                    squares()
            squares()

        @block.tensor
        def _(pe):
            ring = Tiles()

            def product(dst, a_hi, a_lo, b_hi, b_lo, start, stop_):
                pe.matmul(dst, a_hi, b_hi, start=start, stop=False)
                pe.matmul(dst, a_hi, b_lo, start=False, stop=False)
                return pe.matmul(dst, a_lo, b_hi, start=False, stop=stop_)

            def turn_rows():
                xns[0] += TT
                pe.wait_ge(xn_done, xns[0])
                for k in range(KC):
                    for t in range(TT):
                        o = (k % 2) * SEQ + t * P
                        ins = pe.transpose(bank[k // 2][:, o:o + P], h[:, t, k * P:(k + 1) * P], ident)
                    ins.then_inc(tp_done, 1)
                turned[0] += 1

            xns, turned = [0], [0]

            def lhs(k, t):
                s = slice(t * P, (t + 1) * P)
                return hT_hi[:, k, s], hT_lo[:, k, s]

            def lhs_listed(k, t):
                s = slice((k % 2) * P, (k % 2 + 1) * P)
                return hT_hi[:, k // 2, s], hT_lo[:, k // 2, s]

            def up(dst, left, ntt, n, waits_rows=False):
                for a in range(2):
                    if waits_rows:
                        pe.wait_ge(hl_done, 2 * (turned[0] - 1) + 1 + a)
                    t_, _, q, _ = ring.next()
                    pe.wait_ge(lo_done, FREE_RAW + t_ + 1)
                    for k in range(4):
                        s = slice(k * n, (k + 1) * n)
                        for t in range(ntt):
                            ins = product(dst[t][:, 0:n], *left(4 * a + k, t), w_hi[:, q, s], w_lo[:, q, s],
                                          a == 0 and k == 0, a == 1 and k == 3)
                    ins.then_inc(w_used, 1)

            def down(at, nd, ntt, dst, first, last):
                pe.wait_ge(hidl_done, at + ntt)
                for b in range(nd):
                    t_, _, q, _ = ring.next()
                    pe.wait_ge(lo_done, FREE_RAW + t_ + 1)
                    for i in range(2):
                        f = 2 * b + i
                        for t in range(ntt):
                            o = slice(t * P, (t + 1) * P)
                            for c in range(2):
                                s = slice(i * D + c * COL, i * D + (c + 1) * COL)
                                ins = product(dst(t, c), hid_hi[:, f, o], hid_lo[:, f, o], w_hi[:, q, s], w_lo[:, q, s],
                                              first and f == 0, last and f == 2 * nd - 1)
                    ins.then_inc(w_used, 1)

            def turn_hidden(at, ntt, n, src, width_, dst):
                for t in range(ntt):
                    pe.wait_ge(sq_done, at + t + 1)
                    for f in range(n):
                        ins = pe.transpose(dst[t][:, f * P:(f + 1) * P],
                                           scr(src + t * width_ + f * P, P), ident)
                    ins.then_inc(ht_done, 1)

            pe.wait_ge(c_in, 16)
            pe.wait_ge(r_in, 16 * R_LOADS)
            pe.transpose(bank[7][:, 0:NG], slab[0:NG, S_RAW:S_RAW + P], ident[0:NG, 0:NG]).then_inc(gc_t, 1)

            jobs_done, idx_done = [0], [0]
            groups_done = 0
            ub = 0
            for l in LAYERS:
                m = l % DEPTH
                widths = groups(width(l))
                if 0 < l <= DEPTH:
                    pe.wait_ge(ada_e, 5 * l)
                turn_rows()
                pe.wait_ge(hl_done, 2 * turned[0])
                ring.stage()

                def project(c, n, g):
                    pe.wait_ge(pge_done, FREE_BANKS + TT * (groups_done + c - 1))
                    up([bank[4 + 2 * g], bank[5 + 2 * g]], lhs, TT, n)

                group_loop(pe, ring, widths, 0, project)
                groups_done += len(widths)

                pe.wait_ge(rope_v, l + 1)
                pe.wait_ge(rope_p, l + 1)
                pe.wait_ge(pge_done, proj_evac(l))
                ps = pairs(l)
                for i, (where, c) in enumerate(ps):
                    b = i // 2
                    if i % 2 == 0 and b >= 4:
                        pe.wait_ge(qte_done, BANKS0[l] + b - 3)
                    for t in range(TT):
                        src = prj[:, t, c:c + P] if where == "big" else h[:, t, c:c + P]
                        o = (i % 2) * SEQ + t * P
                        ins = pe.transpose(bank[b % 4][:, o:o + P], src, ident)
                    if i % 2 or i == len(ps) - 1:
                        ins.then_inc(qt_done, 1)
                pe.wait_ge(qte_done, BANKS0[l] + (len(ps) + 1) // 2)

                if l >= DEPTH:
                    for i in range(I2):
                        n = idx_done[0] = idx_done[0] + 1
                        if i >= 2:
                            pe.wait_ge(ixe_done, n - 2)
                        s = slice(HD * (i % 2), HD * (i % 2) + HD)
                        for t in range(TT):
                            ins = pe.matmul(bank[6 + i % 2][:, t * SEQ:(t + 1) * SEQ], qkT[s, 4 + i // 2, t * P:(t + 1) * P],
                                            qkT[s, 6, :], start=True, stop=True)
                        ins.then_inc(ix_done, 1)

                js = jobs(l)
                j0 = jobs_done[0]
                for n in range(len(js) + 2):
                    if n < len(js):
                        qp, kp, base, dims, _, _, _, _, _ = js[n]
                        b = (j0 + n) % 2
                        if n >= 2:
                            pe.wait_ge(nm_done, j0 + n - 1)
                        s = slice(base, base + dims)
                        for t in range(TT):
                            ins = pe.matmul(bank[b][:, t * SEQ:(t + 1) * SEQ], qkT[s, qp, t * P:(t + 1) * P], qkT[s, kp, :],
                                            start=True, stop=True)
                        ins.then_inc(sc_done, 1)
                    if 1 <= n <= len(js):
                        i = n - 1
                        b = (j0 + i) % 2
                        pe.wait_ge(ex_done, TT * (j0 + i + 1))
                        if i >= 2:
                            pe.wait_ge(pte_done, j0 + i - 1)
                        for t in range(TT):
                            for k in range(TT):
                                ins = pe.transpose(bank[2 + b][:, k * SEQ + t * P:k * SEQ + (t + 1) * P],
                                                   scr(X_P + b * COL + t * SEQ + k * P, P), ident)
                        ins.then_inc(pt_done, 1)
                    if n >= 2:
                        i = n - 2
                        b = (j0 + i) % 2
                        vc = js[i][4]
                        pe.wait_ge(pte_done, j0 + i + 1)
                        if i >= 2:
                            pe.wait_ge(y_done, TT * (j0 + i - 1))
                        for t in range(TT):
                            for k in range(TT):
                                ins = pe.matmul(bank[4 + b][:, t * HD:(t + 1) * HD],
                                                scr(X_PT + b * COL + k * SEQ + t * P, P), prj[:, k, vc:vc + HD],
                                                start=k == 0, stop=k == TT - 1)
                        ins.then_inc(av_done, 1)
                jobs_done[0] += len(js)

                turn_rows()
                ring.stage()
                for c in range(D // COL):
                    up([bank[4 + 2 * c], bank[5 + 2 * c]], lhs, TT, COL, waits_rows=c == 0)
                turn_rows()

                J = steps(l)
                if l < MOE:
                    nd = 2 if l < DEPTH else 1
                    nf, wid = (4, F_UP) if l < DEPTH else (2, F_GATED)
                    a2 = X_ACT2
                    ring.stage(RAW, SPLIT if l < DEPTH else 3)

                    def step(j, first=False):
                        up([bank[0], bank[1]], lhs, TT, COL, waits_rows=isinstance(j, int) and j == 0)
                        if not (isinstance(j, int) and j == 0):
                            down(ub + TT * (j - 1), nd, TT, lambda t, c: bank[4 + 2 * t + c][:, :], first, False)
                        turn_hidden(ub + TT * j, TT, nf, a2, wid, [bank[2], bank[3]])

                    step(0)
                    step(1, True)
                    with pe.Fori(0, J - 2) as j:
                        ring.enter(j, 2 + nd)
                        step(j + 2)
                    ring.leave(J - 2)
                    down(ub + TT * (J - 1), nd, TT, lambda t, c: bank[4 + 2 * t + c][:, :], False, True)
                    ub += TT * J
                    if l < DEPTH:
                        pe.wait_ge(ada_used, NPIECE * 9 * (l + 1))
                        pe.wait_ge(act_done, ub)
                        for c in range(48):
                            ins = pe.matmul(bank[0][:, c:c + 1], big[:, c * P:(c + 1) * P], ones[:, 0:1], start=True, stop=True)
                        ins.then_inc(ada_t, 1)
                        for i in range(4):
                            if i == 3:
                                pe.wait_ge(ada_e, 5 * l + 2)
                            o = (2 + 3 * (i // 2)) * D + (i % 2) * COL
                            pe.matmul(bank[1 + i % 3][:, :], ones, big[:, o:o + COL], start=True, stop=True).then_inc(ada_t, 1)
                        if l == DEPTH - 1:
                            xns[0] += TT
                    continue

                pe.wait_ge(hl_done, 2 * turned[0])
                for t in range(TT):
                    for k in range(KC):
                        ins = product(bank[4][:, t * NE:(t + 1) * NE], *lhs(k, t), wr_hi[:, k, :], wr_lo[:, k, :],
                                      k == 0, k == KC - 1)
                ins.then_inc(lg_done, 1)
                pe.wait_ge(sel_done, 2)
                sel = rt[:, 5]
                pe.matmul(bank[5][:, 0:NE], before, sel[:, 0, :], start=True, stop=True)
                pe.matmul(bank[5][:, NE:2 * NE], ones, sel[:, 0, :], start=True, stop=False)
                pe.matmul(bank[5][:, NE:2 * NE], before, sel[:, 1, :], start=False, stop=True)
                pe.matmul(bank[5][:, 2 * NE:3 * NE], ones, sel[:, 0, :], start=True, stop=False)
                pe.matmul(bank[5][:, 2 * NE:3 * NE], ones, sel[:, 1, :], start=False, stop=True).then_inc(cnt_done, 1)
                pe.nop().then_inc(st_done, 1)

                def expert(n, t0):
                    ring.t, ring.i, ring.split = t0, 0, 3
                    pe.wait_ge(g_done, 4 * n + 4)
                    for k in range(KC):
                        for t in range(TT):
                            ins = pe.matmul(bank[2 + k // 4][:, (k % 4) * P:(k % 4 + 1) * P], h[:, t, k * P:(k + 1) * P],
                                            scr(X_G + t * P, P), start=t == 0, stop=t == TT - 1)
                    ins.then_inc(ga_done, 1)
                    for t in range(TT):
                        ins = pe.transpose(bank[1][:, t * P:(t + 1) * P], scr(X_GW + t * P, P), ident)
                    ins.then_inc(gt_t, 1)
                    pe.wait_ge(gl_done, n + 1)
                    pe.wait_ge(gt_e, n + 1)

                    def step(j, first=False):
                        up([bank[0]], lhs_listed, 1, COL)
                        if not (isinstance(j, int) and j == 0):
                            down(ub + n * MJ + j - 1, 1, 1, lambda t, c: bank[2 + c][:, :], first, False)
                        turn_hidden(ub + n * MJ + j, 1, 2, X_MACT2, F_GATED, [bank[1]])

                    step(0)
                    step(1, True)
                    with pe.Fori(0, MJ - 2) as j:
                        ring.enter(j, 3)
                        step(j + 2)
                    ring.leave(MJ - 2)
                    down(ub + n * MJ + MJ - 1, 1, 1, lambda t, c: bank[2 + c][:, :], False, True)
                    pe.wait_ge(ye_done, 2 * n + 2)
                    pe.wait_ge(ma_done, 4 * n + 1)
                    for t in range(TT):
                        for c in range(2):
                            ins = pe.matmul(bank[4 + 2 * t + c][:, :], scr(X_GT + t * P, P), scr(X_YE + c * COL, COL),
                                            start=True, stop=True)
                    ins.then_inc(st_done, 1)

                t0 = ring.t
                with pe.Fori(0, NE) as e:
                    expert(e, t0 + e * MT)
                if OVERFLOW:
                    pe.wait_ge(flag_done, 1)
                    full = pe.value_load(flag[0:1, 0:1], min_val=0, max_val=SEQ)
                    with pe.If(full > P):
                        with pe.Fori(0, NE) as e:
                            expert(e + NE, t0 + NE * MT + e * MT)


_INS = ["x", "norm1", "w_in", "q_norm", "k_norm", "out_norm_a", "out_norm_b", "w_out", "norm2", "w_mlp_in",
        "w_mlp_out", "final_norm", "c_2", "positions_2", "w_in_2", "w_out_2", "diff_lambda_2", "diff_subln_2",
        "w_ada_2", "b_ada_2", "g_attn_2", "g_ffn_2", "w_ff_gate_2", "w_ff_up_2", "w_ff_down_2", "w_router_2",
        "w_exp_gate_2", "w_exp_up_2", "w_exp_down_2", "g_final_2"]


def kernel(**inputs):
    import concourse.bacc as _bacc
    from concourse.bass_utils import run_bass_kernel_spmd as _run

    nc = _bacc.Bacc("TRN2", target_bir_lowering=False, num_devices=1)
    arrays = {f"in_{n}": np.ascontiguousarray(inputs[n]) for n in _INS}
    arrays["in_consts"] = constants()
    A = {n[3:]: nc.dram_tensor(n, a.shape, mybir.dt.from_np(a.dtype), kind="ExternalInput").ap()
         for n, a in arrays.items()}
    out = nc.dram_tensor("out_0", (1, SEQ, D), F32, kind="ExternalOutput").ap()
    build(nc, A, out)
    r = _run(nc, [arrays], core_ids=[0])
    return r.results[0]["out_0"]
```

```python
from contextlib import ExitStack

import numpy as np

import concourse.bass as bass
from concourse import mybir

F32 = mybir.dt.float32
F32R = mybir.dt.float32r
I32 = mybir.dt.int32
ALU = mybir.AluOpType
ACT = mybir.ActivationFunctionType
AX = mybir.AxisListType

P = 128
D = 1024
SEQ = 256
TT = SEQ // P
KC = D // P
DEPTH = 2
HD = 64
HA, KVA, HB = 8, 2, 8
QA1, KA1, VA1 = 0, HA * HD, (HA + KVA) * HD
QB1 = VA1 + KVA * HD
KB1, VB1 = QB1 + HB * HD, QB1 + 2 * HB * HD
IN1 = VB1 + HB * HD
FF1 = 4 * D
A2, I2, B2, C2 = 6, 4, 4, 6
QA2 = 0
KA2 = QA2 + A2 * HD
VA2 = KA2 + HD
QI2 = VA2 + HD
KI2 = QI2 + I2 * HD
WI2 = KI2 + HD
QB2 = WI2 + I2
KB2 = QB2 + B2 * HD
VB2 = KB2 + B2 * HD
QC2 = VB2 + B2 * HD
KC2 = QC2 + C2 * HD
VC2 = KC2 + C2 * HD
IN2 = VC2 + C2 * HD
FF2 = 2816
NE = 8
TOPK = SEQ // 4
ADA = 6 * D
COLUMN_VECTORS = (0, 1, 3, 4)
EPS, SUB_EPS = 1e-6, 1e-5
MASKED, TAKEN = -1e30, -3e38

TILE = 2048
RAW = 4
MORE_RAW = 6
FREE_RAW, FREE_SPLIT, FREE_BANKS = 6, 4, 4
V_LOADS = 4 * DEPTH + 2
R_LOADS = 4 + 2 * DEPTH + 1
SPLIT = 4
COL = 512
PIECE = 2048
NPIECE = ADA // PIECE
F_UP = 512
F_GATED = 256

_at = {}
_n = 0
for _name, _w in (("ident", P), ("ones", P), ("before", P), ("iota", P), ("dilated", TT * SEQ), ("causal", TT * SEQ),
                  ("ax_cos", TT * HD), ("ax_sin", TT * HD), ("pr_cos", TT * 16), ("pr_sin", TT * 16),
                  ("inv64", 8), ("inv32", 4), ("earlier", NE * NE)):
    _at[_name] = (_n, _w)
    _n += _w
CONST_W = _n

G_NORM1, G_NORM2, G_OUT, G_ATTN, G_FFN, G_C = 0, 16, 32, 48, 64, 80
NG = 88

S_RAW = RAW * TILE
X_QKT = 0
X_SM, X_P, X_PT = 4352, 5376, 6400
X_SELW = 7424
X_HTF = 6144
X_ADA, X_ACT, X_ACT2 = 0, 6144, 7168
X_MACT, X_MACT2, X_G, X_GW, X_YE, X_HGF = 4096, 4352, 4608, 4864, 5376, 6400
X_GT = (5120, 7424)
SCRATCH = 8192
X_LAM, X_ANG, X_WR, X_POS, X_LAMS = 512, 1024, 1280, 1408, 1424
C_RT = TT * IN2


def constants():
    f = np.float32
    out = np.zeros((P, CONST_W), f)

    def put(name, a):
        o, w = _at[name]
        out[:, o:o + w] = np.asarray(a, f).reshape(-1, w) if np.ndim(a) > 1 else np.asarray(a, f)[None, :]

    def by_token(a):
        return a.reshape(TT, P, -1).transpose(1, 0, 2).reshape(P, -1)

    put("ident", np.eye(P))
    put("ones", np.ones((P, P)))
    put("before", np.triu(np.ones((P, P)), 1))
    put("iota", np.arange(P))
    q, k = np.arange(SEQ)[:, None], np.arange(SEQ)[None, :]
    off = np.abs(q - k)
    times = np.zeros((SEQ, SEQ))
    for window, dil in ((128, 1), (512, 4), (2048, 16)):
        times += (off % dil == 0) & (off // dil <= window // (2 * dil))
    bias = np.where(times > 0, np.log(np.maximum(times, 1)) * HD ** 0.5, MASKED)
    put("dilated", by_token(bias))
    put("causal", by_token(np.where(k <= q, 0.0, MASKED)))

    def rope(pos, half, theta):
        freqs = (f(theta) ** (-np.arange(half, dtype=f) / f(half))).astype(f)
        ang = pos.astype(f)[:, None] * freqs[None, :]
        c, s = np.cos(ang), np.sin(ang)
        return np.concatenate([c, c], 1), np.concatenate([-s, s], 1)

    pos = np.arange(SEQ)
    rc, rs = rope(pos // 64, 16, 10000.0)
    cc, cs = rope(pos % 64, 16, 10000.0)
    put("ax_cos", by_token(np.concatenate([rc, cc], 1)))
    put("ax_sin", by_token(np.concatenate([rs, cs], 1)))
    pc, ps = rope(pos, 8, 500000.0)
    put("pr_cos", by_token(pc))
    put("pr_sin", by_token(ps))
    put("inv64", 1.0 / (500000.0 ** (np.arange(0, 16, 2, dtype=f) / 16)))
    put("inv32", 1.0 / (500000.0 ** (np.arange(0, 8, 2, dtype=f) / 8)))
    put("earlier", (np.arange(NE)[None, :] < np.arange(NE)[:, None]).reshape(-1))
    return out


class Tiles:

    def __init__(self):
        self.t, self.i, self.start = 0, 0, 0
        self.loads = [0] * MORE_RAW
        self.raw, self.split, self.old = RAW, SPLIT, SPLIT

    def stage(self, raw=RAW, split=SPLIT):
        self.old = self.split
        self.i, self.raw, self.split, self.start = 0, raw, split, self.t

    def freed(self):
        return self.t - (self.old if self.i < 2 else self.split) + 1

    def next(self):
        s = self.i % self.raw
        self.loads[s] = self.loads[s] + 1
        got = (self.t, s, self.i % self.split, self.loads[s])
        self.t = self.t + 1
        self.i += 1
        return got

    def enter(self, it, n):
        per = [sum((self.i + k) % self.raw == s for k in range(n)) for s in range(MORE_RAW)]
        self.kept = (self.t, self.i, list(self.loads), n, per)
        self.t = self.t + it * n
        self.loads = [c + it * m if m else c for c, m in zip(self.loads, per)]

    def leave(self, steps):
        t, i, loads, n, per = self.kept
        self.t, self.i = t + steps * n, i + steps * n
        self.loads = [c + steps * m for c, m in zip(loads, per)]


def build(nc, A, out):
    ctx = ExitStack()
    with ctx:
        def sb(name, shape, dt=F32):
            return ctx.enter_context(nc.sbuf_tensor(name, shape, dt))

        def sem(name):
            return ctx.enter_context(nc.semaphore(name))

        x = sb("x", [P, TT, D])
        h = sb("h", [P, TT, D])
        hT_hi = sb("hT_hi", [P, KC, SEQ], F32R)
        hT_lo = sb("hT_lo", [P, KC, SEQ], F32R)
        big = sb("big", [P, ADA])
        slab = sb("slab", [P, S_RAW + SCRATCH])
        w_hi = sb("w_hi", [P, SPLIT, TILE], F32R)
        w_lo = sb("w_lo", [P, SPLIT, TILE], F32R)
        hid_hi = sb("hid_hi", [P, 4, SEQ], F32R)
        hid_lo = sb("hid_lo", [P, 4, SEQ], F32R)
        const = sb("const", [P, CONST_W])
        rowg = sb("rowg", [P, D])
        gcol = sb("gcol", [P, NG])
        modcol = sb("modcol", [P, DEPTH, 4 * KC])
        modg = sb("modg", [P, DEPTH, 2, KC])
        qkg = sb("qkg", [P, DEPTH, 2, HD])
        subg = sb("subg", [P, DEPTH, HD])
        nlam = sb("nlam", [P, DEPTH])
        posi = sb("posi", [P, TT], I32)
        rope64 = sb("rope64", [P, 2, TT, 16])
        rope32 = sb("rope32", [P, 2, TT, 8])
        wr_hi = sb("wr_hi", [P, KC, NE], F32R)
        wr_lo = sb("wr_lo", [P, KC, NE], F32R)
        stat = sb("stat", [P, 3, 20])
        att = sb("att", [P, 4, 20, TT])
        half = sb("half", [P, 1])
        flag = sb("flag", [1, 1], I32)

        def k_(name, *shape):
            o, w = _at[name]
            a = const[:, o:o + w]
            if len(shape) == 2:
                a = a.rearrange("p (a b) -> p a b", a=shape[0])
            return a

        ident, ones, before, iota = k_("ident"), k_("ones"), k_("before"), k_("iota")

        def scr(o, n, *shape):
            a = slab[:, S_RAW + o:S_RAW + o + n]
            if len(shape) == 2:
                a = a.rearrange("p (a b) -> p a b", a=shape[0])
            if len(shape) == 3:
                a = a.rearrange("p (a b c) -> p a b c", a=shape[0], b=shape[1])
            return a

        def raw(s):
            return slab[:, s * TILE:(s + 1) * TILE]

        csilu = sb("csilu", [P, KC])
        lam = scr(X_LAM, DEPTH * 4 * 32, DEPTH, 4 * 32)
        ang = scr(X_ANG, 4 * TT * 12, 4, TT * 12)
        posf = scr(X_POS, TT)
        lgT = slab[0:NE, S_RAW + X_YE:S_RAW + X_YE + SEQ]
        lams = scr(X_LAMS, 4 * DEPTH)
        wr = scr(X_WR, KC * NE, KC, NE)
        rt = big[:, C_RT:C_RT + 14 * TT * NE].rearrange("p (i t e) -> p i t e", i=14, t=TT)
        prj = big[:, 0:TT * IN2].rearrange("p (t n) -> p t n", t=TT)
        htf = scr(X_HTF, KC * SEQ, KC, SEQ)
        qkT = scr(X_QKT, 17 * SEQ, 17, SEQ)
        bank = [ctx.enter_context(nc.psum_tensor(f"bank{i}", [P, COL], F32)) for i in range(8)]
        gates = nc.dram_tensor("gates", (DEPTH, P, 2, D), F32, kind="Internal").ap()

        w_loaded = [sem(f"w_loaded{i}") for i in range(6)]
        hi_done, lo_done = sem("hi_done"), sem("lo_done")
        hi_quarter = sem("hi_quarter")
        w_used = sem("w_used")
        c_in, r_in, v_in = sem("c_in"), sem("r_in"), sem("v_in")
        x_in = sem("x_in")
        row_in, row_used = sem("row_in"), sem("row_used")
        gc_t, gc_d = sem("gc_t"), sem("gc_d")
        sin_a, sin_d, sin_h = sem("sin_a"), sem("sin_d"), sem("sin_h")
        lam_s, lam_e = sem("lam_s"), sem("lam_e")
        half_d = sem("half_d")
        ss_done, ms_done, rstd_done, xn_done = sem("ss_done"), sem("ms_done"), sem("rstd_done"), sem("xn_done")
        tp_done, tpe_done, hh_done, hl_done = sem("tp_done"), sem("tpe_done"), sem("hh_done"), sem("hl_done")
        pge_done = sem("pge_done")
        xu_done = sem("xu_done")
        rope_v, rope_p = sem("rope_v"), sem("rope_p")
        qt_done, qte_done = sem("qt_done"), sem("qte_done")
        sc_done, nm_done, ex_done, pt_done = sem("sc_done"), sem("nm_done"), sem("ex_done"), sem("pt_done")
        pte_done, av_done, y_done = sem("pte_done"), sem("av_done"), sem("y_done")
        ix_done, ixe_done = sem("ix_done"), sem("ixe_done")
        dve_chain, pool_chain = sem("dve_chain"), sem("pool_chain")
        act_done, sq_done = sem("act_done"), sem("sq_done")
        ht_done, hidh_done, hidl_done = sem("ht_done"), sem("hidh_done"), sem("hidl_done")
        ada_in = [sem(f"ada_in{i}") for i in range(NPIECE)]
        ada_used, ada_t, ada_e, gate_out = sem("ada_used"), sem("ada_t"), sem("ada_e"), sem("gate_out")
        lg_done, rex_done, sel_done, cnt_done = sem("lg_done"), sem("rex_done"), sem("sel_done"), sem("cnt_done")
        g_done, gt_t, gt_e, ga_done = sem("g_done"), sem("gt_t"), sem("gt_e"), sem("ga_done")
        gf_done, gh_done, gl_done = sem("gf_done"), sem("gh_done"), sem("gl_done")
        ye_done, st_done, ma_done = sem("ye_done"), sem("st_done"), sem("ma_done")
        moved = sem("moved")
        acc_zero, lgt_done, lge_done = sem("acc_zero"), sem("lgt_done"), sem("lge_done")
        flag_done, out_done = sem("flag_done"), sem("out_done")

        LAYERS = range(2 * DEPTH)

        def width(l):
            return IN1 if l < DEPTH else IN2

        def groups(n):
            return [min(COL, n - c) for c in range(0, n, COL)]

        GROUPS0 = {}
        n = 0
        for l in LAYERS:
            for which in (0, 1):
                GROUPS0[l, which] = n
                n += len(groups(width(l))) if which == 0 else D // COL
        def pairs(l):
            if l < DEPTH:
                return ([("big", QA1 + P * i) for i in range(4)] + [("dup", 0), ("dup", P)]
                        + [("big", QB1 + P * i) for i in range(8)])
            return ([("big", QA2 + P * i) for i in range(3)] + [("dup", 0)] + [("big", QI2 + P * i) for i in range(2)]
                    + [("dup", P)] + [("big", QB2 + P * i) for i in range(4)] + [("big", QC2 + P * i) for i in range(6)])

        BANKS0 = {l: sum((len(pairs(m)) + 1) // 2 for m in LAYERS if m < l) for l in LAYERS}

        def jobs(l):
            full = HD ** -0.5
            if l < DEPTH:
                a = [(i // 2, 4 + i // 4, HD * (i % 2), HD, VA1 + HD * (i // 4), None, full, HD * i, 0) for i in range(HA)]
                b = [(6 + i // 2, 10 + i // 2, HD * (i % 2), HD, VB1 + HD * i, "dilated", full, HA * HD + HD * i, 0)
                     for i in range(HB)]
                return a + b
            c = [(11 + i // 2, 14 + i // 2, HD * (i % 2), HD, VC2 + HD * i, "causal", full, (A2 + B2 + i) * HD, 0)
                 for i in range(C2)]
            b = [(7 + i // 4, 9 + i // 4, 32 * (i % 4), 32, VB2 + HD * (i // 2), "causal", 32 ** -0.5,
                  A2 * HD + HD * (i // 2), 1 + i % 2) for i in range(2 * B2)]
            a = [(i // 2, 3, HD * (i % 2), HD, VA2, "chosen", full, HD * i, 0) for i in range(A2)]
            return b + c + a

        GATE_BANKS = [(4, 5, 6, 7)] * (DEPTH - 1) + [(1, 2, 3, 1)]
        SC_BANKS = (0, 1, 6)
        IX_BANKS = (6, 2, 4, 5)
        LAST_BANKS = (3, 7)

        JOBS0 = {l: sum(len(jobs(m)) for m in LAYERS if m < l) for l in LAYERS}

        def steps(l):
            return FF1 // F_UP if l < DEPTH else FF2 // F_GATED

        STEPS0 = {l: sum(steps(m) for m in LAYERS if m < l) for l in LAYERS}
        MOE = 2 * DEPTH - 1
        MJ = FF2 // F_GATED
        MT = 3 * MJ

        def w_in_of(l):
            return (A["w_in"] if l < DEPTH else A["w_in_2"])[l % DEPTH].rearrange("(k p) n -> p k n", p=P)

        def w_out_of(l):
            return (A["w_out"] if l < DEPTH else A["w_out_2"])[l % DEPTH].rearrange("(k p) n -> p k n", p=P)



        NORMED = TT * (3 * len(LAYERS) + (len(LAYERS) >= DEPTH))

        def tiles_before_w_out(l):
            def ff(i):
                return steps(i) * (4 if i < DEPTH else 3)
            return sum(2 * len(groups(width(i))) + 4 + ff(i) for i in LAYERS if i < l) + 2 * len(groups(width(l)))

        def proj_evac(l, columns=None):
            before_ = sum(len(groups(width(i))) for i in LAYERS if i < l)
            return FREE_BANKS + TT * (before_ + -(-(columns or width(l)) // COL))

        def expert_ring(ring, i, p, t0, loads0, ahead=2):
            done = MT * p + ahead
            ring.t, ring.i, ring.raw, ring.split = t0 + i * (2 * MT) + done, done, MORE_RAW, 3
            ring.loads = [c + i * (2 * MT // MORE_RAW) + sum(k % MORE_RAW == s for k in range(done))
                          for s, c in enumerate(loads0)]

        def each_expert(eng, n0, body):
            body(0, 0, n0, True, False)
            with eng.Fori(0, NE // 2 - 1) as i:
                body(i, 1, 2 * i + (n0 + 1), False, False)
                body(i + 1, 0, 2 * i + (n0 + 2), False, False)
            body(NE // 2 - 1, 1, n0 + NE - 1, False, True)

        def expert_steps(eng, ring, step):
            with eng.Fori(0, (MJ - 3) // 2) as jj:
                ring.enter(jj, 6)
                step(2 * jj + 2)
                step(2 * jj + 3)
            ring.leave((MJ - 3) // 2)
            step(MJ - 1)

        def expert_after(t0, loads0):
            return t0 + NE * MT, [c + NE * MT // MORE_RAW for c in loads0]

        def silu_col(k):
            return csilu[:, k:k + 1] if isinstance(k, int) else csilu[:, bass.ds(k, 1)]

        def gate_mul(dve, at, ntt, src, dst, banks):
            for t in range(ntt):
                dve.wait_ge(act_done, at + t + 1)
                dve.tensor_tensor(scr(dst + t * F_GATED, F_GATED), scr(src + t * F_GATED, F_GATED),
                                  banks[t][:, F_GATED:2 * F_GATED], ALU.mult).then_inc(sq_done, 1)

        def rope_steps(eng, link, v, heads, half_, cos, sin, tmp):
            n = 2 * half_
            a, b = scr(tmp, heads * n, heads, n), scr(tmp + 320, heads * n, heads, n)
            link(eng.tensor_tensor(a, v[:, :, 0:n], cos.unsqueeze(1).broadcast_to([P, heads, n]), ALU.mult))
            for o, i in ((0, half_), (half_, 0)):
                s = sin[:, o:o + half_].unsqueeze(1).broadcast_to([P, heads, half_])
                link(eng.tensor_tensor(b[:, :, o:o + half_], v[:, :, i:i + half_], s, ALU.mult))
            link(eng.tensor_tensor(v[:, :, 0:n], a, b, ALU.add))

        block = ctx.enter_context(nc.Block())

        def group_loop(eng, ring, widths, body):
            full = widths.count(COL) // 2
            done = 0
            if full > 1:
                with eng.Fori(0, full) as it:
                    ring.enter(it, 4)
                    body(2 * it, COL, 0)
                    body(2 * it + 1, COL, 1)
                ring.leave(full)
                done = 2 * full
            for c in range(done, len(widths)):
                body(c, widths[c], c % 2)

        @block.sync
        def _(sp):
            ring = Tiles()

            def stage(raw_slots=RAW):
                ring.stage(raw_slots)
                if ring.t:
                    sp.wait_ge(lo_done, FREE_RAW + ring.t)

            def tile(parts):
                t, s, _, _ = ring.next()
                sp.wait_ge(lo_done, FREE_RAW + t - ring.raw + 1)
                for dst, src in parts(raw(s)):
                    sp.dma_start(dst, src).then_inc(w_loaded[s], 16)

            def cols(w, c, n):
                for a in range(2):
                    def parts(r, a=a):
                        d = r[:, 0:4 * n].rearrange("p (k n) -> p k n", k=4)
                        for b in range(2):
                            k = 4 * a + 2 * b
                            yield d[:, 2 * b:2 * b + 2, :], w[:, k:k + 2, bass.ds(c, n)]
                    tile(parts)

            def gated(wg, wu, c):
                for a in range(2):
                    def parts(r, a=a):
                        d = r.rearrange("p (k b n) -> p k b n", k=4, b=2)
                        for b, w in enumerate((wg, wu)):
                            yield d[:, :, b, :], w[:, 4 * a:4 * a + 4, bass.ds(c, F_GATED)]
                    tile(parts)

            def rows(w, r0, n):
                for b in range(n):
                    def parts(r, b=b):
                        d = r.rearrange("p (i n) -> p i n", i=2)
                        for i in (1, 0):
                            yield d[:, i:i + 1, :], w[:, bass.ds(r0 + 2 * b + i, 1), :]
                    tile(parts)

            def project(w, widths):
                stage()
                group_loop(sp, ring, widths, lambda c, n, g: cols(w, c * COL, n))

            def ada_piece(l, k, n):
                to = scr(X_ADA + n * PIECE, PIECE)
                at = NPIECE * (9 * l + k) + n
                if not isinstance(at, int) or at >= NPIECE:
                    sp.wait_ge(ada_used, at - NPIECE + 1)
                if isinstance(k, int) and k == KC:
                    sp.dma_start(to[0:1, :], A["b_ada_2"][l:l + 1, n * PIECE:(n + 1) * PIECE]).then_inc(ada_in[n], 16)
                else:
                    src = A["w_ada_2"][l].rearrange("(k p) n -> p k n", p=P)
                    sp.dma_start(to.unsqueeze(1), src[:, bass.ds(k, 1), n * PIECE:(n + 1) * PIECE]).then_inc(ada_in[n], 16)

            def row(src, n):
                if n:
                    sp.wait_ge(row_used, n)
                sp.dma_start(rowg[:, :], src).then_inc(row_in, 16)

            sp.dma_start(x[:, :, :], A["x"][0].rearrange("(t p) d -> p t d", p=P)).then_inc(x_in, 16)
            sp.dma_start(const[:, :], A["consts"]).then_inc(c_in, 16)
            g = slab[:, S_RAW:S_RAW + P]
            for at, src in ((G_NORM1, A["norm1"]), (G_NORM2, A["norm2"]), (G_ATTN, A["g_attn_2"]),
                            (G_FFN, A["g_ffn_2"])):
                sp.dma_start(g[at:at + 16, :], src.rearrange("l (k n) -> (l k) n", n=P)).then_inc(r_in, 16)
            for l in range(DEPTH):
                for i, src in enumerate((A["out_norm_a"], A["out_norm_b"])):
                    at = G_OUT + KC * l + 4 * i
                    sp.dma_start(g[at:at + 4, :], src[l].rearrange("(k n) -> k n", n=P)).then_inc(r_in, 16)
            sp.dma_start(g[G_C:G_C + KC, :], A["c_2"][0].rearrange("(k n) -> k n", n=P)).then_inc(r_in, 16)
            nrow = 0
            for l in LAYERS:
                m = l % DEPTH
                project(w_in_of(l), groups(width(l)))
                if l >= DEPTH:
                    if l == DEPTH:
                        sp.wait_ge(gate_out, 16 * DEPTH)
                    row(gates[m, :, 0, :], nrow)
                    nrow += 1
                project(w_out_of(l), groups(D))
                if l < DEPTH:
                    w1 = A["w_mlp_in"][l].rearrange("(k p) n -> p k n", p=P)
                    w2 = A["w_mlp_out"][l].rearrange("(r p) n -> p r n", p=P)
                    J = steps(l)
                    stage()
                    cols(w1, 0, F_UP)
                    sp.wait_ge(hl_done, 2 * (3 * l + 1) + 2)
                    for n in range(NPIECE):
                        ada_piece(l, 0, n)
                    with sp.Fori(0, J - 1) as j:
                        ring.enter(j, 4)
                        cols(w1, j * F_UP + F_UP, F_UP)
                        ada_piece(l, j + 1, 0)
                        rows(w2, j * 4, 1)
                        ada_piece(l, j + 1, 1)
                        rows(w2, j * 4 + 2, 1)
                        ada_piece(l, j + 1, 2)
                    ring.leave(J - 1)
                    rows(w2, 4 * (J - 1), 2)
                    for n in range(NPIECE):
                        ada_piece(l, KC, n)
                    if l == DEPTH - 1:
                        row(A["final_norm"].rearrange("(a n) -> a n", a=1).broadcast_to([P, D]), nrow)
                        nrow += 1
                elif l < MOE:
                    wg = A["w_ff_gate_2"][0].rearrange("(k p) n -> p k n", p=P)
                    wu = A["w_ff_up_2"][0].rearrange("(k p) n -> p k n", p=P)
                    wd = A["w_ff_down_2"][0].rearrange("(r p) n -> p r n", p=P)
                    J = steps(l)
                    stage(3)
                    gated(wg, wu, 0)
                    with sp.Fori(0, J - 1) as j:
                        ring.enter(j, 3)
                        gated(wg, wu, j * F_GATED + F_GATED)
                        rows(wd, j * 2, 1)
                    ring.leave(J - 1)
                    rows(wd, 2 * (J - 1), 1)
                    row(gates[m, :, 1, :], nrow)
                    nrow += 1
                else:
                    stage(MORE_RAW)

                    def expert_loads(t0, loads0, n0):
                        def weights(e):
                            return [A[n][0, bass.ds(e, 1)].rearrange("a (k p) n -> p (a k) n", p=P)
                                    for n in ("w_exp_gate_2", "w_exp_up_2", "w_exp_down_2")]

                        def body(i, p, n, first, last):
                            wg, wu, wd = weights(2 * i + p)
                            expert_ring(ring, i, p, t0, loads0)

                            def step(j, norm=False):
                                gated(wg, wu, j * F_GATED + F_GATED)
                                if norm:
                                    sp.wait_ge(sc_done, JOBS0[l] + len(jobs(l)))
                                rows(wd, j * 2, 1)

                            def final(j):
                                if not last:
                                    gated(*weights(2 * i + p + 1)[:2], 0)
                                rows(wd, j * 2, 1)

                            step(0, first and n0 == 0)
                            step(1)
                            if first and n0 == 0:
                                row(gates[m, :, 1, :], nrow)
                            expert_steps(sp, ring, lambda j: final(j) if isinstance(j, int) else step(j))

                        ring.t, ring.i, ring.loads = t0, 0, list(loads0)
                        gated(*weights(0)[:2], 0)
                        each_expert(sp, n0, body)

                    t0, loads0 = ring.t, list(ring.loads)
                    expert_loads(t0, loads0, 0)
                    nrow += 1
                    sp.wait_ge(flag_done, 1)
                    full = sp.value_load(flag[0:1, 0:1], min_val=0, max_val=SEQ)
                    with sp.If(full > P):
                        expert_loads(*expert_after(t0, loads0), NE)
            row(A["g_final_2"].rearrange("(a n) -> a n", a=1).broadcast_to([P, D]), nrow)
            for t in range(TT):
                sp.wait_ge(xn_done, NORMED + t + 1)
                sp.dma_start(out[0, t * P:(t + 1) * P, :], h[:, t, :]).then_inc(out_done, 16)
            sp.wait_ge(out_done, 16 * TT)

        @block.gpsimd
        def _(pool):
            n_chain = [0]

            def link(ins):
                n_chain[0] += 1
                ins.then_inc(pool_chain, 1)
                pool.wait_ge(pool_chain, n_chain[0])

            roots = [0]

            def root(n):
                roots[0] += 1
                pool.wait_ge(ms_done, roots[0])
                pool.tensor_tensor(stat[:, 2, 0:n], stat[:, 1, 0:n], half[:, 0:1].broadcast_to([P, n]), ALU.pow).then_inc(rstd_done, 1)

            def norm_roots():
                for t in range(TT):
                    roots[0] += 1
                    pool.wait_ge(ms_done, roots[0])
                    pool.tensor_tensor(stat[:, 2, t:t + 1], stat[:, 1, t:t + 1], half[:, 0:1], ALU.pow).then_inc(rstd_done, 1)

            def rope(src, heads, d, half_, cos, sin):
                for t in range(TT):
                    v = prj[:, t, src:src + heads * d].rearrange("p (h d) -> p h d", h=heads)
                    rope_steps(pool, link, v, heads, half_, cos[:, t, :], sin[:, t, :], X_PT)

            for l in range(DEPTH):
                pool.dma_start(qkg[:, l, 0, :], A["q_norm"][l:l + 1, :].broadcast_to([P, HD])).then_inc(v_in, 16)
                pool.dma_start(qkg[:, l, 1, :], A["k_norm"][l:l + 1, :].broadcast_to([P, HD])).then_inc(v_in, 16)
                pool.dma_start(subg[:, l, :], A["diff_subln_2"][l:l + 1, :].broadcast_to([P, HD])).then_inc(v_in, 16)
                pool.dma_start(lam[:, l, :], A["diff_lambda_2"][l:l + 1].rearrange("a b c -> a (b c)").broadcast_to([P, 4 * 32])
                             ).then_inc(v_in, 16)
            with nc.allow_non_contiguous_dma(reason="256 positions"):
                pool.dma_start(posi[:, :].unsqueeze(2), A["positions_2"].rearrange("a (t p) -> p t a", p=P)).then_inc(v_in, 16)
            pool.dma_start(wr[:, :, :], A["w_router_2"][0].rearrange("(k p) e -> p k e", p=P)).then_inc(v_in, 16)

            def lo(t, n):
                pool.wait_ge(lo_done, FREE_RAW + t)
                for i in range(n):
                    pool.wait_ge(hi_done, t + i + 1)
                    pool.tensor_tensor(w_lo[:, i, :], raw(i), w_hi[:, i, :].bitcast(F32), ALU.subtract).then_inc(lo_done, 1)

            pool.wait_ge(half_d, 1)
            for l in LAYERS:
                if l == 0:
                    norm_roots()
                if l != DEPTH:
                    lo(tiles_before_w_out(l) - 2 * len(groups(width(l))), 2)
                if l:
                    norm_roots()
                def rope_when(n, src, heads, d, half_, cos, sin):
                    pool.wait_ge(pge_done, proj_evac(l, src + heads * d))
                    rope(src, heads, d, half_, cos, sin)
                    if n:
                        pool.nop().then_inc(rope_p, 1)

                if l < DEPTH:
                    root((HA + KVA) * TT)
                    cos, sin = k_("pr_cos", TT, 16), k_("pr_sin", TT, 16)
                    rope_when(1, QB1, HB, HD, 8, cos, sin)
                    rope_when(1, KB1, HB, HD, 8, cos, sin)
                else:
                    if l == DEPTH:
                        pool.wait_ge(sin_d, 1)
                    rope_when(1, QB2, 4 * B2, 32, 4, rope32[:, 0], rope32[:, 1])
                    rope_when(0, QC2, C2, HD, 8, rope64[:, 0], rope64[:, 1])
                    rope_when(1, KC2, C2, HD, 8, rope64[:, 0], rope64[:, 1])
                if l >= DEPTH:
                    root(TT * B2)
                lo(tiles_before_w_out(l), 4)
                if l < DEPTH:
                    root(2 * TT)
                if l == MOE:
                    pool.wait_ge(av_done, JOBS0[l] + len(jobs(l)))
                    pool.memset(big[:, 0:TT * D], 0.0).then_inc(acc_zero, 1)
                lo(tiles_before_w_out(l) + 4, 2)
                norm_roots()
                if l < DEPTH:
                    ub = 2 * STEPS0[l]

                    def square(j):
                        for t in range(TT):
                            pool.wait_ge(act_done, ub + j * TT + t + 1)
                            a = scr(X_ACT + t * F_UP, F_UP)
                            pool.tensor_tensor(scr(X_ACT2 + t * F_UP, F_UP), a, a, ALU.mult).then_inc(sq_done, 1)

                    with pool.Fori(0, steps(l)) as j:
                        square(j)
                if l == DEPTH - 1:
                    lo(tiles_before_w_out(l) + 4 + 4 * steps(l), 2)
                    norm_roots()
            norm_roots()

        @block.vector
        def _(dve):
            ring = Tiles()
            n_chain = [0]

            def mark(ins):
                n_chain[0] += 1
                ins.then_inc(dve_chain, 1)
                return n_chain[0]

            def link(ins):
                dve.wait_ge(dve_chain, mark(ins))

            def lo():
                t, s, q, _ = ring.next()
                dve.wait_ge(hi_done, t + 1)
                dve.tensor_tensor(w_lo[:, q, :], raw(s), w_hi[:, q, :].bitcast(F32), ALU.subtract).then_inc(lo_done, 1)

            def pool_tiles(n):
                for _ in range(n):
                    ring.next()

            def pool_is_through():
                dve.wait_ge(lo_done, FREE_RAW + ring.t)

            def norm(to=None):
                xns[0] += TT
                sums[0] += TT
                for t in range(TT):
                    dve.wait_ge(ss_done, sums[0] - TT + t + 1)
                    dve.tensor_scalar(stat[:, 1, t:t + 1], stat[:, 0, t:t + 1], 1.0 / D, EPS, ALU.mult, ALU.add
                                      ).then_inc(ms_done, 1)
                if updates[0]:
                    dve.wait_ge(xu_done, updates[0])
                for t in range(TT):
                    roots[0] += 1
                    dve.wait_ge(rstd_done, roots[0])
                    if to is None:
                        dve.tensor_scalar(h[:, t, :], x[:, t, :], stat[:, 2, t:t + 1], None, ALU.mult).then_inc(xn_done, 1)
                    else:
                        dve.scalar_tensor_tensor(to[:, t, :], x[:, t, :], stat[:, 2, t:t + 1], rowg[:, :], ALU.mult, ALU.mult
                                                 ).then_inc(xn_done, 1)

            sums, roots, turned, xns, updates = [0], [0], [0], [0], [0]

            def turn(gain, shift):
                m = turned[0]
                turned[0] += 1
                for k in range(KC):
                    src = bank[k // 2][:, (k % 2) * SEQ:(k % 2 + 1) * SEQ]
                    dve.wait_ge(tp_done, KC * m + k - k % 2 + 2)
                    if gain is None:
                        dve.tensor_copy(htf[:, k, :], src).then_inc(tpe_done, 1)
                    elif shift is None:
                        dve.tensor_scalar(htf[:, k, :], src, gain(k), None, ALU.mult).then_inc(tpe_done, 1)
                    else:
                        dve.tensor_scalar(htf[:, k, :], src, gain(k), shift(k), ALU.mult, ALU.add).then_inc(tpe_done, 1)
                for b in range(2):
                    ks = slice(4 * b, 4 * b + 4)
                    dve.wait_ge(hh_done, 2 * m + b + 1)
                    dve.tensor_tensor(hT_lo[:, ks, :], htf[:, ks, :], hT_hi[:, ks, :].bitcast(F32), ALU.subtract
                                      ).then_inc(hl_done, 1)

            def gain_of(at):
                return lambda k: gcol[:, at + k:at + k + 1]

            def gated_gain(l, which):
                return lambda k: modg[:, l, which, k:k + 1]

            def shift_of(l, v):
                return lambda k: modcol[:, l, KC * v + k:KC * v + k + 1]

            def x_update(c, gated_, src, wait):
                wait()
                for t in range(TT):
                    at = x[:, t, c * COL:(c + 1) * COL]
                    if gated_:
                        tmp = scr(X_SM + t * COL, COL)
                        link(dve.tensor_tensor(tmp, src(t), rowg[:, c * COL:(c + 1) * COL], ALU.mult))
                        ins = dve.tensor_tensor(at, tmp, at, ALU.add)
                    else:
                        ins = dve.tensor_tensor(at, src(t), at, ALU.add)
                    if c == D // COL - 1:
                        updated(ins)

            def updated(ins):
                updates[0] += 1
                ins.then_inc(xu_done, 1)

            mark(dve.memset(half[:, :], -0.5))
            dve.memset(stat[:, :, :], 0.0).then_inc(lo_done, FREE_RAW)
            dve.memset(ang[:, :, :], 0.0).then_inc(w_used, FREE_SPLIT)
            dve.wait_ge(lo_done, FREE_RAW)
            dve.wait_ge(w_used, FREE_SPLIT)
            dve.wait_ge(dve_chain, 1)
            dve.nop().then_inc(half_d, 1)
            dve.nop().then_inc(pge_done, FREE_BANKS)
            dve.wait_ge(gc_t, 1)
            dve.tensor_copy(gcol[:, :], bank[7][:, 0:NG]).then_inc(gc_d, 1)

            def tables():
                dve.wait_ge(v_in, 16 * V_LOADS)
                link(dve.tensor_copy(posf[:, :], posi[:, :]))
                dve.wait_ge(c_in, 16)
                inv = const[:, _at["inv64"][0]:_at["inv64"][0] + 12]
                for t in range(TT):
                    mark(dve.tensor_scalar(ang[:, 0, 12 * t:12 * t + 12], inv, posf[:, t:t + 1], None, ALU.mult))
                dve.wait_ge(dve_chain, n_chain[0])
                big_f = 12582912.0
                link(dve.tensor_scalar(ang[:, 1], ang[:, 0], float(1 / (2 * np.pi)), None, ALU.mult))
                link(dve.tensor_scalar(ang[:, 1], ang[:, 1], big_f, None, ALU.add))
                link(dve.tensor_scalar(ang[:, 1], ang[:, 1], big_f, None, ALU.subtract))
                p1 = 6.28125
                p2 = float(np.float32(round((2 * np.pi - p1) * 2 ** 21) / 2 ** 21))
                p3 = float(2 * np.pi - p1 - p2)
                for part in (p1, p2, p3):
                    link(dve.scalar_tensor_tensor(ang[:, 0], ang[:, 1], -part, ang[:, 0], ALU.mult, ALU.add))
                pi = float(np.float32(3.1415925))
                link(dve.tensor_scalar(ang[:, 0], ang[:, 0], pi, -pi, ALU.min, ALU.max))
                dve.tensor_scalar(ang[:, 1], ang[:, 0], 0.5, None, ALU.mult).then_inc(sin_a, 1)
                dve.wait_ge(sin_h, 2)
                link(dve.tensor_tensor(ang[:, 3], ang[:, 3], ang[:, 3], ALU.mult))
                link(dve.tensor_scalar(ang[:, 3], ang[:, 3], -2.0, 1.0, ALU.mult, ALU.add))
                for tab, o, n in ((rope64, 0, 8), (rope32, 8, 4)):
                    for t in range(TT):
                        a = 12 * t + o
                        mark(dve.tensor_copy(tab[:, 0, t, 0:n], ang[:, 3, a:a + n]))
                        mark(dve.tensor_copy(tab[:, 0, t, n:2 * n], ang[:, 3, a:a + n]))
                        mark(dve.tensor_scalar(tab[:, 1, t, 0:n], ang[:, 2, a:a + n], -1.0, None, ALU.mult))
                        mark(dve.tensor_copy(tab[:, 1, t, n:2 * n], ang[:, 2, a:a + n]))
                dve.wait_ge(dve_chain, n_chain[0])
                dve.nop().then_inc(sin_d, 1)
                for l in range(DEPTH):
                    v = lam[:, l, :].rearrange("p (a b n) -> p a b n", a=2, b=2)
                    link(dve.tensor_tensor(v[:, :, 0, :], v[:, :, 0, :], v[:, :, 1, :], ALU.mult))
                    r = dve.tensor_reduce(lams[:, 2 * l:2 * l + 2], v[:, :, 0, :], AX.X, ALU.add)
                    r.then_inc(lam_s, 1)
                dve.wait_ge(lam_e, 1)
                for l in range(DEPTH):
                    start = 0.8 - 0.6 * float(np.exp(-0.3 * l))
                    link(dve.tensor_tensor(nlam[:, l:l + 1], lams[:, 5 + 2 * l:6 + 2 * l], lams[:, 4 + 2 * l:5 + 2 * l], ALU.subtract))
                    link(dve.tensor_scalar(nlam[:, l:l + 1], nlam[:, l:l + 1], start, None, ALU.subtract))
                    link(dve.tensor_scalar(subg[:, l, :], subg[:, l, :], 1.0 - start, None, ALU.mult))
                link(dve.tensor_copy(wr_hi[:, :, :], wr[:, :, :]))
                link(dve.tensor_tensor(wr_lo[:, :, :], wr[:, :, :], wr_hi[:, :, :].bitcast(F32), ALU.subtract))

            dve.wait_ge(x_in, 16)

            jobs_done = [0]
            idx_done = [0]
            rows_used = [0]
            ub = 0
            for l in LAYERS:
                m = l % DEPTH
                widths = groups(width(l))
                if l == DEPTH:
                    norm()
                    dve.wait_ge(ada_e, 5 * DEPTH)
                    for d in range(DEPTH):
                        for which, v, at in ((0, 1, G_ATTN), (1, 3, G_FFN)):
                            mark(dve.scalar_tensor_tensor(modg[:, d, which, :], modcol[:, d, KC * v:KC * v + KC], 1.0,
                                                          gcol[:, at + KC * d:at + KC * d + KC], ALU.add, ALU.mult))
                    dve.wait_ge(dve_chain, n_chain[0])
                else:
                    norm()
                if l == 0:
                    pool_tiles(2)
                if l < DEPTH:
                    turn(gain_of(G_NORM1 + KC * m), None)
                else:
                    turn(gated_gain(m, 0), shift_of(m, 0))
                if l == 0:
                    tables()
                pool_is_through()
                t1, t2 = X_SM, X_SM + 640
                nh = HA + KVA
                vh = prj[:, :, 0:nh * HD].rearrange("p t (h d) -> p t h d", h=nh)

                def head_norms():
                    dve.wait_ge(pge_done, proj_evac(l, VA1))
                    v = prj[:, :, 0:nh * HD]
                    link(dve.tensor_tensor(scr(X_SM, TT * nh * HD, TT, nh * HD), v, v, ALU.mult))
                    link(dve.tensor_reduce(stat[:, 0, 0:TT * nh], scr(X_SM, TT * nh * HD, TT * nh, HD), AX.X, ALU.add))
                    dve.tensor_scalar(stat[:, 1, 0:TT * nh], stat[:, 0, 0:TT * nh], 1.0 / HD, EPS, ALU.mult, ALU.add
                                      ).then_inc(ms_done, 1)
                    roots[0] += 1

                def head_rope():
                    dve.wait_ge(rstd_done, roots[0])
                    r = stat[:, 2, 0:TT * nh].rearrange("p (t h) -> p t h", t=TT).unsqueeze(3).broadcast_to([P, TT, nh, HD])
                    link(dve.tensor_tensor(vh, vh, r, ALU.mult))
                    for i, (a, b) in enumerate(((0, HA), (HA, nh))):
                        for t in range(TT):
                            g = qkg[:, m, i, :].unsqueeze(1).broadcast_to([P, b - a, HD])
                            mark(dve.tensor_tensor(vh[:, t, a:b, :], vh[:, t, a:b, :], g, ALU.mult))
                    dve.wait_ge(dve_chain, n_chain[0])
                    for t in range(TT):
                        cos, sin = k_("ax_cos", TT, HD)[:, t, :], k_("ax_sin", TT, HD)[:, t, :]
                        a1 = scr(t1, nh * HD, nh, HD)
                        a2 = scr(t2, nh * HD, nh, 2, HD // 2)
                        v4 = vh[:, t].rearrange("p h (b d) -> p h b d", b=2)
                        s4 = sin.rearrange("p (b d) -> p b d", b=2)
                        mark(dve.tensor_tensor(a1, vh[:, t], cos.unsqueeze(1).broadcast_to([P, nh, HD]), ALU.mult))
                        for o, i in ((0, 16), (16, 0)):
                            s = s4[:, :, o:o + 16].unsqueeze(1).broadcast_to([P, nh, 2, 16])
                            mark(dve.tensor_tensor(a2[:, :, :, o:o + 16], v4[:, :, :, i:i + 16], s, ALU.mult))
                        dve.wait_ge(dve_chain, n_chain[0])
                        b2 = scr(t2, nh * HD, nh, HD)
                        mark(dve.tensor_tensor(vh[:, t, 0:HA], a1[:, 0:HA], b2[:, 0:HA], ALU.add))
                        for i in range(KVA):
                            for d in range(2):
                                o = P * i + HD * d
                                mark(dve.tensor_tensor(h[:, t, o:o + HD], a1[:, HA + i], b2[:, HA + i], ALU.add))
                        dve.wait_ge(dve_chain, n_chain[0])
                    dve.nop().then_inc(rope_v, 1)

                def chosen_rope(src, heads):
                    for t in range(TT):
                        v = prj[:, t, src:src + heads * HD].rearrange("p (h d) -> p h d", h=heads)
                        rope_steps(dve, link, v, heads, 8, rope64[:, 0, t, :], rope64[:, 1, t, :], X_SM)

                def dsa_rope():
                    dve.wait_ge(pge_done, proj_evac(l, QB2))
                    chosen_rope(QA2, A2 + 1)

                def index_rope():
                    chosen_rope(QI2, I2 + 1)
                    for t in range(TT):
                        for i, src in enumerate((KA2, KI2)):
                            for d in range(2):
                                o = P * i + HD * d
                                mark(dve.tensor_copy(h[:, t, o:o + HD], prj[:, t, src:src + HD]))
                    wi = prj[:, :, WI2:WI2 + I2]
                    mark(dve.tensor_scalar(wi, wi, I2 ** -0.5, None, ALU.mult))
                    dve.wait_ge(dve_chain, n_chain[0])
                    dve.nop().then_inc(rope_v, 1)

                between = {2: (head_norms, head_rope)} if l < DEPTH else {2: (dsa_rope,), 3: (index_rope,)}
                for c in range(len(widths)):
                    if c < len(widths) - 1:
                        lo()
                        lo()
                    for part in between.get(c, ()):
                        part()

                picks = []
                if l >= DEPTH:
                    selw = selm = scr(X_SELW, TT * SEQ, TT, SEQ)
                    for i in range(I2):
                        n = idx_done[0] = idx_done[0] + 1
                        r = scr(X_SM, TT * SEQ, TT, SEQ)
                        dve.wait_ge(ix_done, n)
                        last = dve.tensor_scalar(r, bank[IX_BANKS[i]][:, :].rearrange("p (t n) -> p t n", t=TT),
                                                 HD ** -0.5, 0.0, ALU.mult, ALU.max)
                        last.then_inc(ixe_done, 1)
                        dve.wait_ge(ixe_done, n)
                        for t in range(TT):
                            w = prj[:, t, WI2 + i:WI2 + i + 1]
                            if i == 0:
                                mark(dve.tensor_scalar(selw[:, t], r[:, t], w, None, ALU.mult))
                            else:
                                mark(dve.scalar_tensor_tensor(selw[:, t], r[:, t], w, selw[:, t], ALU.mult, ALU.add))
                        dve.wait_ge(dve_chain, n_chain[0])
                    link(dve.tensor_tensor(selw, selw, k_("causal", TT, SEQ), ALU.add))

                    def pick(t):
                        m8 = rt[:, 12 + t, :, :].rearrange("p a b -> p (a b)")[:, 0:8]
                        last = [None, None]

                        def find():
                            if waits[t]:
                                dve.wait_ge(dve_chain, waits[t])
                            waits[t] = mark(dve.max(m8, selw[:, t]))

                        def strike():
                            dve.wait_ge(dve_chain, waits[t])
                            waits[t] = mark(dve.match_replace(selw[:, t], m8, selw[:, t], TAKEN))
                        return find, strike

                    waits = [0, 0]
                    fs = [pick(t) for t in range(TT)]
                    for _ in range(TOPK // 8):
                        for phase in range(2):
                            picks += [fs[t][phase] for t in range(TT)]

                def finish_picks():
                    dve.wait_ge(dve_chain, n_chain[0])
                    link(dve.tensor_scalar(selm, selw, TAKEN / 2, MASKED, ALU.is_gt, ALU.mult))
                    link(dve.tensor_tensor(selm, selm, k_("causal", TT, SEQ), ALU.add))

                js = jobs(l)
                j0 = jobs_done[0]

                yd = h[:, :, A2 * HD:(A2 + B2) * HD]
                squared = scr(4 * SEQ, TT * B2 * HD)

                yh = yd.rearrange("p t (h d) -> p t h d", h=B2)

                def diff_squares():
                    link(dve.tensor_tensor(squared.rearrange("p (t n) -> p t n", t=TT), yd, yd, ALU.mult))

                def diff_sums():
                    link(dve.tensor_reduce(stat[:, 0, 0:TT * B2], squared.rearrange("p (a n) -> p a n", n=HD), AX.X, ALU.add))
                    dve.tensor_scalar(stat[:, 1, 0:TT * B2], stat[:, 0, 0:TT * B2], 1.0 / HD, SUB_EPS, ALU.mult, ALU.add
                                      ).then_inc(ms_done, 1)
                    roots[0] += 1

                def diff_scale():
                    dve.wait_ge(rstd_done, roots[0])
                    r = stat[:, 2, 0:TT * B2].rearrange("p (t h) -> p t h", t=TT).unsqueeze(3).broadcast_to([P, TT, B2, HD])
                    link(dve.tensor_tensor(yh, yh, r, ALU.mult))

                def diff_gain(t):
                    g = subg[:, m, :].unsqueeze(1).broadcast_to([P, B2, HD])
                    link(dve.tensor_tensor(yh[:, t], yh[:, t], g, ALU.mult))

                first_diff = 2 * B2 + 8
                diff_steps = (diff_squares, diff_sums, diff_scale, lambda: diff_gain(0), lambda: diff_gain(1)) if l >= DEPTH else ()
                ring.stage()
                pool_tiles(4)
                for n in range(len(js) + 3):
                    if n < len(js):
                        _, _, _, _, _, mask, scale, _, _ = js[n]
                        b = (j0 + n) % 2
                        if mask == "chosen" and js[n - 1][5] != "chosen":
                            finish_picks()
                        sm = scr(X_SM + b * COL, COL, TT, SEQ)
                        dve.wait_ge(sc_done, j0 + n + 1)
                        if n >= 2:
                            dve.wait_ge(ex_done, TT * (j0 + n - 1))
                        else:
                            dve.wait_ge(dve_chain, n_chain[0])
                        mx = att[:, 0, n, :]
                        ps = bank[SC_BANKS[n % 3]][:, :].rearrange("p (t n) -> p t n", t=TT)
                        for t in range(TT):
                            if mask is None:
                                mark(dve.tensor_scalar(sm[:, t], ps[:, t], scale, TAKEN, ALU.mult, ALU.max, accum_out=mx[:, t:t + 1]))
                            else:
                                mk = selm if mask == "chosen" else k_(mask, TT, SEQ)
                                mark(dve.tensor_tensor_reduce(sm[:, t], ps[:, t], mk[:, t], scale, TAKEN,
                                                              ALU.add, ALU.max, mx[:, t:t + 1]))
                        dve.wait_ge(dve_chain, n_chain[0])
                        dve.tensor_scalar(att[:, 1, n, :], mx, -1.0, None, ALU.mult).then_inc(nm_done, 1)
                    for _ in range(2 + n % 2):
                        if picks:
                            picks.pop(0)()
                    if n >= 3:
                        i = n - 3
                        _, _, _, _, _, _, _, yc, part = js[i]
                        b = (j0 + i) % 2
                        dve.wait_ge(ex_done, TT * (j0 + i + 1))
                        link(dve.reciprocal(att[:, 3, i, :], att[:, 2, i, :]))
                        if part == 2:
                            link(dve.tensor_scalar(att[:, 3, i, :], att[:, 3, i, :], nlam[:, m:m + 1], None, ALU.mult))
                        dve.wait_ge(av_done, j0 + i + 1)
                        for t in range(TT):
                            o = bank[4 + b][:, t * HD:(t + 1) * HD]
                            y = h[:, t, yc:yc + HD]
                            w = att[:, 3, i, t:t + 1]
                            if part == 2:
                                dve.wait_ge(y_done, TT * (j0 + i))
                                ins = dve.scalar_tensor_tensor(y, o, w, y, ALU.mult, ALU.add)
                            else:
                                ins = dve.tensor_scalar(y, o, w, None, ALU.mult)
                            ins.then_inc(y_done, 1)
                    if 0 <= n - first_diff < len(diff_steps):
                        dve.wait_ge(y_done, TT * (j0 + n - 2))
                        diff_steps[n - first_diff]()
                jobs_done[0] += len(js)
                dve.wait_ge(y_done, TT * jobs_done[0])
                if l < DEPTH:
                    dve.wait_ge(ss_done, sums[0] + 2 * TT)
                    sums[0] += 2 * TT
                    dve.tensor_scalar(stat[:, 1, 0:2 * TT], stat[:, 0, 0:2 * TT], 1.0 / (HA * HD), EPS, ALU.mult, ALU.add
                                      ).then_inc(ms_done, 1)
                    roots[0] += 1
                    dve.wait_ge(rstd_done, roots[0])
                    for t in range(TT):
                        for i in range(2):
                            y = h[:, t, i * HA * HD:(i + 1) * HA * HD]
                            c = stat[:, 2, 2 * t + i:2 * t + i + 1]
                            ins = dve.tensor_scalar(y, y, c, None, ALU.mult)
                            if i:
                                ins.then_inc(xn_done, 1)
                    turn(gain_of(G_OUT + KC * m), None)
                else:
                    dve.nop().then_inc(xn_done, TT)
                    turn(None, None)

                xns[0] += TT
                if l >= DEPTH:
                    rows_used[0] += 1
                    dve.wait_ge(row_in, 16 * rows_used[0])
                J = steps(l)
                start, t0 = ring.start, ring.t
                ring.stage(RAW if l < DEPTH else 3 if l < MOE else MORE_RAW, SPLIT if l < DEPTH else 3)
                pool_tiles(2)
                for c in range(D // COL):
                    used = start + 2 * c + 2
                    x_update(c, l >= DEPTH, lambda t: bank[4 + 2 * (c % 2) + t][:, :],
                             lambda: dve.wait_ge(w_used, FREE_SPLIT + used))
                if l >= DEPTH:
                    dve.wait_ge(xu_done, updates[0])
                    dve.nop().then_inc(row_used, 1)

                norm()
                if l < DEPTH:
                    turn(gain_of(G_NORM2 + KC * m), None)
                else:
                    turn(gated_gain(m, 1), shift_of(m, 2))
                pool_is_through()

                def hid_lo_part(at, t, n, b):
                    dve.wait_ge(hidh_done, at + t + 1)
                    src = b[:, 0:n * P].rearrange("p (f n) -> p f n", f=n)
                    o = slice(t * P, (t + 1) * P)
                    dve.tensor_tensor(hid_lo[:, 0:n, o], src, hid_hi[:, 0:n, o].bitcast(F32), ALU.subtract
                                      ).then_inc(hidl_done, 1)

                if l < DEPTH:
                    def ada(k, n):
                        acc = big[:, n * PIECE:(n + 1) * PIECE]
                        w = scr(X_ADA + n * PIECE, PIECE)
                        c = None if isinstance(k, int) and k == KC else silu_col(k)
                        at = 9 * l + k
                        dve.wait_ge(ada_in[n], 16 * (at + 1))
                        if isinstance(k, int) and k == 0:
                            ins = dve.tensor_scalar(acc, w, c, None, ALU.mult)
                        else:
                            dve.wait_ge(ada_used, NPIECE * (at - 1) + n + 1)
                            if isinstance(k, int) and k == KC:
                                ins = dve.tensor_tensor(acc[0:1, :], w[0:1, :], acc[0:1, :], ALU.add)
                            else:
                                ins = dve.scalar_tensor_tensor(acc, w, c, acc, ALU.mult, ALU.add)
                        ins.then_inc(ada_used, 1)

                    def step(j, more):
                        ada(j, 0)
                        if more:
                            lo()
                        ada(j, 1)
                        if more:
                            lo()
                        ada(j, 2)
                        lo()
                        lo()
                        for t in range(TT):
                            hid_lo_part(ub + j * TT, t, 4, bank[2 + t])

                    step(0, True)
                    with dve.Fori(0, J - 2) as j:
                        ring.enter(j, 4)
                        step(j + 1, True)
                    ring.leave(J - 2)
                    step(J - 1, False)
                    for n in range(NPIECE):
                        ada(KC, n)
                    ub += J * TT
                elif l < MOE:
                    def step(j, more):
                        if more:
                            lo()
                        gate_mul(dve, ub + j * TT, TT, X_ACT, X_ACT2, [bank[0], bank[1]])
                        if more:
                            lo()
                        lo()
                        for t in range(TT):
                            hid_lo_part(ub + j * TT, t, 2, bank[2 + t])

                    with dve.Fori(0, J - 1) as j:
                        ring.enter(j, 3)
                        step(j, True)
                    ring.leave(J - 1)
                    step(J - 1, False)
                    ub += J * TT
                if l < MOE:
                    if l >= DEPTH:
                        rows_used[0] += 1
                        dve.wait_ge(row_in, 16 * rows_used[0])
                    end = ring.t
                    ring.stage()
                    pool_tiles(2)
                    for c in range(2):
                        x_update(c, l >= DEPTH, lambda t: bank[4 + 2 * t + c][:, :],
                                 lambda: dve.wait_ge(w_used, FREE_SPLIT + end))
                    if l >= DEPTH:
                        dve.wait_ge(xu_done, updates[0])
                        dve.nop().then_inc(row_used, 1)
                    if l == DEPTH - 1:
                        rows_used[0] += 1
                        dve.wait_ge(row_in, 16 * rows_used[0])
                        norm(x)
                        dve.wait_ge(xn_done, xns[0])
                        updates[0] += TT
                        dve.nop().then_inc(xu_done, TT)
                        dve.nop().then_inc(row_used, 1)
                    continue

                lg, m8, nm, ex, gt, sel, den, wts, pos, tot = (rt[:, i] for i in range(10))
                dve.wait_ge(lgt_done, 1)
                dve.tensor_copy(lgT, bank[6][0:NE, 0:SEQ]).then_inc(lge_done, 1)
                dve.wait_ge(lg_done, 1)
                link(dve.tensor_copy(lg, bank[4][:, 0:TT * NE].rearrange("p (t e) -> p t e", t=TT)))
                for t in range(TT):
                    mark(dve.max(m8[:, t, :], lg[:, t, :]))
                dve.wait_ge(dve_chain, n_chain[0])
                dve.tensor_scalar(nm[:, :, 0:1], m8[:, :, 0:1], -1.0, None, ALU.mult).then_inc(sel_done, 1)
                cmp = scr(X_MACT, 2 * NE * NE, 2, NE, NE)
                for t in range(TT):
                    mine = lg[:, t, :].unsqueeze(2).broadcast_to([P, NE, NE])
                    other = lg[:, t, :].unsqueeze(1).broadcast_to([P, NE, NE])
                    mark(dve.tensor_tensor(cmp[:, 0], other, mine, ALU.is_gt))
                    link(dve.tensor_tensor(cmp[:, 1], other, mine, ALU.is_equal))
                    link(dve.tensor_tensor(cmp[:, 1], cmp[:, 1], k_("earlier", NE, NE), ALU.mult))
                    link(dve.tensor_tensor(cmp[:, 0], cmp[:, 0], cmp[:, 1], ALU.add))
                    link(dve.tensor_reduce(gt[:, t, :], cmp[:, 0], AX.X, ALU.add))
                dve.tensor_scalar(sel, gt, 2.0, None, ALU.is_lt).then_inc(sel_done, 1)
                dve.wait_ge(sel_done, 2)
                dve.wait_ge(rex_done, TT)
                link(dve.tensor_tensor(ex, ex, sel, ALU.mult))
                link(dve.tensor_reduce(den[:, :, 0:1], ex, AX.X, ALU.add))
                link(dve.reciprocal(den[:, :, 0:1], den[:, :, 0:1]))
                for t in range(TT):
                    mark(dve.tensor_scalar(wts[:, t, :], ex[:, t, :], den[:, t, 0:1], None, ALU.mult))
                dve.wait_ge(cnt_done, 1)
                cnt = bank[5][:, 0:3 * NE].rearrange("p (t e) -> p t e", t=3)
                link(dve.tensor_scalar(pos, cnt[:, 0:2, :], 1.0, None, ALU.add))
                link(dve.tensor_tensor(pos, pos, sel, ALU.mult))
                link(dve.tensor_scalar(pos, pos, -1.0, None, ALU.add))
                link(dve.tensor_reduce(tot[0:1, 0, 0:1], cnt[0:1, 2, :], AX.X, ALU.max))
                dve.tensor_copy(flag[0:1, 0:1], tot[0:1, 0, 0:1]).then_inc(flag_done, 1)
                acc = big[:, 0:TT * D].rearrange("p (t n) -> p t n", t=TT)
                dve.wait_ge(acc_zero, 1)
                dve.nop().then_inc(ma_done, 1)

                def lists(e, n):
                    if not (isinstance(n, int) and n == 0):
                        dve.wait_ge(ga_done, n)
                        dve.wait_ge(gt_t, n)
                    pe_, we = pos[:, :, bass.ds(e, 1)], wts[:, :, bass.ds(e, 1)]
                    for t in range(TT):
                        dve.tensor_scalar(scr(X_G + t * P, P), iota, pe_[:, t], None, ALU.is_equal).then_inc(g_done, 1)
                        dve.tensor_scalar(scr(X_GW + t * P, P), iota, pe_[:, t], we[:, t], ALU.is_equal, ALU.mult
                                          ).then_inc(g_done, 1)

                def listed_rows(p, n):
                    dve.wait_ge(ga_done, n + 1)
                    if not (isinstance(n, int) and n == 0):
                        dve.wait_ge(gh_done, n)
                        dve.wait_ge(gl_done, n)
                    for k in range(KC):
                        dve.tensor_scalar(scr(X_HGF + k * P, P), bank[4 + k // 4][:, (k % 4) * P:(k % 4 + 1) * P],
                                          modg[:, m, 1, k:k + 1], modcol[:, m, KC * 2 + k:KC * 2 + k + 1], ALU.mult, ALU.add
                                          ).then_inc(gf_done, 1)
                    o = slice(KC // 2 * p, KC // 2 * (p + 1))
                    dve.wait_ge(gh_done, n + 1)
                    dve.tensor_tensor(hT_lo[:, o, :], scr(X_HGF, KC * P, KC // 2, SEQ), hT_hi[:, o, :].bitcast(F32),
                                      ALU.subtract).then_inc(gl_done, 1)

                def add_output(n):
                    dve.wait_ge(st_done, n + 1)
                    for t in range(TT):
                        for c in range(2):
                            at = acc[:, t, c * COL:(c + 1) * COL]
                            dve.wait_ge(ma_done, 4 * n + 1)
                            dve.tensor_tensor(at, bank[4 + 2 * t + c][:, :], at, ALU.add).then_inc(ma_done, 1)

                def experts(t0, loads0, n0):
                    def body(i, p, n, first, last):
                        expert_ring(ring, i, p, t0, loads0)

                        def step(j, more=True, between=None):
                            if more:
                                lo()
                            gate_mul(dve, ub + n * MJ + j, 1, X_MACT, X_MACT2, [bank[0]])
                            if between:
                                between()
                            if more:
                                lo()
                            lo()
                            hid_lo_part(ub + n * MJ + j, 0, 2, bank[1])

                        step(0)
                        if not last:
                            lists(2 * i + p + 1, n + 1)
                        step(1, between=None if first else lambda: add_output(n - 1))
                        if not last:
                            listed_rows((p + 1) % 2, n + 1)
                        expert_steps(dve, ring, lambda j: step(j, not (last and isinstance(j, int))))

                    lists(0, n0)
                    listed_rows(0, n0)
                    each_expert(dve, n0, body)
                    add_output(n0 + NE - 1)

                loads0 = [0] * MORE_RAW
                experts(t0, loads0, 0)
                full = dve.value_load(flag[0:1, 0:1], min_val=0, max_val=SEQ)
                dve.wait_ge(ma_done, 1 + 4 * NE)
                with dve.If(full > P):
                    dve.tensor_scalar(pos, pos, -float(P), None, ALU.add).then_inc(moved, 1)
                    dve.wait_ge(moved, 1)
                    expert_ring(ring, NE // 2, 0, t0, loads0, 0)
                    lo()
                    lo()
                    experts(t0 + NE * MT, loads0, NE)
                    dve.wait_ge(ma_done, 1 + 8 * NE)
                rows_used[0] += 1
                dve.wait_ge(row_in, 16 * rows_used[0])
                for t in range(TT):
                    ins = dve.tensor_tensor(acc[:, t, :], acc[:, t, :], rowg[:, :], ALU.mult)
                    link(ins)
                    if t == TT - 1:
                        dve.nop().then_inc(row_used, 1)
                    updated(dve.tensor_tensor(x[:, t, :], acc[:, t, :], x[:, t, :], ALU.add))
            rows_used[0] += 1
            dve.wait_ge(row_in, 16 * rows_used[0])
            norm(h)

        @block.scalar
        def _(act):
            ring = Tiles()

            def stage():
                ring.stage()
                act.wait_ge(w_used, FREE_SPLIT + ring.t)

            def hi():
                freed = ring.freed()
                t, s, q, n = ring.next()
                act.wait_ge(w_loaded[s], 32 * n)
                act.wait_ge(w_used, FREE_SPLIT + freed)
                act.activation(w_hi[:, q, :], raw(s), ACT.Copy).then_inc(hi_done, 1)

            quarter = [0, None]

            def hi_quarter_of_tile():
                k = quarter[0]
                quarter[0] += 1
                if k % 4 == 0:
                    t, s, q, n = quarter[1] = ring.next()
                    act.wait_ge(w_loaded[s], 32 * n)
                    act.wait_ge(w_used, FREE_SPLIT + t - ring.split + 1)
                t, s, q, n = quarter[1]
                o = slice(k % 4 * COL, (k % 4 + 1) * COL)
                act.activation(w_hi[:, q, o], raw(s)[:, o], ACT.Copy).then_inc(hi_done if k % 4 == 3 else hi_quarter, 1)

            updates = [0]

            def squares():
                if not updates[0]:
                    act.wait_ge(x_in, 16)
                    act.wait_ge(lo_done, FREE_RAW)
                for t in range(TT):
                    if updates[0]:
                        act.wait_ge(xu_done, TT * (updates[0] - 1) + t + 1)
                    act.activation(h[:, t, :], x[:, t, :], ACT.Square, accum_out=stat[:, 0, t:t + 1]).then_inc(ss_done, 1)
                updates[0] += 1

            turned = [0]

            def turn():
                m = turned[0]
                turned[0] += 1
                for b in range(2):
                    ks = slice(4 * b, 4 * b + 4)
                    act.wait_ge(tpe_done, KC * m + 4 * (b + 1))
                    act.activation(hT_hi[:, ks, :], htf[:, ks, :], ACT.Copy).then_inc(hh_done, 1)

            def ada_columns(l):
                act.wait_ge(ada_t, 5 * l + 1)
                act.activation(modcol[:, l, :], bank[0][:, 0:4 * KC], ACT.Copy).then_inc(ada_e, 1)

            def ada_gates(l):
                for i, b in enumerate(GATE_BANKS[l]):
                    act.wait_ge(ada_t, 5 * l + 2 + i)
                    act.activation(scr(X_ADA + i * COL, COL), bank[b][:, :], ACT.Copy).then_inc(ada_e, 1)
                act.wait_ge(ada_e, 5 * (l + 1))
                act.dma_start(gates[l].rearrange("p a n -> p (a n)"), scr(X_ADA, 2 * D)).then_inc(gate_out, 16)

            def tables():
                act.wait_ge(gc_d, 1)
                act.activation(csilu[:, :], gcol[:, G_C:G_C + KC], ACT.Silu)
                act.wait_ge(sin_a, 1)
                act.activation(ang[:, 2], ang[:, 0], ACT.Sin).then_inc(sin_h, 1)
                act.activation(ang[:, 3], ang[:, 1], ACT.Sin).then_inc(sin_h, 1)
                act.wait_ge(lam_s, DEPTH)
                act.activation(lams[:, 4:8], lams[:, 0:4], ACT.Exp).then_inc(lam_e, 1)

            jobs_done = [0]
            ub = 0
            for l in LAYERS:
                m = l % DEPTH
                widths = groups(width(l))
                squares()
                if l == 0:
                    hi()
                    hi()
                if 0 < l <= DEPTH:
                    ada_columns(l - 1)
                if l == DEPTH:
                    ada_gates(l - 1)
                turn()
                if 0 < l < DEPTH:
                    ada_gates(l - 1)
                if l == 0:
                    tables()

                def project(c, n, g):
                    hi()
                    hi()
                    empty(c, n, [4 + 2 * g, 5 + 2 * g], ring.start)

                def empty(c, n, banks, start):
                    act.wait_ge(w_used, FREE_SPLIT + start + 2 * c + 2)
                    for t in range(TT):
                        act.activation(prj[:, t, bass.ds(c * COL, n)], bank[banks[t]][:, 0:n], ACT.Copy).then_inc(pge_done, 1)

                start = ring.start
                group_loop(act, ring, widths[:-1], project)

                nb = (len(pairs(l)) + 1) // 2
                if 0 < l <= DEPTH:
                    act.wait_ge(gate_out, 16 * l)
                for i in range(nb):
                    w = min(2, len(pairs(l)) - 2 * i)
                    act.wait_ge(qt_done, BANKS0[l] + i + 1)
                    act.activation(qkT[:, 2 * i:2 * i + w, :], bank[i % 4][:, 0:w * SEQ].rearrange("p (a n) -> p a n", a=w),
                                   ACT.Copy).then_inc(qte_done, 1)

                js = jobs(l)
                j0 = jobs_done[0]
                for n in range(len(js) + 2):
                    if n == 2:
                        empty(len(widths) - 1, widths[-1], LAST_BANKS, start)
                        stage()
                    if n >= 2:
                        b = (j0 + n) % 2
                        act.wait_ge(pt_done, j0 + n - 1)
                        if n >= 4:
                            act.wait_ge(av_done, j0 + n - 3)
                        act.activation(scr(X_PT + b * COL, COL), bank[2 + b][:, :], ACT.Copy).then_inc(pte_done, 1)
                    if n < len(js):
                        b = (j0 + n) % 2
                        act.wait_ge(nm_done, j0 + n + 1)
                        if n >= 2:
                            act.wait_ge(pt_done, j0 + n - 1)
                        for t in range(TT):
                            act.activation(scr(X_P + b * COL + t * SEQ, SEQ), scr(X_SM + b * COL + t * SEQ, SEQ), ACT.Exp,
                                           bias=att[:, 1, n, t:t + 1], accum_out=att[:, 2, n, t:t + 1]).then_inc(ex_done, 1)
                    if 2 <= n < 18:
                        hi_quarter_of_tile()
                jobs_done[0] += len(js)
                if l < DEPTH:
                    act.wait_ge(y_done, TT * jobs_done[0])
                    for t in range(TT):
                        for i in range(2):
                            w = HA * HD
                            act.activation(scr(X_SM + (2 * t + i) * w, w), h[:, t, i * w:(i + 1) * w], ACT.Square,
                                           accum_out=stat[:, 0, 2 * t + i:2 * t + i + 1]).then_inc(ss_done, 1)
                turn()
                J = steps(l)
                t0, loads0 = ring.t, list(ring.loads)
                ring.stage(RAW if l < DEPTH else 3 if l < MOE else MORE_RAW, SPLIT if l < DEPTH else 3)
                hi()
                hi()
                squares()
                turn()

                def first_tiles():
                    ring.stage()
                    hi()
                    hi()

                def hid_high_part(at, t, n, b):
                    act.wait_ge(ht_done, at + t + 1)
                    src = b[:, 0:n * P].rearrange("p (f n) -> p f n", f=n)
                    act.activation(hid_hi[:, 0:n, t * P:(t + 1) * P], src, ACT.Copy).then_inc(hidh_done, 1)

                if l < DEPTH:
                    def step(j, more):
                        up = 2 if isinstance(j, int) and j == 0 else 4 * j
                        if more:
                            hi()
                        act.wait_ge(w_used, FREE_SPLIT + ring.start + up)
                        for t in range(TT):
                            act.activation(scr(X_ACT + t * F_UP, F_UP), bank[t][:, :], ACT.Relu).then_inc(act_done, 1)
                        if more:
                            hi()
                        hi()
                        hi()
                        for t in range(TT):
                            hid_high_part(ub + j * TT, t, 4, bank[2 + t])

                    step(0, True)
                    with act.Fori(0, J - 2) as j:
                        ring.enter(j, 4)
                        step(j + 1, True)
                    ring.leave(J - 2)
                    step(J - 1, False)
                    ub += J * TT
                    first_tiles()
                elif l < MOE:
                    def step(j, more):
                        up = 2 if isinstance(j, int) and j == 0 else 3 * j + 1
                        if more:
                            hi()
                        act.wait_ge(w_used, FREE_SPLIT + ring.start + up)
                        for t in range(TT):
                            act.activation(scr(X_ACT + t * F_GATED, F_GATED), bank[t][:, 0:F_GATED], ACT.Silu).then_inc(act_done, 1)
                        if more:
                            hi()
                        hi()
                        for t in range(TT):
                            hid_high_part(ub + j * TT, t, 2, bank[2 + t])

                    step(0, True)
                    with act.Fori(0, J - 2) as j:
                        ring.enter(j, 3)
                        step(j + 1, True)
                    ring.leave(J - 2)
                    step(J - 1, False)
                    ub += J * TT
                    first_tiles()
                else:
                    lg, nm, ex = rt[:, 0], rt[:, 2], rt[:, 3]
                    act.wait_ge(sel_done, 1)
                    for t in range(TT):
                        act.activation(ex[:, t, :], lg[:, t, :], ACT.Exp, bias=nm[:, t, 0:1]).then_inc(rex_done, 1)

                    def listed_rows(p, n):
                        act.wait_ge(gt_t, n + 1)
                        act.activation(scr(X_GT[p], TT * P), bank[6][:, 0:TT * P], ACT.Copy).then_inc(gt_e, 1)
                        act.wait_ge(gf_done, KC * (n + 1))
                        o = slice(KC // 2 * p, KC // 2 * (p + 1))
                        act.activation(hT_hi[:, o, :], scr(X_HGF, KC * P, KC // 2, SEQ), ACT.Copy).then_inc(gh_done, 1)

                    def output(n, used):
                        act.wait_ge(w_used, FREE_SPLIT + used)
                        if not (isinstance(n, int) and n == 0):
                            act.wait_ge(st_done, n)
                        for c in range(2):
                            act.activation(scr(X_YE + c * COL, COL), bank[2 + c][:, :], ACT.Copy).then_inc(ye_done, 1)

                    def experts(t0, loads0, n0):
                        def body(i, p, n, first, last):
                            expert_ring(ring, i, p, t0, loads0)
                            te = t0 + i * (2 * MT) + MT * p

                            def step(j, up, more=True):
                                if more:
                                    hi()
                                act.wait_ge(w_used, FREE_SPLIT + up)
                                act.activation(scr(X_MACT, F_GATED), bank[0][:, 0:F_GATED], ACT.Silu).then_inc(act_done, 1)
                                if more:
                                    hi()
                                hi()
                                hid_high_part(ub + n * MJ + j, 0, 2, bank[1])

                            step(0, te + (2 if first else 1))
                            if not first:
                                output(n - 1, te + 2)
                            step(1, te + 4)
                            if not last:
                                listed_rows((p + 1) % 2, n + 1)
                            expert_steps(act, ring, lambda j: step(j, te + 3 * j + 1, not (last and isinstance(j, int))))

                        listed_rows(0, n0)
                        each_expert(act, n0, body)
                        output(n0 + NE - 1, t0 + NE * MT)

                    experts(t0, loads0, 0)
                    act.wait_ge(flag_done, 1)
                    full = act.value_load(flag[0:1, 0:1], min_val=0, max_val=SEQ)
                    with act.If(full > P):
                        t1, loads1 = expert_after(t0, loads0)
                        ring.t, ring.i, ring.loads = t1, 0, list(loads1)
                        hi()
                        hi()
                        experts(t1, loads1, NE)
                if l == DEPTH - 1:
                    squares()
            squares()

        @block.tensor
        def _(pe):
            ring = Tiles()

            def product(dst, a_hi, a_lo, b_hi, b_lo, start, stop_):
                pe.matmul(dst, a_hi, b_hi, start=start, stop=False)
                pe.matmul(dst, a_hi, b_lo, start=False, stop=False)
                return pe.matmul(dst, a_lo, b_hi, start=False, stop=stop_)

            def turn_rows():
                xns[0] += TT
                pe.wait_ge(xn_done, xns[0])
                for k in range(KC):
                    for t in range(TT):
                        o = (k % 2) * SEQ + t * P
                        ins = pe.transpose(bank[k // 2][:, o:o + P], h[:, t, k * P:(k + 1) * P], ident)
                    ins.then_inc(tp_done, 1)
                turned[0] += 1

            xns, turned = [0], [0]

            def lhs(k, t):
                s = slice(t * P, (t + 1) * P)
                return hT_hi[:, k, s], hT_lo[:, k, s]

            def lhs_listed(k, t):
                s = slice((k % 2) * P, (k % 2 + 1) * P)
                return hT_hi[:, k // 2, s], hT_lo[:, k // 2, s]

            def up(dst, left, ntt, n, waits_rows=False):
                for a in range(2):
                    if waits_rows:
                        pe.wait_ge(hl_done, 2 * (turned[0] - 1) + 1 + a)
                    t_, _, q, _ = ring.next()
                    pe.wait_ge(lo_done, FREE_RAW + t_ + 1)
                    for k in range(4):
                        s = slice(k * n, (k + 1) * n)
                        for t in range(ntt):
                            ins = product(dst[t][:, 0:n], *left(4 * a + k, t), w_hi[:, q, s], w_lo[:, q, s],
                                          a == 0 and k == 0, a == 1 and k == 3)
                    ins.then_inc(w_used, 1)

            def down(at, nd, ntt, dst, first, last):
                pe.wait_ge(hidl_done, at + ntt)
                for b in range(nd):
                    t_, _, q, _ = ring.next()
                    pe.wait_ge(lo_done, FREE_RAW + t_ + 1)
                    for i in range(2):
                        f = 2 * b + i
                        for t in range(ntt):
                            o = slice(t * P, (t + 1) * P)
                            for c in range(2):
                                s = slice(i * D + c * COL, i * D + (c + 1) * COL)
                                ins = product(dst(t, c), hid_hi[:, f, o], hid_lo[:, f, o], w_hi[:, q, s], w_lo[:, q, s],
                                              first and f == 0, last and f == 2 * nd - 1)
                    ins.then_inc(w_used, 1)

            def turn_hidden(at, ntt, n, src, width_, dst):
                for t in range(ntt):
                    pe.wait_ge(sq_done, at + t + 1)
                    for f in range(n):
                        ins = pe.transpose(dst[t][:, f * P:(f + 1) * P],
                                           scr(src + t * width_ + f * P, P), ident)
                    ins.then_inc(ht_done, 1)

            pe.wait_ge(c_in, 16)
            pe.wait_ge(r_in, 16 * R_LOADS)
            pe.transpose(bank[7][:, 0:NG], slab[0:NG, S_RAW:S_RAW + P], ident[0:NG, 0:NG]).then_inc(gc_t, 1)

            def gate_rows(l, banks):
                for i, b in enumerate(banks):
                    if b in banks[:i]:
                        pe.wait_ge(ada_e, 5 * l + 2 + banks.index(b))
                    o = (2 + 3 * (i // 2)) * D + (i % 2) * COL
                    pe.matmul(bank[b][:, :], ones, big[:, o:o + COL], start=True, stop=True).then_inc(ada_t, 1)

            jobs_done, idx_done = [0], [0]
            groups_done = 0
            ub = 0
            for l in LAYERS:
                m = l % DEPTH
                widths = groups(width(l))
                if 0 < l <= DEPTH:
                    pe.wait_ge(ada_e, 5 * l - (4 if l < DEPTH else 0))
                turn_rows()
                if 0 < l < DEPTH:
                    gate_rows(l - 1, GATE_BANKS[l - 1])
                    pe.wait_ge(ada_e, 5 * l)
                pe.wait_ge(hl_done, 2 * turned[0])
                ring.stage()

                def project(c, n, g):
                    pe.wait_ge(pge_done, FREE_BANKS + TT * (groups_done + c - 1))
                    up([bank[4 + 2 * g], bank[5 + 2 * g]], lhs, TT, n)

                group_loop(pe, ring, widths[:-1], project)

                pe.wait_ge(rope_v, l + 1)
                all_but_last = proj_evac(l) - TT
                pe.wait_ge(pge_done, all_but_last)
                ps = pairs(l)
                pool_pairs = (6, 10) if l < DEPTH else (7, 11)
                for i, (where, c) in enumerate(ps):
                    b = i // 2
                    if i in pool_pairs:
                        pe.wait_ge(rope_p, 2 * l + 1 + pool_pairs.index(i))
                    if i % 2 == 0 and b >= 4:
                        pe.wait_ge(qte_done, BANKS0[l] + b - 3)
                    for t in range(TT):
                        src = prj[:, t, c:c + P] if where == "big" else h[:, t, c:c + P]
                        o = (i % 2) * SEQ + t * P
                        ins = pe.transpose(bank[b % 4][:, o:o + P], src, ident)
                    if i % 2 or i == len(ps) - 1:
                        ins.then_inc(qt_done, 1)
                pe.wait_ge(qte_done, BANKS0[l] + (len(ps) + 1) // 2)

                if l >= DEPTH:
                    for i in range(I2):
                        n = idx_done[0] = idx_done[0] + 1
                        s = slice(HD * (i % 2), HD * (i % 2) + HD)
                        for t in range(TT):
                            ins = pe.matmul(bank[IX_BANKS[i]][:, t * SEQ:(t + 1) * SEQ], qkT[s, 4 + i // 2, t * P:(t + 1) * P],
                                            qkT[s, 6, :], start=True, stop=True)
                        ins.then_inc(ix_done, 1)

                js = jobs(l)
                j0 = jobs_done[0]
                for n in range(len(js) + 3):
                    if n == 2:
                        up([bank[b] for b in LAST_BANKS], lhs, TT, widths[-1])
                        groups_done += len(widths)
                        if l >= DEPTH:
                            pe.wait_ge(ixe_done, idx_done[0])
                    if n < len(js):
                        qp, kp, base, dims, _, _, _, _, _ = js[n]
                        b = SC_BANKS[n % 3]
                        if n >= 3:
                            pe.wait_ge(nm_done, j0 + n - 2)
                        s = slice(base, base + dims)
                        for t in range(TT):
                            ins = pe.matmul(bank[b][:, t * SEQ:(t + 1) * SEQ], qkT[s, qp, t * P:(t + 1) * P], qkT[s, kp, :],
                                            start=True, stop=True)
                        ins.then_inc(sc_done, 1)
                    if 2 <= n <= len(js) + 1:
                        i = n - 2
                        b = (j0 + i) % 2
                        pe.wait_ge(ex_done, TT * (j0 + i + 1))
                        if i == 1:
                            pe.wait_ge(pge_done, proj_evac(l))
                        if i >= 2:
                            pe.wait_ge(pte_done, j0 + i - 1)
                        for t in range(TT):
                            for k in range(TT):
                                ins = pe.transpose(bank[2 + b][:, k * SEQ + t * P:k * SEQ + (t + 1) * P],
                                                   scr(X_P + b * COL + t * SEQ + k * P, P), ident)
                        ins.then_inc(pt_done, 1)
                    if n >= 3:
                        i = n - 3
                        b = (j0 + i) % 2
                        vc = js[i][4]
                        pe.wait_ge(pte_done, j0 + i + 1)
                        if i >= 2:
                            pe.wait_ge(y_done, TT * (j0 + i - 1))
                        for t in range(TT):
                            for k in range(TT):
                                ins = pe.matmul(bank[4 + b][:, t * HD:(t + 1) * HD],
                                                scr(X_PT + b * COL + k * SEQ + t * P, P), prj[:, k, vc:vc + HD],
                                                start=k == 0, stop=k == TT - 1)
                        ins.then_inc(av_done, 1)
                jobs_done[0] += len(js)

                turn_rows()
                ring.stage()
                for c in range(D // COL):
                    up([bank[4 + 2 * c], bank[5 + 2 * c]], lhs, TT, COL, waits_rows=c == 0)
                turn_rows()

                J = steps(l)
                if l < MOE:
                    nd = 2 if l < DEPTH else 1
                    nf, wid = (4, F_UP) if l < DEPTH else (2, F_GATED)
                    a2 = X_ACT2
                    ring.stage(RAW, SPLIT if l < DEPTH else 3)

                    def step(j, first=False):
                        up([bank[0], bank[1]], lhs, TT, COL, waits_rows=isinstance(j, int) and j == 0)
                        if not (isinstance(j, int) and j == 0):
                            down(ub + TT * (j - 1), nd, TT, lambda t, c: bank[4 + 2 * t + c][:, :], first, False)
                        turn_hidden(ub + TT * j, TT, nf, a2, wid, [bank[2], bank[3]])

                    step(0)
                    step(1, True)
                    with pe.Fori(0, J - 2) as j:
                        ring.enter(j, 2 + nd)
                        step(j + 2)
                    ring.leave(J - 2)
                    down(ub + TT * (J - 1), nd, TT, lambda t, c: bank[4 + 2 * t + c][:, :], False, True)
                    ub += TT * J
                    if l < DEPTH:
                        pe.wait_ge(ada_used, NPIECE * 9 * (l + 1))
                        pe.wait_ge(act_done, ub)
                        for i, v in enumerate(COLUMN_VECTORS):
                            for k in range(KC):
                                o = v * D + k * P
                                ins = pe.matmul(bank[0][:, KC * i + k:KC * i + k + 1], big[:, o:o + P], ones[:, 0:1],
                                                start=True, stop=True)
                        ins.then_inc(ada_t, 1)
                        if l == DEPTH - 1:
                            gate_rows(l, GATE_BANKS[l])
                        if l == DEPTH - 1:
                            xns[0] += TT
                    continue

                pe.wait_ge(hl_done, 2 * turned[0])
                for k in range(KC):
                    ins = product(bank[6][0:NE, 0:SEQ], wr_hi[:, k, :], wr_lo[:, k, :], hT_hi[:, k, :], hT_lo[:, k, :],
                                  k == 0, k == KC - 1)
                ins.then_inc(lgt_done, 1)
                pe.wait_ge(lge_done, 1)
                for t in range(TT):
                    ins = pe.transpose(bank[4][:, t * NE:(t + 1) * NE], lgT[:, t * P:(t + 1) * P], ident[0:NE, 0:NE])
                ins.then_inc(lg_done, 1)
                pe.wait_ge(sel_done, 2)
                sel = rt[:, 5]
                pe.matmul(bank[5][:, 0:NE], before, sel[:, 0, :], start=True, stop=True)
                pe.matmul(bank[5][:, NE:2 * NE], ones, sel[:, 0, :], start=True, stop=False)
                pe.matmul(bank[5][:, NE:2 * NE], before, sel[:, 1, :], start=False, stop=True)
                pe.matmul(bank[5][:, 2 * NE:3 * NE], ones, sel[:, 0, :], start=True, stop=False)
                pe.matmul(bank[5][:, 2 * NE:3 * NE], ones, sel[:, 1, :], start=False, stop=True).then_inc(cnt_done, 1)

                def gather(n):
                    pe.wait_ge(g_done, 4 * n + 4)
                    if isinstance(n, int) and n % NE == 0:
                        pe.wait_ge(ma_done, 4 * n + 1)
                    else:
                        pe.wait_ge(ma_done, 4 * n - 3)
                    if not (isinstance(n, int) and n == 0):
                        pe.wait_ge(gt_e, n)
                    for k in range(KC):
                        for t in range(TT):
                            ins = pe.matmul(bank[4 + k // 4][:, (k % 4) * P:(k % 4 + 1) * P], h[:, t, k * P:(k + 1) * P],
                                            scr(X_G + t * P, P), start=t == 0, stop=t == TT - 1)
                    ins.then_inc(ga_done, 1)
                    for t in range(TT):
                        ins = pe.transpose(bank[6][:, t * P:(t + 1) * P], scr(X_GW + t * P, P), ident)
                    ins.then_inc(gt_t, 1)

                def scatter(p, n):
                    pe.wait_ge(ye_done, 2 * n + 2)
                    pe.wait_ge(gt_e, n + 1)
                    pe.wait_ge(gf_done, KC * (n + 1))
                    for t in range(TT):
                        for c in range(2):
                            ins = pe.matmul(bank[4 + 2 * t + c][:, :], scr(X_GT[p] + t * P, P), scr(X_YE + c * COL, COL),
                                            start=True, stop=True)
                    ins.then_inc(st_done, 1)

                def sums(n, j, first, last):
                    down(ub + n * MJ + j, 1, 1, lambda t, c: bank[2 + c][:, :], first, last)

                def experts(t0, n0):
                    def body(i, p, n, first, last):
                        ring.t, ring.i, ring.split = t0 + i * (2 * MT) + MT * p - (not first), 0 if first else 2, 3
                        pe.wait_ge(gl_done, n + 1)

                        def rows_up(j):
                            up([bank[0]], lambda k, t: lhs_listed(k + KC * p, t), 1, COL)

                        def turn(j):
                            turn_hidden(ub + n * MJ + j, 1, 2, X_MACT2, F_GATED, [bank[1]])

                        rows_up(0)
                        if not first:
                            sums(n - 1, MJ - 1, False, True)
                        turn(0)
                        rows_up(1)
                        if not first:
                            scatter(1 - p, n - 1)
                        sums(n, 0, True, False)
                        turn(1)
                        if not last:
                            gather(n + 1)
                        with pe.Fori(0, MJ - 2) as j:
                            ring.enter(j, 3)
                            rows_up(j + 2)
                            sums(n, j + 1, False, False)
                            turn(j + 2)
                        ring.leave(MJ - 2)

                    gather(n0)
                    each_expert(pe, n0, body)
                    sums(n0 + NE - 1, MJ - 1, False, True)
                    scatter(1, n0 + NE - 1)

                t0 = ring.t
                experts(t0, 0)
                pe.wait_ge(flag_done, 1)
                full = pe.value_load(flag[0:1, 0:1], min_val=0, max_val=SEQ)
                with pe.If(full > P):
                    experts(t0 + NE * MT, NE)

_INS = ["x", "norm1", "w_in", "q_norm", "k_norm", "out_norm_a", "out_norm_b", "w_out", "norm2", "w_mlp_in",
        "w_mlp_out", "final_norm", "c_2", "positions_2", "w_in_2", "w_out_2", "diff_lambda_2", "diff_subln_2",
        "w_ada_2", "b_ada_2", "g_attn_2", "g_ffn_2", "w_ff_gate_2", "w_ff_up_2", "w_ff_down_2", "w_router_2",
        "w_exp_gate_2", "w_exp_up_2", "w_exp_down_2", "g_final_2"]


def kernel(**inputs):
    import concourse.bacc as _bacc
    from concourse.bass_utils import run_bass_kernel_spmd as _run

    nc = _bacc.Bacc("TRN2", target_bir_lowering=False, num_devices=1)
    arrays = {f"in_{n}": np.ascontiguousarray(inputs[n]) for n in _INS}
    arrays["in_consts"] = constants()
    A = {n[3:]: nc.dram_tensor(n, a.shape, mybir.dt.from_np(a.dtype), kind="ExternalInput").ap()
         for n, a in arrays.items()}
    out = nc.dram_tensor("out_0", (1, SEQ, D), F32, kind="ExternalOutput").ap()
    build(nc, A, out)
    r = _run(nc, [arrays], core_ids=[0])
    return r.results[0]["out_0"]
```

```python
from contextlib import ExitStack

import numpy as np

import concourse.bass as bass
from concourse import mybir

F32 = mybir.dt.float32
F32R = mybir.dt.float32r
I32 = mybir.dt.int32
ALU = mybir.AluOpType
ACT = mybir.ActivationFunctionType
AX = mybir.AxisListType

P = 128
D = 1024
SEQ = 256
TT = SEQ // P
KC = D // P
DEPTH = 2
HD = 64
HA, KVA, HB = 8, 2, 8
QA1, KA1, VA1 = 0, HA * HD, (HA + KVA) * HD
QB1 = VA1 + KVA * HD
KB1, VB1 = QB1 + HB * HD, QB1 + 2 * HB * HD
IN1 = VB1 + HB * HD
FF1 = 4 * D
A2, I2, B2, C2 = 6, 4, 4, 6
QA2 = 0
KA2 = QA2 + A2 * HD
VA2 = KA2 + HD
QI2 = VA2 + HD
KI2 = QI2 + I2 * HD
WI2 = KI2 + HD
QB2 = WI2 + I2
KB2 = QB2 + B2 * HD
VB2 = KB2 + B2 * HD
QC2 = VB2 + B2 * HD
KC2 = QC2 + C2 * HD
VC2 = KC2 + C2 * HD
IN2 = VC2 + C2 * HD
FF2 = 2816
NE = 8
TOPK = SEQ // 4
ADA = 6 * D
COLUMN_VECTORS = (0, 1, 3, 4)
EPS, SUB_EPS = 1e-6, 1e-5
MASKED, TAKEN = -1e30, -3e38

TILE = 2048
RAW = 4
MORE_RAW = 6
FREE_RAW, FREE_SPLIT, FREE_BANKS = 6, 4, 4
V_LOADS = 4 * DEPTH + 2
R_LOADS = 4 + 2 * DEPTH + 1
SPLIT = 4
COL = 512
PIECE = 2048
NPIECE = ADA // PIECE
F_UP = 512
F_GATED = 256

_at = {}
_n = 0
for _name, _w in (("ident", P), ("ones", P), ("before", P), ("iota", P), ("dilated", TT * SEQ), ("causal", TT * SEQ),
                  ("ax_cos", TT * HD), ("ax_sin", TT * HD), ("pr_cos", TT * 16), ("pr_sin", TT * 16),
                  ("inv64", 8), ("inv32", 4), ("earlier", NE * NE)):
    _at[_name] = (_n, _w)
    _n += _w
CONST_W = _n

G_NORM1, G_NORM2, G_OUT, G_ATTN, G_FFN, G_C = 0, 16, 32, 48, 64, 80
NG = 88

S_RAW = RAW * TILE
X_QKT = 0
X_SM, X_P, X_PT = 4352, 5376, 6400
X_SELW = 7424
X_HTF = 6144
X_ADA, X_ACT, X_ACT2 = 0, 6144, 7168
X_MACT, X_MACT2, X_G, X_GW, X_YE, X_HGF = 4096, 4352, 4608, 4864, 5376, 6400
X_GT = (5120, 7424)
SCRATCH = 8192
X_LAM, X_ANG, X_WR, X_POS, X_LAMS = 512, 1024, 1280, 1408, 1424
C_RT = TT * IN2


def constants():
    f = np.float32
    out = np.zeros((P, CONST_W), f)

    def put(name, a):
        o, w = _at[name]
        out[:, o:o + w] = np.asarray(a, f).reshape(-1, w) if np.ndim(a) > 1 else np.asarray(a, f)[None, :]

    def by_token(a):
        return a.reshape(TT, P, -1).transpose(1, 0, 2).reshape(P, -1)

    put("ident", np.eye(P))
    put("ones", np.ones((P, P)))
    put("before", np.triu(np.ones((P, P)), 1))
    put("iota", np.arange(P))
    q, k = np.arange(SEQ)[:, None], np.arange(SEQ)[None, :]
    off = np.abs(q - k)
    times = np.zeros((SEQ, SEQ))
    for window, dil in ((128, 1), (512, 4), (2048, 16)):
        times += (off % dil == 0) & (off // dil <= window // (2 * dil))
    bias = np.where(times > 0, np.log(np.maximum(times, 1)) * HD ** 0.5, MASKED)
    put("dilated", by_token(bias))
    put("causal", by_token(np.where(k <= q, 0.0, MASKED)))

    def rope(pos, half, theta):
        freqs = (f(theta) ** (-np.arange(half, dtype=f) / f(half))).astype(f)
        ang = pos.astype(f)[:, None] * freqs[None, :]
        c, s = np.cos(ang), np.sin(ang)
        return np.concatenate([c, c], 1), np.concatenate([-s, s], 1)

    pos = np.arange(SEQ)
    rc, rs = rope(pos // 64, 16, 10000.0)
    cc, cs = rope(pos % 64, 16, 10000.0)
    put("ax_cos", by_token(np.concatenate([rc, cc], 1)))
    put("ax_sin", by_token(np.concatenate([rs, cs], 1)))
    pc, ps = rope(pos, 8, 500000.0)
    put("pr_cos", by_token(pc))
    put("pr_sin", by_token(ps))
    put("inv64", 1.0 / (500000.0 ** (np.arange(0, 16, 2, dtype=f) / 16)))
    put("inv32", 1.0 / (500000.0 ** (np.arange(0, 8, 2, dtype=f) / 8)))
    put("earlier", (np.arange(NE)[None, :] < np.arange(NE)[:, None]).reshape(-1))
    return out


class Tiles:

    def __init__(self):
        self.t, self.i, self.start = 0, 0, 0
        self.loads = [0] * MORE_RAW
        self.raw, self.split, self.old = RAW, SPLIT, SPLIT

    def stage(self, raw=RAW, split=SPLIT):
        self.old = self.split
        self.i, self.raw, self.split, self.start = 0, raw, split, self.t

    def freed(self):
        return self.t - (self.old if self.i < 2 else self.split) + 1

    def next(self):
        s = self.i % self.raw
        self.loads[s] = self.loads[s] + 1
        got = (self.t, s, self.i % self.split, self.loads[s])
        self.t = self.t + 1
        self.i += 1
        return got

    def enter(self, it, n):
        per = [sum((self.i + k) % self.raw == s for k in range(n)) for s in range(MORE_RAW)]
        self.kept = (self.t, self.i, list(self.loads), n, per)
        self.t = self.t + it * n
        self.loads = [c + it * m if m else c for c, m in zip(self.loads, per)]

    def leave(self, steps):
        t, i, loads, n, per = self.kept
        self.t, self.i = t + steps * n, i + steps * n
        self.loads = [c + steps * m for c, m in zip(loads, per)]


def build(nc, A, out):
    ctx = ExitStack()
    with ctx:
        def sb(name, shape, dt=F32):
            return ctx.enter_context(nc.sbuf_tensor(name, shape, dt))

        def sem(name):
            return ctx.enter_context(nc.semaphore(name))

        x = sb("x", [P, TT, D])
        h = sb("h", [P, TT, D])
        hT_hi = sb("hT_hi", [P, KC, SEQ], F32R)
        hT_lo = sb("hT_lo", [P, KC, SEQ], F32R)
        big = sb("big", [P, ADA])
        slab = sb("slab", [P, S_RAW + SCRATCH])
        w_hi = sb("w_hi", [P, SPLIT, TILE], F32R)
        w_lo = sb("w_lo", [P, SPLIT, TILE], F32R)
        hid_hi = sb("hid_hi", [P, 4, SEQ], F32R)
        hid_lo = sb("hid_lo", [P, 4, SEQ], F32R)
        const = sb("const", [P, CONST_W])
        rowg = sb("rowg", [P, D])
        gcol = sb("gcol", [P, NG])
        modcol = sb("modcol", [P, DEPTH, 4 * KC])
        modg = sb("modg", [P, DEPTH, 2, KC])
        qkg = sb("qkg", [P, DEPTH, 2, HD])
        subg = sb("subg", [P, DEPTH, HD])
        nlam = sb("nlam", [P, DEPTH])
        posi = sb("posi", [P, TT], I32)
        rope64 = sb("rope64", [P, 2, TT, 16])
        rope32 = sb("rope32", [P, 2, TT, 8])
        wr_hi = sb("wr_hi", [P, KC, NE], F32R)
        wr_lo = sb("wr_lo", [P, KC, NE], F32R)
        stat = sb("stat", [P, 3, 20])
        att = sb("att", [P, 4, 20, TT])
        half = sb("half", [P, 1])
        flag = sb("flag", [1, 1], I32)

        def k_(name, *shape):
            o, w = _at[name]
            a = const[:, o:o + w]
            if len(shape) == 2:
                a = a.rearrange("p (a b) -> p a b", a=shape[0])
            return a

        ident, ones, before, iota = k_("ident"), k_("ones"), k_("before"), k_("iota")

        def scr(o, n, *shape):
            a = slab[:, S_RAW + o:S_RAW + o + n]
            if len(shape) == 2:
                a = a.rearrange("p (a b) -> p a b", a=shape[0])
            if len(shape) == 3:
                a = a.rearrange("p (a b c) -> p a b c", a=shape[0], b=shape[1])
            return a

        def raw(s):
            return slab[:, s * TILE:(s + 1) * TILE]

        csilu = sb("csilu", [P, KC])
        lam = scr(X_LAM, DEPTH * 4 * 32, DEPTH, 4 * 32)
        ang = scr(X_ANG, 4 * TT * 12, 4, TT * 12)
        posf = scr(X_POS, TT)
        lgT = slab[0:NE, S_RAW + X_YE:S_RAW + X_YE + SEQ]
        lams = scr(X_LAMS, 4 * DEPTH)
        wr = scr(X_WR, KC * NE, KC, NE)
        rt = big[:, C_RT:C_RT + 14 * TT * NE].rearrange("p (i t e) -> p i t e", i=14, t=TT)
        prj = big[:, 0:TT * IN2].rearrange("p (t n) -> p t n", t=TT)
        htf = scr(X_HTF, KC * SEQ, KC, SEQ)
        qkT = scr(X_QKT, 17 * SEQ, 17, SEQ)
        bank = [ctx.enter_context(nc.psum_tensor(f"bank{i}", [P, COL], F32)) for i in range(8)]
        gates = nc.dram_tensor("gates", (DEPTH, P, 2, D), F32, kind="Internal").ap()

        w_loaded = [sem(f"w_loaded{i}") for i in range(6)]
        hi_done, lo_done = sem("hi_done"), sem("lo_done")
        hi_quarter = sem("hi_quarter")
        w_used = sem("w_used")
        consts_loaded = sem("consts_loaded")
        gains_loaded = sem("gains_loaded")
        small_loaded = sem("small_loaded")
        x_loaded = sem("x_loaded")
        row_loaded = sem("row_loaded")
        row_used = sem("row_used")
        gains_turned = sem("gains_turned")
        gains_ready = sem("gains_ready")
        angles_ready = sem("angles_ready")
        rope_tables_ready = sem("rope_tables_ready")
        sines_ready = sem("sines_ready")
        lambda_summed = sem("lambda_summed")
        lambda_exps_ready = sem("lambda_exps_ready")
        half_ready = sem("half_ready")
        squares_summed = sem("squares_summed")
        means_ready = sem("means_ready")
        roots_ready = sem("roots_ready")
        rows_normed = sem("rows_normed")
        rows_turned = sem("rows_turned")
        rows_scaled = sem("rows_scaled")
        rows_hi_done = sem("rows_hi_done")
        rows_lo_done = sem("rows_lo_done")
        group_stored = sem("group_stored")
        x_updated = sem("x_updated")
        rope_dve_done = sem("rope_dve_done")
        rope_pool_done = sem("rope_pool_done")
        heads_turned = sem("heads_turned")
        heads_stored = sem("heads_stored")
        scores_ready = sem("scores_ready")
        max_ready = sem("max_ready")
        probs_ready = sem("probs_ready")
        probs_turned = sem("probs_turned")
        probs_stored = sem("probs_stored")
        weighted_ready = sem("weighted_ready")
        head_output_done = sem("head_output_done")
        index_ready = sem("index_ready")
        index_read = sem("index_read")
        dve_chain = sem("dve_chain")
        pool_chain = sem("pool_chain")
        activated = sem("activated")
        hidden_ready = sem("hidden_ready")
        hidden_turned = sem("hidden_turned")
        hidden_hi_done = sem("hidden_hi_done")
        hidden_lo_done = sem("hidden_lo_done")
        ada_in = [sem(f"ada_in{i}") for i in range(NPIECE)]
        ada_used = sem("ada_used")
        ada_summed = sem("ada_summed")
        ada_stored = sem("ada_stored")
        gates_stored = sem("gates_stored")
        logits_ready = sem("logits_ready")
        router_exps_ready = sem("router_exps_ready")
        selected = sem("selected")
        counts_ready = sem("counts_ready")
        list_ready = sem("list_ready")
        list_turned = sem("list_turned")
        list_stored = sem("list_stored")
        gathered = sem("gathered")
        gathered_scaled = sem("gathered_scaled")
        gathered_hi_done = sem("gathered_hi_done")
        gathered_lo_done = sem("gathered_lo_done")
        output_stored = sem("output_stored")
        scattered = sem("scattered")
        output_added = sem("output_added")
        places_moved = sem("places_moved")
        sums_cleared = sem("sums_cleared")
        logits_by_expert_ready = sem("logits_by_expert_ready")
        logits_by_expert_stored = sem("logits_by_expert_stored")
        fullest_counted = sem("fullest_counted")
        out_stored = sem("out_stored")

        LAYERS = range(2 * DEPTH)

        def width(l):
            return IN1 if l < DEPTH else IN2

        def groups(n):
            return [min(COL, n - c) for c in range(0, n, COL)]

        GROUPS0 = {}
        n = 0
        for l in LAYERS:
            for which in (0, 1):
                GROUPS0[l, which] = n
                n += len(groups(width(l))) if which == 0 else D // COL
        def pairs(l):
            if l < DEPTH:
                return ([("big", QA1 + P * i) for i in range(4)] + [("dup", 0), ("dup", P)]
                        + [("big", QB1 + P * i) for i in range(8)])
            return ([("big", QA2 + P * i) for i in range(3)] + [("dup", 0)] + [("big", QI2 + P * i) for i in range(2)]
                    + [("dup", P)] + [("big", QB2 + P * i) for i in range(4)] + [("big", QC2 + P * i) for i in range(6)])

        BANKS0 = {l: sum((len(pairs(m)) + 1) // 2 for m in LAYERS if m < l) for l in LAYERS}

        def jobs(l):
            full = HD ** -0.5
            if l < DEPTH:
                a = [(i // 2, 4 + i // 4, HD * (i % 2), HD, VA1 + HD * (i // 4), None, full, HD * i, 0) for i in range(HA)]
                b = [(6 + i // 2, 10 + i // 2, HD * (i % 2), HD, VB1 + HD * i, "dilated", full, HA * HD + HD * i, 0)
                     for i in range(HB)]
                return a + b
            c = [(11 + i // 2, 14 + i // 2, HD * (i % 2), HD, VC2 + HD * i, "causal", full, (A2 + B2 + i) * HD, 0)
                 for i in range(C2)]
            b = [(7 + i // 4, 9 + i // 4, 32 * (i % 4), 32, VB2 + HD * (i // 2), "causal", 32 ** -0.5,
                  A2 * HD + HD * (i // 2), 1 + i % 2) for i in range(2 * B2)]
            a = [(i // 2, 3, HD * (i % 2), HD, VA2, "chosen", full, HD * i, 0) for i in range(A2)]
            return b + c + a

        GATE_BANKS = [(4, 5, 6, 7)] * (DEPTH - 1) + [(1, 2, 3, 1)]
        SC_BANKS = (0, 1, 6)
        IX_BANKS = (6, 2, 4, 5)
        LAST_BANKS = (3, 7)

        JOBS0 = {l: sum(len(jobs(m)) for m in LAYERS if m < l) for l in LAYERS}

        def steps(l):
            return FF1 // F_UP if l < DEPTH else FF2 // F_GATED

        STEPS0 = {l: sum(steps(m) for m in LAYERS if m < l) for l in LAYERS}
        MOE = 2 * DEPTH - 1
        MJ = FF2 // F_GATED
        MT = 3 * MJ

        def w_in_of(l):
            return (A["w_in"] if l < DEPTH else A["w_in_2"])[l % DEPTH].rearrange("(k p) n -> p k n", p=P)

        def w_out_of(l):
            return (A["w_out"] if l < DEPTH else A["w_out_2"])[l % DEPTH].rearrange("(k p) n -> p k n", p=P)



        NORMED = TT * (3 * len(LAYERS) + (len(LAYERS) >= DEPTH))

        def tiles_before_w_out(l):
            def ff(i):
                return steps(i) * (4 if i < DEPTH else 3)
            return sum(2 * len(groups(width(i))) + 4 + ff(i) for i in LAYERS if i < l) + 2 * len(groups(width(l)))

        def proj_evac(l, columns=None):
            before_ = sum(len(groups(width(i))) for i in LAYERS if i < l)
            return FREE_BANKS + TT * (before_ + -(-(columns or width(l)) // COL))

        def expert_ring(ring, i, p, t0, loads0, ahead=2):
            done = MT * p + ahead
            ring.t, ring.i, ring.raw, ring.split = t0 + i * (2 * MT) + done, done, MORE_RAW, 3
            ring.loads = [c + i * (2 * MT // MORE_RAW) + sum(k % MORE_RAW == s for k in range(done))
                          for s, c in enumerate(loads0)]

        def each_expert(eng, n0, body):
            body(0, 0, n0, True, False)
            with eng.Fori(0, NE // 2 - 1) as i:
                body(i, 1, 2 * i + (n0 + 1), False, False)
                body(i + 1, 0, 2 * i + (n0 + 2), False, False)
            body(NE // 2 - 1, 1, n0 + NE - 1, False, True)

        def expert_steps(eng, ring, step):
            with eng.Fori(0, (MJ - 3) // 2) as jj:
                ring.enter(jj, 6)
                step(2 * jj + 2)
                step(2 * jj + 3)
            ring.leave((MJ - 3) // 2)
            step(MJ - 1)

        def expert_after(t0, loads0):
            return t0 + NE * MT, [c + NE * MT // MORE_RAW for c in loads0]

        def silu_col(k):
            return csilu[:, k:k + 1] if isinstance(k, int) else csilu[:, bass.ds(k, 1)]

        def gate_mul(dve, at, ntt, src, dst, banks):
            for t in range(ntt):
                dve.wait_ge(activated, at + t + 1)
                dve.tensor_tensor(scr(dst + t * F_GATED, F_GATED), scr(src + t * F_GATED, F_GATED),
                                  banks[t][:, F_GATED:2 * F_GATED], ALU.mult).then_inc(hidden_ready, 1)

        def rope_steps(eng, link, v, heads, half_, cos, sin, tmp):
            n = 2 * half_
            a, b = scr(tmp, heads * n, heads, n), scr(tmp + 320, heads * n, heads, n)
            link(eng.tensor_tensor(a, v[:, :, 0:n], cos.unsqueeze(1).broadcast_to([P, heads, n]), ALU.mult))
            for o, i in ((0, half_), (half_, 0)):
                s = sin[:, o:o + half_].unsqueeze(1).broadcast_to([P, heads, half_])
                link(eng.tensor_tensor(b[:, :, o:o + half_], v[:, :, i:i + half_], s, ALU.mult))
            link(eng.tensor_tensor(v[:, :, 0:n], a, b, ALU.add))

        block = ctx.enter_context(nc.Block())

        def group_loop(eng, ring, widths, body):
            full = widths.count(COL) // 2
            done = 0
            if full > 1:
                with eng.Fori(0, full) as it:
                    ring.enter(it, 4)
                    body(2 * it, COL, 0)
                    body(2 * it + 1, COL, 1)
                ring.leave(full)
                done = 2 * full
            for c in range(done, len(widths)):
                body(c, widths[c], c % 2)

        @block.sync
        def _(sp):
            ring = Tiles()

            def stage(raw_slots=RAW):
                ring.stage(raw_slots)
                if ring.t:
                    sp.wait_ge(lo_done, FREE_RAW + ring.t)

            def tile(parts):
                t, s, _, _ = ring.next()
                sp.wait_ge(lo_done, FREE_RAW + t - ring.raw + 1)
                for dst, src in parts(raw(s)):
                    sp.dma_start(dst, src).then_inc(w_loaded[s], 16)

            def cols(w, c, n):
                for a in range(2):
                    def parts(r, a=a):
                        d = r[:, 0:4 * n].rearrange("p (k n) -> p k n", k=4)
                        for b in range(2):
                            k = 4 * a + 2 * b
                            yield d[:, 2 * b:2 * b + 2, :], w[:, k:k + 2, bass.ds(c, n)]
                    tile(parts)

            def gated(wg, wu, c):
                for a in range(2):
                    def parts(r, a=a):
                        d = r.rearrange("p (k b n) -> p k b n", k=4, b=2)
                        for b, w in enumerate((wg, wu)):
                            yield d[:, :, b, :], w[:, 4 * a:4 * a + 4, bass.ds(c, F_GATED)]
                    tile(parts)

            def rows(w, r0, n):
                for b in range(n):
                    def parts(r, b=b):
                        d = r.rearrange("p (i n) -> p i n", i=2)
                        for i in (1, 0):
                            yield d[:, i:i + 1, :], w[:, bass.ds(r0 + 2 * b + i, 1), :]
                    tile(parts)

            def project(w, widths):
                stage()
                group_loop(sp, ring, widths, lambda c, n, g: cols(w, c * COL, n))

            def ada_piece(l, k, n):
                to = scr(X_ADA + n * PIECE, PIECE)
                at = NPIECE * (9 * l + k) + n
                if not isinstance(at, int) or at >= NPIECE:
                    sp.wait_ge(ada_used, at - NPIECE + 1)
                if isinstance(k, int) and k == KC:
                    sp.dma_start(to[0:1, :], A["b_ada_2"][l:l + 1, n * PIECE:(n + 1) * PIECE]).then_inc(ada_in[n], 16)
                else:
                    src = A["w_ada_2"][l].rearrange("(k p) n -> p k n", p=P)
                    sp.dma_start(to.unsqueeze(1), src[:, bass.ds(k, 1), n * PIECE:(n + 1) * PIECE]).then_inc(ada_in[n], 16)

            def row(src, n):
                if n:
                    sp.wait_ge(row_used, n)
                sp.dma_start(rowg[:, :], src).then_inc(row_loaded, 16)

            sp.dma_start(x[:, :, :], A["x"][0].rearrange("(t p) d -> p t d", p=P)).then_inc(x_loaded, 16)
            sp.dma_start(const[:, :], A["consts"]).then_inc(consts_loaded, 16)
            g = slab[:, S_RAW:S_RAW + P]
            for at, src in ((G_NORM1, A["norm1"]), (G_NORM2, A["norm2"]), (G_ATTN, A["g_attn_2"]),
                            (G_FFN, A["g_ffn_2"])):
                sp.dma_start(g[at:at + 16, :], src.rearrange("l (k n) -> (l k) n", n=P)).then_inc(gains_loaded, 16)
            for l in range(DEPTH):
                for i, src in enumerate((A["out_norm_a"], A["out_norm_b"])):
                    at = G_OUT + KC * l + 4 * i
                    sp.dma_start(g[at:at + 4, :], src[l].rearrange("(k n) -> k n", n=P)).then_inc(gains_loaded, 16)
            sp.dma_start(g[G_C:G_C + KC, :], A["c_2"][0].rearrange("(k n) -> k n", n=P)).then_inc(gains_loaded, 16)
            nrow = 0
            for l in LAYERS:
                m = l % DEPTH
                project(w_in_of(l), groups(width(l)))
                if l >= DEPTH:
                    if l == DEPTH:
                        sp.wait_ge(gates_stored, 16 * DEPTH)
                    row(gates[m, :, 0, :], nrow)
                    nrow += 1
                project(w_out_of(l), groups(D))
                if l < DEPTH:
                    w1 = A["w_mlp_in"][l].rearrange("(k p) n -> p k n", p=P)
                    w2 = A["w_mlp_out"][l].rearrange("(r p) n -> p r n", p=P)
                    J = steps(l)
                    stage()
                    cols(w1, 0, F_UP)
                    sp.wait_ge(rows_lo_done, 2 * (3 * l + 1) + 2)
                    for n in range(NPIECE):
                        ada_piece(l, 0, n)
                    with sp.Fori(0, J - 1) as j:
                        ring.enter(j, 4)
                        cols(w1, j * F_UP + F_UP, F_UP)
                        ada_piece(l, j + 1, 0)
                        rows(w2, j * 4, 1)
                        ada_piece(l, j + 1, 1)
                        rows(w2, j * 4 + 2, 1)
                        ada_piece(l, j + 1, 2)
                    ring.leave(J - 1)
                    rows(w2, 4 * (J - 1), 2)
                    for n in range(NPIECE):
                        ada_piece(l, KC, n)
                    if l == DEPTH - 1:
                        row(A["final_norm"].rearrange("(a n) -> a n", a=1).broadcast_to([P, D]), nrow)
                        nrow += 1
                elif l < MOE:
                    wg = A["w_ff_gate_2"][0].rearrange("(k p) n -> p k n", p=P)
                    wu = A["w_ff_up_2"][0].rearrange("(k p) n -> p k n", p=P)
                    wd = A["w_ff_down_2"][0].rearrange("(r p) n -> p r n", p=P)
                    J = steps(l)
                    stage(3)
                    gated(wg, wu, 0)
                    with sp.Fori(0, J - 1) as j:
                        ring.enter(j, 3)
                        gated(wg, wu, j * F_GATED + F_GATED)
                        rows(wd, j * 2, 1)
                    ring.leave(J - 1)
                    rows(wd, 2 * (J - 1), 1)
                    row(gates[m, :, 1, :], nrow)
                    nrow += 1
                else:
                    stage(MORE_RAW)

                    def expert_loads(t0, loads0, n0):
                        def weights(e):
                            return [A[n][0, bass.ds(e, 1)].rearrange("a (k p) n -> p (a k) n", p=P)
                                    for n in ("w_exp_gate_2", "w_exp_up_2", "w_exp_down_2")]

                        def body(i, p, n, first, last):
                            wg, wu, wd = weights(2 * i + p)
                            expert_ring(ring, i, p, t0, loads0)

                            def step(j, norm=False):
                                gated(wg, wu, j * F_GATED + F_GATED)
                                if norm:
                                    sp.wait_ge(scores_ready, JOBS0[l] + len(jobs(l)))
                                rows(wd, j * 2, 1)

                            def final(j):
                                if not last:
                                    gated(*weights(2 * i + p + 1)[:2], 0)
                                rows(wd, j * 2, 1)

                            step(0, first and n0 == 0)
                            step(1)
                            if first and n0 == 0:
                                row(gates[m, :, 1, :], nrow)
                            expert_steps(sp, ring, lambda j: final(j) if isinstance(j, int) else step(j))

                        ring.t, ring.i, ring.loads = t0, 0, list(loads0)
                        gated(*weights(0)[:2], 0)
                        each_expert(sp, n0, body)

                    t0, loads0 = ring.t, list(ring.loads)
                    expert_loads(t0, loads0, 0)
                    nrow += 1
                    sp.wait_ge(fullest_counted, 1)
                    full = sp.value_load(flag[0:1, 0:1], min_val=0, max_val=SEQ)
                    with sp.If(full > P):
                        expert_loads(*expert_after(t0, loads0), NE)
            row(A["g_final_2"].rearrange("(a n) -> a n", a=1).broadcast_to([P, D]), nrow)
            for t in range(TT):
                sp.wait_ge(rows_normed, NORMED + t + 1)
                sp.dma_start(out[0, t * P:(t + 1) * P, :], h[:, t, :]).then_inc(out_stored, 16)
            sp.wait_ge(out_stored, 16 * TT)

        @block.gpsimd
        def _(pool):
            n_chain = [0]

            def link(ins):
                n_chain[0] += 1
                ins.then_inc(pool_chain, 1)
                pool.wait_ge(pool_chain, n_chain[0])

            roots = [0]

            def root(n):
                roots[0] += 1
                pool.wait_ge(means_ready, roots[0])
                pool.tensor_tensor(stat[:, 2, 0:n], stat[:, 1, 0:n], half[:, 0:1].broadcast_to([P, n]), ALU.pow).then_inc(roots_ready, 1)

            def norm_roots():
                for t in range(TT):
                    roots[0] += 1
                    pool.wait_ge(means_ready, roots[0])
                    pool.tensor_tensor(stat[:, 2, t:t + 1], stat[:, 1, t:t + 1], half[:, 0:1], ALU.pow).then_inc(roots_ready, 1)

            def rope(src, heads, d, half_, cos, sin):
                for t in range(TT):
                    v = prj[:, t, src:src + heads * d].rearrange("p (h d) -> p h d", h=heads)
                    rope_steps(pool, link, v, heads, half_, cos[:, t, :], sin[:, t, :], X_PT)

            for l in range(DEPTH):
                pool.dma_start(qkg[:, l, 0, :], A["q_norm"][l:l + 1, :].broadcast_to([P, HD])).then_inc(small_loaded, 16)
                pool.dma_start(qkg[:, l, 1, :], A["k_norm"][l:l + 1, :].broadcast_to([P, HD])).then_inc(small_loaded, 16)
                pool.dma_start(subg[:, l, :], A["diff_subln_2"][l:l + 1, :].broadcast_to([P, HD])).then_inc(small_loaded, 16)
                pool.dma_start(lam[:, l, :], A["diff_lambda_2"][l:l + 1].rearrange("a b c -> a (b c)").broadcast_to([P, 4 * 32])
                             ).then_inc(small_loaded, 16)
            with nc.allow_non_contiguous_dma(reason="256 positions"):
                pool.dma_start(posi[:, :].unsqueeze(2), A["positions_2"].rearrange("a (t p) -> p t a", p=P)).then_inc(small_loaded, 16)
            pool.dma_start(wr[:, :, :], A["w_router_2"][0].rearrange("(k p) e -> p k e", p=P)).then_inc(small_loaded, 16)

            def lo(t, n):
                pool.wait_ge(lo_done, FREE_RAW + t)
                for i in range(n):
                    pool.wait_ge(hi_done, t + i + 1)
                    pool.tensor_tensor(w_lo[:, i, :], raw(i), w_hi[:, i, :].bitcast(F32), ALU.subtract).then_inc(lo_done, 1)

            pool.wait_ge(half_ready, 1)
            for l in LAYERS:
                if l == 0:
                    norm_roots()
                if l != DEPTH:
                    lo(tiles_before_w_out(l) - 2 * len(groups(width(l))), 2)
                if l:
                    norm_roots()
                def rope_when(n, src, heads, d, half_, cos, sin):
                    pool.wait_ge(group_stored, proj_evac(l, src + heads * d))
                    rope(src, heads, d, half_, cos, sin)
                    if n:
                        pool.nop().then_inc(rope_pool_done, 1)

                if l < DEPTH:
                    root((HA + KVA) * TT)
                    cos, sin = k_("pr_cos", TT, 16), k_("pr_sin", TT, 16)
                    rope_when(1, QB1, HB, HD, 8, cos, sin)
                    rope_when(1, KB1, HB, HD, 8, cos, sin)
                else:
                    if l == DEPTH:
                        pool.wait_ge(rope_tables_ready, 1)
                    rope_when(1, QB2, 4 * B2, 32, 4, rope32[:, 0], rope32[:, 1])
                    rope_when(0, QC2, C2, HD, 8, rope64[:, 0], rope64[:, 1])
                    rope_when(1, KC2, C2, HD, 8, rope64[:, 0], rope64[:, 1])
                if l >= DEPTH:
                    root(TT * B2)
                lo(tiles_before_w_out(l), 4)
                if l < DEPTH:
                    root(2 * TT)
                if l == MOE:
                    pool.wait_ge(weighted_ready, JOBS0[l] + len(jobs(l)))
                    pool.memset(big[:, 0:TT * D], 0.0).then_inc(sums_cleared, 1)
                lo(tiles_before_w_out(l) + 4, 2)
                norm_roots()
                if l < DEPTH:
                    ub = 2 * STEPS0[l]

                    def square(j):
                        for t in range(TT):
                            pool.wait_ge(activated, ub + j * TT + t + 1)
                            a = scr(X_ACT + t * F_UP, F_UP)
                            pool.tensor_tensor(scr(X_ACT2 + t * F_UP, F_UP), a, a, ALU.mult).then_inc(hidden_ready, 1)

                    with pool.Fori(0, steps(l)) as j:
                        square(j)
                if l == DEPTH - 1:
                    lo(tiles_before_w_out(l) + 4 + 4 * steps(l), 2)
                    norm_roots()
            norm_roots()

        @block.vector
        def _(dve):
            ring = Tiles()
            n_chain = [0]

            def mark(ins):
                n_chain[0] += 1
                ins.then_inc(dve_chain, 1)
                return n_chain[0]

            def link(ins):
                dve.wait_ge(dve_chain, mark(ins))

            def lo():
                t, s, q, _ = ring.next()
                dve.wait_ge(hi_done, t + 1)
                dve.tensor_tensor(w_lo[:, q, :], raw(s), w_hi[:, q, :].bitcast(F32), ALU.subtract).then_inc(lo_done, 1)

            def pool_tiles(n):
                for _ in range(n):
                    ring.next()

            def pool_is_through():
                dve.wait_ge(lo_done, FREE_RAW + ring.t)

            def norm(to=None):
                xns[0] += TT
                sums[0] += TT
                for t in range(TT):
                    dve.wait_ge(squares_summed, sums[0] - TT + t + 1)
                    dve.tensor_scalar(stat[:, 1, t:t + 1], stat[:, 0, t:t + 1], 1.0 / D, EPS, ALU.mult, ALU.add
                                      ).then_inc(means_ready, 1)
                if updates[0]:
                    dve.wait_ge(x_updated, updates[0])
                for t in range(TT):
                    roots[0] += 1
                    dve.wait_ge(roots_ready, roots[0])
                    if to is None:
                        dve.tensor_scalar(h[:, t, :], x[:, t, :], stat[:, 2, t:t + 1], None, ALU.mult).then_inc(rows_normed, 1)
                    else:
                        dve.scalar_tensor_tensor(to[:, t, :], x[:, t, :], stat[:, 2, t:t + 1], rowg[:, :], ALU.mult, ALU.mult
                                                 ).then_inc(rows_normed, 1)

            sums, roots, turned, xns, updates = [0], [0], [0], [0], [0]

            def turn(gain, shift):
                m = turned[0]
                turned[0] += 1
                for k in range(KC):
                    src = bank[k // 2][:, (k % 2) * SEQ:(k % 2 + 1) * SEQ]
                    dve.wait_ge(rows_turned, KC * m + k - k % 2 + 2)
                    if gain is None:
                        dve.tensor_copy(htf[:, k, :], src).then_inc(rows_scaled, 1)
                    elif shift is None:
                        dve.tensor_scalar(htf[:, k, :], src, gain(k), None, ALU.mult).then_inc(rows_scaled, 1)
                    else:
                        dve.tensor_scalar(htf[:, k, :], src, gain(k), shift(k), ALU.mult, ALU.add).then_inc(rows_scaled, 1)
                for b in range(2):
                    ks = slice(4 * b, 4 * b + 4)
                    dve.wait_ge(rows_hi_done, 2 * m + b + 1)
                    dve.tensor_tensor(hT_lo[:, ks, :], htf[:, ks, :], hT_hi[:, ks, :].bitcast(F32), ALU.subtract
                                      ).then_inc(rows_lo_done, 1)

            def gain_of(at):
                return lambda k: gcol[:, at + k:at + k + 1]

            def gated_gain(l, which):
                return lambda k: modg[:, l, which, k:k + 1]

            def shift_of(l, v):
                return lambda k: modcol[:, l, KC * v + k:KC * v + k + 1]

            def x_update(c, gated_, src, wait):
                wait()
                for t in range(TT):
                    at = x[:, t, c * COL:(c + 1) * COL]
                    if gated_:
                        tmp = scr(X_SM + t * COL, COL)
                        link(dve.tensor_tensor(tmp, src(t), rowg[:, c * COL:(c + 1) * COL], ALU.mult))
                        ins = dve.tensor_tensor(at, tmp, at, ALU.add)
                    else:
                        ins = dve.tensor_tensor(at, src(t), at, ALU.add)
                    if c == D // COL - 1:
                        updated(ins)

            def updated(ins):
                updates[0] += 1
                ins.then_inc(x_updated, 1)

            mark(dve.memset(half[:, :], -0.5))
            dve.memset(stat[:, :, :], 0.0).then_inc(lo_done, FREE_RAW)
            dve.memset(ang[:, :, :], 0.0).then_inc(w_used, FREE_SPLIT)
            dve.wait_ge(lo_done, FREE_RAW)
            dve.wait_ge(w_used, FREE_SPLIT)
            dve.wait_ge(dve_chain, 1)
            dve.nop().then_inc(half_ready, 1)
            dve.nop().then_inc(group_stored, FREE_BANKS)
            dve.wait_ge(gains_turned, 1)
            dve.tensor_copy(gcol[:, :], bank[7][:, 0:NG]).then_inc(gains_ready, 1)

            def tables():
                dve.wait_ge(small_loaded, 16 * V_LOADS)
                link(dve.tensor_copy(posf[:, :], posi[:, :]))
                dve.wait_ge(consts_loaded, 16)
                inv = const[:, _at["inv64"][0]:_at["inv64"][0] + 12]
                for t in range(TT):
                    mark(dve.tensor_scalar(ang[:, 0, 12 * t:12 * t + 12], inv, posf[:, t:t + 1], None, ALU.mult))
                dve.wait_ge(dve_chain, n_chain[0])
                big_f = 12582912.0
                link(dve.tensor_scalar(ang[:, 1], ang[:, 0], float(1 / (2 * np.pi)), None, ALU.mult))
                link(dve.tensor_scalar(ang[:, 1], ang[:, 1], big_f, None, ALU.add))
                link(dve.tensor_scalar(ang[:, 1], ang[:, 1], big_f, None, ALU.subtract))
                p1 = 6.28125
                p2 = float(np.float32(round((2 * np.pi - p1) * 2 ** 21) / 2 ** 21))
                p3 = float(2 * np.pi - p1 - p2)
                for part in (p1, p2, p3):
                    link(dve.scalar_tensor_tensor(ang[:, 0], ang[:, 1], -part, ang[:, 0], ALU.mult, ALU.add))
                pi = float(np.float32(3.1415925))
                link(dve.tensor_scalar(ang[:, 0], ang[:, 0], pi, -pi, ALU.min, ALU.max))
                dve.tensor_scalar(ang[:, 1], ang[:, 0], 0.5, None, ALU.mult).then_inc(angles_ready, 1)
                dve.wait_ge(sines_ready, 2)
                link(dve.tensor_tensor(ang[:, 3], ang[:, 3], ang[:, 3], ALU.mult))
                link(dve.tensor_scalar(ang[:, 3], ang[:, 3], -2.0, 1.0, ALU.mult, ALU.add))
                for tab, o, n in ((rope64, 0, 8), (rope32, 8, 4)):
                    for t in range(TT):
                        a = 12 * t + o
                        mark(dve.tensor_copy(tab[:, 0, t, 0:n], ang[:, 3, a:a + n]))
                        mark(dve.tensor_copy(tab[:, 0, t, n:2 * n], ang[:, 3, a:a + n]))
                        mark(dve.tensor_scalar(tab[:, 1, t, 0:n], ang[:, 2, a:a + n], -1.0, None, ALU.mult))
                        mark(dve.tensor_copy(tab[:, 1, t, n:2 * n], ang[:, 2, a:a + n]))
                dve.wait_ge(dve_chain, n_chain[0])
                dve.nop().then_inc(rope_tables_ready, 1)
                for l in range(DEPTH):
                    v = lam[:, l, :].rearrange("p (a b n) -> p a b n", a=2, b=2)
                    link(dve.tensor_tensor(v[:, :, 0, :], v[:, :, 0, :], v[:, :, 1, :], ALU.mult))
                    r = dve.tensor_reduce(lams[:, 2 * l:2 * l + 2], v[:, :, 0, :], AX.X, ALU.add)
                    r.then_inc(lambda_summed, 1)
                dve.wait_ge(lambda_exps_ready, 1)
                for l in range(DEPTH):
                    start = 0.8 - 0.6 * float(np.exp(-0.3 * l))
                    link(dve.tensor_tensor(nlam[:, l:l + 1], lams[:, 5 + 2 * l:6 + 2 * l], lams[:, 4 + 2 * l:5 + 2 * l], ALU.subtract))
                    link(dve.tensor_scalar(nlam[:, l:l + 1], nlam[:, l:l + 1], start, None, ALU.subtract))
                    link(dve.tensor_scalar(subg[:, l, :], subg[:, l, :], 1.0 - start, None, ALU.mult))
                link(dve.tensor_copy(wr_hi[:, :, :], wr[:, :, :]))
                link(dve.tensor_tensor(wr_lo[:, :, :], wr[:, :, :], wr_hi[:, :, :].bitcast(F32), ALU.subtract))

            dve.wait_ge(x_loaded, 16)

            jobs_done = [0]
            idx_done = [0]
            rows_used = [0]
            ub = 0
            for l in LAYERS:
                m = l % DEPTH
                widths = groups(width(l))
                if l == DEPTH:
                    norm()
                    dve.wait_ge(ada_stored, 5 * DEPTH)
                    for d in range(DEPTH):
                        for which, v, at in ((0, 1, G_ATTN), (1, 3, G_FFN)):
                            mark(dve.scalar_tensor_tensor(modg[:, d, which, :], modcol[:, d, KC * v:KC * v + KC], 1.0,
                                                          gcol[:, at + KC * d:at + KC * d + KC], ALU.add, ALU.mult))
                    dve.wait_ge(dve_chain, n_chain[0])
                else:
                    norm()
                if l == 0:
                    pool_tiles(2)
                if l < DEPTH:
                    turn(gain_of(G_NORM1 + KC * m), None)
                else:
                    turn(gated_gain(m, 0), shift_of(m, 0))
                if l == 0:
                    tables()
                pool_is_through()
                t1, t2 = X_SM, X_SM + 640
                nh = HA + KVA
                vh = prj[:, :, 0:nh * HD].rearrange("p t (h d) -> p t h d", h=nh)

                def head_norms():
                    dve.wait_ge(group_stored, proj_evac(l, VA1))
                    v = prj[:, :, 0:nh * HD]
                    link(dve.tensor_tensor(scr(X_SM, TT * nh * HD, TT, nh * HD), v, v, ALU.mult))
                    link(dve.tensor_reduce(stat[:, 0, 0:TT * nh], scr(X_SM, TT * nh * HD, TT * nh, HD), AX.X, ALU.add))
                    dve.tensor_scalar(stat[:, 1, 0:TT * nh], stat[:, 0, 0:TT * nh], 1.0 / HD, EPS, ALU.mult, ALU.add
                                      ).then_inc(means_ready, 1)
                    roots[0] += 1

                def head_rope():
                    dve.wait_ge(roots_ready, roots[0])
                    r = stat[:, 2, 0:TT * nh].rearrange("p (t h) -> p t h", t=TT).unsqueeze(3).broadcast_to([P, TT, nh, HD])
                    link(dve.tensor_tensor(vh, vh, r, ALU.mult))
                    for i, (a, b) in enumerate(((0, HA), (HA, nh))):
                        for t in range(TT):
                            g = qkg[:, m, i, :].unsqueeze(1).broadcast_to([P, b - a, HD])
                            mark(dve.tensor_tensor(vh[:, t, a:b, :], vh[:, t, a:b, :], g, ALU.mult))
                    dve.wait_ge(dve_chain, n_chain[0])
                    for t in range(TT):
                        cos, sin = k_("ax_cos", TT, HD)[:, t, :], k_("ax_sin", TT, HD)[:, t, :]
                        a1 = scr(t1, nh * HD, nh, HD)
                        a2 = scr(t2, nh * HD, nh, 2, HD // 2)
                        v4 = vh[:, t].rearrange("p h (b d) -> p h b d", b=2)
                        s4 = sin.rearrange("p (b d) -> p b d", b=2)
                        mark(dve.tensor_tensor(a1, vh[:, t], cos.unsqueeze(1).broadcast_to([P, nh, HD]), ALU.mult))
                        for o, i in ((0, 16), (16, 0)):
                            s = s4[:, :, o:o + 16].unsqueeze(1).broadcast_to([P, nh, 2, 16])
                            mark(dve.tensor_tensor(a2[:, :, :, o:o + 16], v4[:, :, :, i:i + 16], s, ALU.mult))
                        dve.wait_ge(dve_chain, n_chain[0])
                        b2 = scr(t2, nh * HD, nh, HD)
                        mark(dve.tensor_tensor(vh[:, t, 0:HA], a1[:, 0:HA], b2[:, 0:HA], ALU.add))
                        for i in range(KVA):
                            for d in range(2):
                                o = P * i + HD * d
                                mark(dve.tensor_tensor(h[:, t, o:o + HD], a1[:, HA + i], b2[:, HA + i], ALU.add))
                        dve.wait_ge(dve_chain, n_chain[0])
                    dve.nop().then_inc(rope_dve_done, 1)

                def chosen_rope(src, heads):
                    for t in range(TT):
                        v = prj[:, t, src:src + heads * HD].rearrange("p (h d) -> p h d", h=heads)
                        rope_steps(dve, link, v, heads, 8, rope64[:, 0, t, :], rope64[:, 1, t, :], X_SM)

                def dsa_rope():
                    dve.wait_ge(group_stored, proj_evac(l, QB2))
                    chosen_rope(QA2, A2 + 1)

                def index_rope():
                    chosen_rope(QI2, I2 + 1)
                    for t in range(TT):
                        for i, src in enumerate((KA2, KI2)):
                            for d in range(2):
                                o = P * i + HD * d
                                mark(dve.tensor_copy(h[:, t, o:o + HD], prj[:, t, src:src + HD]))
                    wi = prj[:, :, WI2:WI2 + I2]
                    mark(dve.tensor_scalar(wi, wi, I2 ** -0.5, None, ALU.mult))
                    dve.wait_ge(dve_chain, n_chain[0])
                    dve.nop().then_inc(rope_dve_done, 1)

                between = {2: (head_norms, head_rope)} if l < DEPTH else {2: (dsa_rope,), 3: (index_rope,)}
                for c in range(len(widths)):
                    if c < len(widths) - 1:
                        lo()
                        lo()
                    for part in between.get(c, ()):
                        part()

                picks = []
                if l >= DEPTH:
                    selw = selm = scr(X_SELW, TT * SEQ, TT, SEQ)
                    for i in range(I2):
                        n = idx_done[0] = idx_done[0] + 1
                        r = scr(X_SM, TT * SEQ, TT, SEQ)
                        dve.wait_ge(index_ready, n)
                        last = dve.tensor_scalar(r, bank[IX_BANKS[i]][:, :].rearrange("p (t n) -> p t n", t=TT),
                                                 HD ** -0.5, 0.0, ALU.mult, ALU.max)
                        last.then_inc(index_read, 1)
                        dve.wait_ge(index_read, n)
                        for t in range(TT):
                            w = prj[:, t, WI2 + i:WI2 + i + 1]
                            if i == 0:
                                mark(dve.tensor_scalar(selw[:, t], r[:, t], w, None, ALU.mult))
                            else:
                                mark(dve.scalar_tensor_tensor(selw[:, t], r[:, t], w, selw[:, t], ALU.mult, ALU.add))
                        dve.wait_ge(dve_chain, n_chain[0])
                    link(dve.tensor_tensor(selw, selw, k_("causal", TT, SEQ), ALU.add))

                    def pick(t):
                        m8 = rt[:, 12 + t, :, :].rearrange("p a b -> p (a b)")[:, 0:8]
                        last = [None, None]

                        def find():
                            if waits[t]:
                                dve.wait_ge(dve_chain, waits[t])
                            waits[t] = mark(dve.max(m8, selw[:, t]))

                        def strike():
                            dve.wait_ge(dve_chain, waits[t])
                            waits[t] = mark(dve.match_replace(selw[:, t], m8, selw[:, t], TAKEN))
                        return find, strike

                    waits = [0, 0]
                    fs = [pick(t) for t in range(TT)]
                    for _ in range(TOPK // 8):
                        for phase in range(2):
                            picks += [fs[t][phase] for t in range(TT)]

                def finish_picks():
                    dve.wait_ge(dve_chain, n_chain[0])
                    link(dve.tensor_scalar(selm, selw, TAKEN / 2, MASKED, ALU.is_gt, ALU.mult))
                    link(dve.tensor_tensor(selm, selm, k_("causal", TT, SEQ), ALU.add))

                js = jobs(l)
                j0 = jobs_done[0]

                yd = h[:, :, A2 * HD:(A2 + B2) * HD]
                squared = scr(4 * SEQ, TT * B2 * HD)

                yh = yd.rearrange("p t (h d) -> p t h d", h=B2)

                def diff_squares():
                    link(dve.tensor_tensor(squared.rearrange("p (t n) -> p t n", t=TT), yd, yd, ALU.mult))

                def diff_sums():
                    link(dve.tensor_reduce(stat[:, 0, 0:TT * B2], squared.rearrange("p (a n) -> p a n", n=HD), AX.X, ALU.add))
                    dve.tensor_scalar(stat[:, 1, 0:TT * B2], stat[:, 0, 0:TT * B2], 1.0 / HD, SUB_EPS, ALU.mult, ALU.add
                                      ).then_inc(means_ready, 1)
                    roots[0] += 1

                def diff_scale():
                    dve.wait_ge(roots_ready, roots[0])
                    r = stat[:, 2, 0:TT * B2].rearrange("p (t h) -> p t h", t=TT).unsqueeze(3).broadcast_to([P, TT, B2, HD])
                    link(dve.tensor_tensor(yh, yh, r, ALU.mult))

                def diff_gain(t):
                    g = subg[:, m, :].unsqueeze(1).broadcast_to([P, B2, HD])
                    link(dve.tensor_tensor(yh[:, t], yh[:, t], g, ALU.mult))

                first_diff = 2 * B2 + 8
                diff_steps = (diff_squares, diff_sums, diff_scale, lambda: diff_gain(0), lambda: diff_gain(1)) if l >= DEPTH else ()
                ring.stage()
                pool_tiles(4)
                for n in range(len(js) + 3):
                    if n < len(js):
                        _, _, _, _, _, mask, scale, _, _ = js[n]
                        b = (j0 + n) % 2
                        if mask == "chosen" and js[n - 1][5] != "chosen":
                            finish_picks()
                        sm = scr(X_SM + b * COL, COL, TT, SEQ)
                        dve.wait_ge(scores_ready, j0 + n + 1)
                        if n >= 2:
                            dve.wait_ge(probs_ready, TT * (j0 + n - 1))
                        else:
                            dve.wait_ge(dve_chain, n_chain[0])
                        mx = att[:, 0, n, :]
                        ps = bank[SC_BANKS[n % 3]][:, :].rearrange("p (t n) -> p t n", t=TT)
                        for t in range(TT):
                            if mask is None:
                                mark(dve.tensor_scalar(sm[:, t], ps[:, t], scale, TAKEN, ALU.mult, ALU.max, accum_out=mx[:, t:t + 1]))
                            else:
                                mk = selm if mask == "chosen" else k_(mask, TT, SEQ)
                                mark(dve.tensor_tensor_reduce(sm[:, t], ps[:, t], mk[:, t], scale, TAKEN,
                                                              ALU.add, ALU.max, mx[:, t:t + 1]))
                        dve.wait_ge(dve_chain, n_chain[0])
                        dve.tensor_scalar(att[:, 1, n, :], mx, -1.0, None, ALU.mult).then_inc(max_ready, 1)
                    for _ in range(2 + n % 2):
                        if picks:
                            picks.pop(0)()
                    if n >= 3:
                        i = n - 3
                        _, _, _, _, _, _, _, yc, part = js[i]
                        b = (j0 + i) % 2
                        dve.wait_ge(probs_ready, TT * (j0 + i + 1))
                        link(dve.reciprocal(att[:, 3, i, :], att[:, 2, i, :]))
                        if part == 2:
                            link(dve.tensor_scalar(att[:, 3, i, :], att[:, 3, i, :], nlam[:, m:m + 1], None, ALU.mult))
                        dve.wait_ge(weighted_ready, j0 + i + 1)
                        for t in range(TT):
                            o = bank[4 + b][:, t * HD:(t + 1) * HD]
                            y = h[:, t, yc:yc + HD]
                            w = att[:, 3, i, t:t + 1]
                            if part == 2:
                                dve.wait_ge(head_output_done, TT * (j0 + i))
                                ins = dve.scalar_tensor_tensor(y, o, w, y, ALU.mult, ALU.add)
                            else:
                                ins = dve.tensor_scalar(y, o, w, None, ALU.mult)
                            ins.then_inc(head_output_done, 1)
                    if 0 <= n - first_diff < len(diff_steps):
                        dve.wait_ge(head_output_done, TT * (j0 + n - 2))
                        diff_steps[n - first_diff]()
                jobs_done[0] += len(js)
                dve.wait_ge(head_output_done, TT * jobs_done[0])
                if l < DEPTH:
                    dve.wait_ge(squares_summed, sums[0] + 2 * TT)
                    sums[0] += 2 * TT
                    dve.tensor_scalar(stat[:, 1, 0:2 * TT], stat[:, 0, 0:2 * TT], 1.0 / (HA * HD), EPS, ALU.mult, ALU.add
                                      ).then_inc(means_ready, 1)
                    roots[0] += 1
                    dve.wait_ge(roots_ready, roots[0])
                    for t in range(TT):
                        for i in range(2):
                            y = h[:, t, i * HA * HD:(i + 1) * HA * HD]
                            c = stat[:, 2, 2 * t + i:2 * t + i + 1]
                            ins = dve.tensor_scalar(y, y, c, None, ALU.mult)
                            if i:
                                ins.then_inc(rows_normed, 1)
                    turn(gain_of(G_OUT + KC * m), None)
                else:
                    dve.nop().then_inc(rows_normed, TT)
                    turn(None, None)

                xns[0] += TT
                if l >= DEPTH:
                    rows_used[0] += 1
                    dve.wait_ge(row_loaded, 16 * rows_used[0])
                J = steps(l)
                start, t0 = ring.start, ring.t
                ring.stage(RAW if l < DEPTH else 3 if l < MOE else MORE_RAW, SPLIT if l < DEPTH else 3)
                pool_tiles(2)
                for c in range(D // COL):
                    used = start + 2 * c + 2
                    x_update(c, l >= DEPTH, lambda t: bank[4 + 2 * (c % 2) + t][:, :],
                             lambda: dve.wait_ge(w_used, FREE_SPLIT + used))
                if l >= DEPTH:
                    dve.wait_ge(x_updated, updates[0])
                    dve.nop().then_inc(row_used, 1)

                norm()
                if l < DEPTH:
                    turn(gain_of(G_NORM2 + KC * m), None)
                else:
                    turn(gated_gain(m, 1), shift_of(m, 2))
                pool_is_through()

                def hid_lo_part(at, t, n, b):
                    dve.wait_ge(hidden_hi_done, at + t + 1)
                    src = b[:, 0:n * P].rearrange("p (f n) -> p f n", f=n)
                    o = slice(t * P, (t + 1) * P)
                    dve.tensor_tensor(hid_lo[:, 0:n, o], src, hid_hi[:, 0:n, o].bitcast(F32), ALU.subtract
                                      ).then_inc(hidden_lo_done, 1)

                if l < DEPTH:
                    def ada(k, n):
                        acc = big[:, n * PIECE:(n + 1) * PIECE]
                        w = scr(X_ADA + n * PIECE, PIECE)
                        c = None if isinstance(k, int) and k == KC else silu_col(k)
                        at = 9 * l + k
                        dve.wait_ge(ada_in[n], 16 * (at + 1))
                        if isinstance(k, int) and k == 0:
                            ins = dve.tensor_scalar(acc, w, c, None, ALU.mult)
                        else:
                            dve.wait_ge(ada_used, NPIECE * (at - 1) + n + 1)
                            if isinstance(k, int) and k == KC:
                                ins = dve.tensor_tensor(acc[0:1, :], w[0:1, :], acc[0:1, :], ALU.add)
                            else:
                                ins = dve.scalar_tensor_tensor(acc, w, c, acc, ALU.mult, ALU.add)
                        ins.then_inc(ada_used, 1)

                    def step(j, more):
                        ada(j, 0)
                        if more:
                            lo()
                        ada(j, 1)
                        if more:
                            lo()
                        ada(j, 2)
                        lo()
                        lo()
                        for t in range(TT):
                            hid_lo_part(ub + j * TT, t, 4, bank[2 + t])

                    step(0, True)
                    with dve.Fori(0, J - 2) as j:
                        ring.enter(j, 4)
                        step(j + 1, True)
                    ring.leave(J - 2)
                    step(J - 1, False)
                    for n in range(NPIECE):
                        ada(KC, n)
                    ub += J * TT
                elif l < MOE:
                    def step(j, more):
                        if more:
                            lo()
                        gate_mul(dve, ub + j * TT, TT, X_ACT, X_ACT2, [bank[0], bank[1]])
                        if more:
                            lo()
                        lo()
                        for t in range(TT):
                            hid_lo_part(ub + j * TT, t, 2, bank[2 + t])

                    with dve.Fori(0, J - 1) as j:
                        ring.enter(j, 3)
                        step(j, True)
                    ring.leave(J - 1)
                    step(J - 1, False)
                    ub += J * TT
                if l < MOE:
                    if l >= DEPTH:
                        rows_used[0] += 1
                        dve.wait_ge(row_loaded, 16 * rows_used[0])
                    end = ring.t
                    ring.stage()
                    pool_tiles(2)
                    for c in range(2):
                        x_update(c, l >= DEPTH, lambda t: bank[4 + 2 * t + c][:, :],
                                 lambda: dve.wait_ge(w_used, FREE_SPLIT + end))
                    if l >= DEPTH:
                        dve.wait_ge(x_updated, updates[0])
                        dve.nop().then_inc(row_used, 1)
                    if l == DEPTH - 1:
                        rows_used[0] += 1
                        dve.wait_ge(row_loaded, 16 * rows_used[0])
                        norm(x)
                        dve.wait_ge(rows_normed, xns[0])
                        updates[0] += TT
                        dve.nop().then_inc(x_updated, TT)
                        dve.nop().then_inc(row_used, 1)
                    continue

                lg, m8, nm, ex, gt, sel, den, wts, pos, tot = (rt[:, i] for i in range(10))
                dve.wait_ge(logits_by_expert_ready, 1)
                dve.tensor_copy(lgT, bank[6][0:NE, 0:SEQ]).then_inc(logits_by_expert_stored, 1)
                dve.wait_ge(logits_ready, 1)
                link(dve.tensor_copy(lg, bank[4][:, 0:TT * NE].rearrange("p (t e) -> p t e", t=TT)))
                for t in range(TT):
                    mark(dve.max(m8[:, t, :], lg[:, t, :]))
                dve.wait_ge(dve_chain, n_chain[0])
                dve.tensor_scalar(nm[:, :, 0:1], m8[:, :, 0:1], -1.0, None, ALU.mult).then_inc(selected, 1)
                cmp = scr(X_MACT, 2 * NE * NE, 2, NE, NE)
                for t in range(TT):
                    mine = lg[:, t, :].unsqueeze(2).broadcast_to([P, NE, NE])
                    other = lg[:, t, :].unsqueeze(1).broadcast_to([P, NE, NE])
                    mark(dve.tensor_tensor(cmp[:, 0], other, mine, ALU.is_gt))
                    link(dve.tensor_tensor(cmp[:, 1], other, mine, ALU.is_equal))
                    link(dve.tensor_tensor(cmp[:, 1], cmp[:, 1], k_("earlier", NE, NE), ALU.mult))
                    link(dve.tensor_tensor(cmp[:, 0], cmp[:, 0], cmp[:, 1], ALU.add))
                    link(dve.tensor_reduce(gt[:, t, :], cmp[:, 0], AX.X, ALU.add))
                dve.tensor_scalar(sel, gt, 2.0, None, ALU.is_lt).then_inc(selected, 1)
                dve.wait_ge(selected, 2)
                dve.wait_ge(router_exps_ready, TT)
                link(dve.tensor_tensor(ex, ex, sel, ALU.mult))
                link(dve.tensor_reduce(den[:, :, 0:1], ex, AX.X, ALU.add))
                link(dve.reciprocal(den[:, :, 0:1], den[:, :, 0:1]))
                for t in range(TT):
                    mark(dve.tensor_scalar(wts[:, t, :], ex[:, t, :], den[:, t, 0:1], None, ALU.mult))
                dve.wait_ge(counts_ready, 1)
                cnt = bank[5][:, 0:3 * NE].rearrange("p (t e) -> p t e", t=3)
                link(dve.tensor_scalar(pos, cnt[:, 0:2, :], 1.0, None, ALU.add))
                link(dve.tensor_tensor(pos, pos, sel, ALU.mult))
                link(dve.tensor_scalar(pos, pos, -1.0, None, ALU.add))
                link(dve.tensor_reduce(tot[0:1, 0, 0:1], cnt[0:1, 2, :], AX.X, ALU.max))
                dve.tensor_copy(flag[0:1, 0:1], tot[0:1, 0, 0:1]).then_inc(fullest_counted, 1)
                acc = big[:, 0:TT * D].rearrange("p (t n) -> p t n", t=TT)
                dve.wait_ge(sums_cleared, 1)
                dve.nop().then_inc(output_added, 1)

                def lists(e, n):
                    if not (isinstance(n, int) and n == 0):
                        dve.wait_ge(gathered, n)
                        dve.wait_ge(list_turned, n)
                    pe_, we = pos[:, :, bass.ds(e, 1)], wts[:, :, bass.ds(e, 1)]
                    for t in range(TT):
                        dve.tensor_scalar(scr(X_G + t * P, P), iota, pe_[:, t], None, ALU.is_equal).then_inc(list_ready, 1)
                        dve.tensor_scalar(scr(X_GW + t * P, P), iota, pe_[:, t], we[:, t], ALU.is_equal, ALU.mult
                                          ).then_inc(list_ready, 1)

                def listed_rows(p, n):
                    dve.wait_ge(gathered, n + 1)
                    if not (isinstance(n, int) and n == 0):
                        dve.wait_ge(gathered_hi_done, n)
                        dve.wait_ge(gathered_lo_done, n)
                    for k in range(KC):
                        dve.tensor_scalar(scr(X_HGF + k * P, P), bank[4 + k // 4][:, (k % 4) * P:(k % 4 + 1) * P],
                                          modg[:, m, 1, k:k + 1], modcol[:, m, KC * 2 + k:KC * 2 + k + 1], ALU.mult, ALU.add
                                          ).then_inc(gathered_scaled, 1)
                    o = slice(KC // 2 * p, KC // 2 * (p + 1))
                    dve.wait_ge(gathered_hi_done, n + 1)
                    dve.tensor_tensor(hT_lo[:, o, :], scr(X_HGF, KC * P, KC // 2, SEQ), hT_hi[:, o, :].bitcast(F32),
                                      ALU.subtract).then_inc(gathered_lo_done, 1)

                def add_output(n):
                    dve.wait_ge(scattered, n + 1)
                    for t in range(TT):
                        for c in range(2):
                            at = acc[:, t, c * COL:(c + 1) * COL]
                            dve.wait_ge(output_added, 4 * n + 1)
                            dve.tensor_tensor(at, bank[4 + 2 * t + c][:, :], at, ALU.add).then_inc(output_added, 1)

                def experts(t0, loads0, n0):
                    def body(i, p, n, first, last):
                        expert_ring(ring, i, p, t0, loads0)

                        def step(j, more=True, between=None):
                            if more:
                                lo()
                            gate_mul(dve, ub + n * MJ + j, 1, X_MACT, X_MACT2, [bank[0]])
                            if between:
                                between()
                            if more:
                                lo()
                            lo()
                            hid_lo_part(ub + n * MJ + j, 0, 2, bank[1])

                        step(0)
                        if not last:
                            lists(2 * i + p + 1, n + 1)
                        step(1, between=None if first else lambda: add_output(n - 1))
                        if not last:
                            listed_rows((p + 1) % 2, n + 1)
                        expert_steps(dve, ring, lambda j: step(j, not (last and isinstance(j, int))))

                    lists(0, n0)
                    listed_rows(0, n0)
                    each_expert(dve, n0, body)
                    add_output(n0 + NE - 1)

                loads0 = [0] * MORE_RAW
                experts(t0, loads0, 0)
                full = dve.value_load(flag[0:1, 0:1], min_val=0, max_val=SEQ)
                dve.wait_ge(output_added, 1 + 4 * NE)
                with dve.If(full > P):
                    dve.tensor_scalar(pos, pos, -float(P), None, ALU.add).then_inc(places_moved, 1)
                    dve.wait_ge(places_moved, 1)
                    expert_ring(ring, NE // 2, 0, t0, loads0, 0)
                    lo()
                    lo()
                    experts(t0 + NE * MT, loads0, NE)
                    dve.wait_ge(output_added, 1 + 8 * NE)
                rows_used[0] += 1
                dve.wait_ge(row_loaded, 16 * rows_used[0])
                for t in range(TT):
                    ins = dve.tensor_tensor(acc[:, t, :], acc[:, t, :], rowg[:, :], ALU.mult)
                    link(ins)
                    if t == TT - 1:
                        dve.nop().then_inc(row_used, 1)
                    updated(dve.tensor_tensor(x[:, t, :], acc[:, t, :], x[:, t, :], ALU.add))
            rows_used[0] += 1
            dve.wait_ge(row_loaded, 16 * rows_used[0])
            norm(h)

        @block.scalar
        def _(act):
            ring = Tiles()

            def stage():
                ring.stage()
                act.wait_ge(w_used, FREE_SPLIT + ring.t)

            def hi():
                freed = ring.freed()
                t, s, q, n = ring.next()
                act.wait_ge(w_loaded[s], 32 * n)
                act.wait_ge(w_used, FREE_SPLIT + freed)
                act.activation(w_hi[:, q, :], raw(s), ACT.Copy).then_inc(hi_done, 1)

            quarter = [0, None]

            def hi_quarter_of_tile():
                k = quarter[0]
                quarter[0] += 1
                if k % 4 == 0:
                    t, s, q, n = quarter[1] = ring.next()
                    act.wait_ge(w_loaded[s], 32 * n)
                    act.wait_ge(w_used, FREE_SPLIT + t - ring.split + 1)
                t, s, q, n = quarter[1]
                o = slice(k % 4 * COL, (k % 4 + 1) * COL)
                act.activation(w_hi[:, q, o], raw(s)[:, o], ACT.Copy).then_inc(hi_done if k % 4 == 3 else hi_quarter, 1)

            updates = [0]

            def squares():
                if not updates[0]:
                    act.wait_ge(x_loaded, 16)
                    act.wait_ge(lo_done, FREE_RAW)
                for t in range(TT):
                    if updates[0]:
                        act.wait_ge(x_updated, TT * (updates[0] - 1) + t + 1)
                    act.activation(h[:, t, :], x[:, t, :], ACT.Square, accum_out=stat[:, 0, t:t + 1]).then_inc(squares_summed, 1)
                updates[0] += 1

            turned = [0]

            def turn():
                m = turned[0]
                turned[0] += 1
                for b in range(2):
                    ks = slice(4 * b, 4 * b + 4)
                    act.wait_ge(rows_scaled, KC * m + 4 * (b + 1))
                    act.activation(hT_hi[:, ks, :], htf[:, ks, :], ACT.Copy).then_inc(rows_hi_done, 1)

            def ada_columns(l):
                act.wait_ge(ada_summed, 5 * l + 1)
                act.activation(modcol[:, l, :], bank[0][:, 0:4 * KC], ACT.Copy).then_inc(ada_stored, 1)

            def ada_gates(l):
                for i, b in enumerate(GATE_BANKS[l]):
                    act.wait_ge(ada_summed, 5 * l + 2 + i)
                    act.activation(scr(X_ADA + i * COL, COL), bank[b][:, :], ACT.Copy).then_inc(ada_stored, 1)
                act.wait_ge(ada_stored, 5 * (l + 1))
                act.dma_start(gates[l].rearrange("p a n -> p (a n)"), scr(X_ADA, 2 * D)).then_inc(gates_stored, 16)

            def tables():
                act.wait_ge(gains_ready, 1)
                act.activation(csilu[:, :], gcol[:, G_C:G_C + KC], ACT.Silu)
                act.wait_ge(angles_ready, 1)
                act.activation(ang[:, 2], ang[:, 0], ACT.Sin).then_inc(sines_ready, 1)
                act.activation(ang[:, 3], ang[:, 1], ACT.Sin).then_inc(sines_ready, 1)
                act.wait_ge(lambda_summed, DEPTH)
                act.activation(lams[:, 4:8], lams[:, 0:4], ACT.Exp).then_inc(lambda_exps_ready, 1)

            jobs_done = [0]
            ub = 0
            for l in LAYERS:
                m = l % DEPTH
                widths = groups(width(l))
                squares()
                if l == 0:
                    hi()
                    hi()
                if 0 < l <= DEPTH:
                    ada_columns(l - 1)
                if l == DEPTH:
                    ada_gates(l - 1)
                turn()
                if 0 < l < DEPTH:
                    ada_gates(l - 1)
                if l == 0:
                    tables()

                def project(c, n, g):
                    hi()
                    hi()
                    empty(c, n, [4 + 2 * g, 5 + 2 * g], ring.start)

                def empty(c, n, banks, start):
                    act.wait_ge(w_used, FREE_SPLIT + start + 2 * c + 2)
                    for t in range(TT):
                        act.activation(prj[:, t, bass.ds(c * COL, n)], bank[banks[t]][:, 0:n], ACT.Copy).then_inc(group_stored, 1)

                start = ring.start
                group_loop(act, ring, widths[:-1], project)

                nb = (len(pairs(l)) + 1) // 2
                if 0 < l <= DEPTH:
                    act.wait_ge(gates_stored, 16 * l)
                for i in range(nb):
                    w = min(2, len(pairs(l)) - 2 * i)
                    act.wait_ge(heads_turned, BANKS0[l] + i + 1)
                    act.activation(qkT[:, 2 * i:2 * i + w, :], bank[i % 4][:, 0:w * SEQ].rearrange("p (a n) -> p a n", a=w),
                                   ACT.Copy).then_inc(heads_stored, 1)

                js = jobs(l)
                j0 = jobs_done[0]
                for n in range(len(js) + 2):
                    if n == 2:
                        empty(len(widths) - 1, widths[-1], LAST_BANKS, start)
                        stage()
                    if n >= 2:
                        b = (j0 + n) % 2
                        act.wait_ge(probs_turned, j0 + n - 1)
                        if n >= 4:
                            act.wait_ge(weighted_ready, j0 + n - 3)
                        act.activation(scr(X_PT + b * COL, COL), bank[2 + b][:, :], ACT.Copy).then_inc(probs_stored, 1)
                    if n < len(js):
                        b = (j0 + n) % 2
                        act.wait_ge(max_ready, j0 + n + 1)
                        if n >= 2:
                            act.wait_ge(probs_turned, j0 + n - 1)
                        for t in range(TT):
                            act.activation(scr(X_P + b * COL + t * SEQ, SEQ), scr(X_SM + b * COL + t * SEQ, SEQ), ACT.Exp,
                                           bias=att[:, 1, n, t:t + 1], accum_out=att[:, 2, n, t:t + 1]).then_inc(probs_ready, 1)
                    if 2 <= n < 18:
                        hi_quarter_of_tile()
                jobs_done[0] += len(js)
                if l < DEPTH:
                    act.wait_ge(head_output_done, TT * jobs_done[0])
                    for t in range(TT):
                        for i in range(2):
                            w = HA * HD
                            act.activation(scr(X_SM + (2 * t + i) * w, w), h[:, t, i * w:(i + 1) * w], ACT.Square,
                                           accum_out=stat[:, 0, 2 * t + i:2 * t + i + 1]).then_inc(squares_summed, 1)
                turn()
                J = steps(l)
                t0, loads0 = ring.t, list(ring.loads)
                ring.stage(RAW if l < DEPTH else 3 if l < MOE else MORE_RAW, SPLIT if l < DEPTH else 3)
                hi()
                hi()
                squares()
                turn()

                def first_tiles():
                    ring.stage()
                    hi()
                    hi()

                def hid_high_part(at, t, n, b):
                    act.wait_ge(hidden_turned, at + t + 1)
                    src = b[:, 0:n * P].rearrange("p (f n) -> p f n", f=n)
                    act.activation(hid_hi[:, 0:n, t * P:(t + 1) * P], src, ACT.Copy).then_inc(hidden_hi_done, 1)

                if l < DEPTH:
                    def step(j, more):
                        up = 2 if isinstance(j, int) and j == 0 else 4 * j
                        if more:
                            hi()
                        act.wait_ge(w_used, FREE_SPLIT + ring.start + up)
                        for t in range(TT):
                            act.activation(scr(X_ACT + t * F_UP, F_UP), bank[t][:, :], ACT.Relu).then_inc(activated, 1)
                        if more:
                            hi()
                        hi()
                        hi()
                        for t in range(TT):
                            hid_high_part(ub + j * TT, t, 4, bank[2 + t])

                    step(0, True)
                    with act.Fori(0, J - 2) as j:
                        ring.enter(j, 4)
                        step(j + 1, True)
                    ring.leave(J - 2)
                    step(J - 1, False)
                    ub += J * TT
                    first_tiles()
                elif l < MOE:
                    def step(j, more):
                        up = 2 if isinstance(j, int) and j == 0 else 3 * j + 1
                        if more:
                            hi()
                        act.wait_ge(w_used, FREE_SPLIT + ring.start + up)
                        for t in range(TT):
                            act.activation(scr(X_ACT + t * F_GATED, F_GATED), bank[t][:, 0:F_GATED], ACT.Silu).then_inc(activated, 1)
                        if more:
                            hi()
                        hi()
                        for t in range(TT):
                            hid_high_part(ub + j * TT, t, 2, bank[2 + t])

                    step(0, True)
                    with act.Fori(0, J - 2) as j:
                        ring.enter(j, 3)
                        step(j + 1, True)
                    ring.leave(J - 2)
                    step(J - 1, False)
                    ub += J * TT
                    first_tiles()
                else:
                    lg, nm, ex = rt[:, 0], rt[:, 2], rt[:, 3]
                    act.wait_ge(selected, 1)
                    for t in range(TT):
                        act.activation(ex[:, t, :], lg[:, t, :], ACT.Exp, bias=nm[:, t, 0:1]).then_inc(router_exps_ready, 1)

                    def listed_rows(p, n):
                        act.wait_ge(list_turned, n + 1)
                        act.activation(scr(X_GT[p], TT * P), bank[6][:, 0:TT * P], ACT.Copy).then_inc(list_stored, 1)
                        act.wait_ge(gathered_scaled, KC * (n + 1))
                        o = slice(KC // 2 * p, KC // 2 * (p + 1))
                        act.activation(hT_hi[:, o, :], scr(X_HGF, KC * P, KC // 2, SEQ), ACT.Copy).then_inc(gathered_hi_done, 1)

                    def output(n, used):
                        act.wait_ge(w_used, FREE_SPLIT + used)
                        if not (isinstance(n, int) and n == 0):
                            act.wait_ge(scattered, n)
                        for c in range(2):
                            act.activation(scr(X_YE + c * COL, COL), bank[2 + c][:, :], ACT.Copy).then_inc(output_stored, 1)

                    def experts(t0, loads0, n0):
                        def body(i, p, n, first, last):
                            expert_ring(ring, i, p, t0, loads0)
                            te = t0 + i * (2 * MT) + MT * p

                            def step(j, up, more=True):
                                if more:
                                    hi()
                                act.wait_ge(w_used, FREE_SPLIT + up)
                                act.activation(scr(X_MACT, F_GATED), bank[0][:, 0:F_GATED], ACT.Silu).then_inc(activated, 1)
                                if more:
                                    hi()
                                hi()
                                hid_high_part(ub + n * MJ + j, 0, 2, bank[1])

                            step(0, te + (2 if first else 1))
                            if not first:
                                output(n - 1, te + 2)
                            step(1, te + 4)
                            if not last:
                                listed_rows((p + 1) % 2, n + 1)
                            expert_steps(act, ring, lambda j: step(j, te + 3 * j + 1, not (last and isinstance(j, int))))

                        listed_rows(0, n0)
                        each_expert(act, n0, body)
                        output(n0 + NE - 1, t0 + NE * MT)

                    experts(t0, loads0, 0)
                    act.wait_ge(fullest_counted, 1)
                    full = act.value_load(flag[0:1, 0:1], min_val=0, max_val=SEQ)
                    with act.If(full > P):
                        t1, loads1 = expert_after(t0, loads0)
                        ring.t, ring.i, ring.loads = t1, 0, list(loads1)
                        hi()
                        hi()
                        experts(t1, loads1, NE)
                if l == DEPTH - 1:
                    squares()
            squares()

        @block.tensor
        def _(pe):
            ring = Tiles()

            def product(dst, a_hi, a_lo, b_hi, b_lo, start, stop_):
                pe.matmul(dst, a_hi, b_hi, start=start, stop=False)
                pe.matmul(dst, a_hi, b_lo, start=False, stop=False)
                return pe.matmul(dst, a_lo, b_hi, start=False, stop=stop_)

            def turn_rows():
                xns[0] += TT
                pe.wait_ge(rows_normed, xns[0])
                for k in range(KC):
                    for t in range(TT):
                        o = (k % 2) * SEQ + t * P
                        ins = pe.transpose(bank[k // 2][:, o:o + P], h[:, t, k * P:(k + 1) * P], ident)
                    ins.then_inc(rows_turned, 1)
                turned[0] += 1

            xns, turned = [0], [0]

            def lhs(k, t):
                s = slice(t * P, (t + 1) * P)
                return hT_hi[:, k, s], hT_lo[:, k, s]

            def lhs_listed(k, t):
                s = slice((k % 2) * P, (k % 2 + 1) * P)
                return hT_hi[:, k // 2, s], hT_lo[:, k // 2, s]

            def up(dst, left, ntt, n, waits_rows=False):
                for a in range(2):
                    if waits_rows:
                        pe.wait_ge(rows_lo_done, 2 * (turned[0] - 1) + 1 + a)
                    t_, _, q, _ = ring.next()
                    pe.wait_ge(lo_done, FREE_RAW + t_ + 1)
                    for k in range(4):
                        s = slice(k * n, (k + 1) * n)
                        for t in range(ntt):
                            ins = product(dst[t][:, 0:n], *left(4 * a + k, t), w_hi[:, q, s], w_lo[:, q, s],
                                          a == 0 and k == 0, a == 1 and k == 3)
                    ins.then_inc(w_used, 1)

            def down(at, nd, ntt, dst, first, last):
                pe.wait_ge(hidden_lo_done, at + ntt)
                for b in range(nd):
                    t_, _, q, _ = ring.next()
                    pe.wait_ge(lo_done, FREE_RAW + t_ + 1)
                    for i in range(2):
                        f = 2 * b + i
                        for t in range(ntt):
                            o = slice(t * P, (t + 1) * P)
                            for c in range(2):
                                s = slice(i * D + c * COL, i * D + (c + 1) * COL)
                                ins = product(dst(t, c), hid_hi[:, f, o], hid_lo[:, f, o], w_hi[:, q, s], w_lo[:, q, s],
                                              first and f == 0, last and f == 2 * nd - 1)
                    ins.then_inc(w_used, 1)

            def turn_hidden(at, ntt, n, src, width_, dst):
                for t in range(ntt):
                    pe.wait_ge(hidden_ready, at + t + 1)
                    for f in range(n):
                        ins = pe.transpose(dst[t][:, f * P:(f + 1) * P],
                                           scr(src + t * width_ + f * P, P), ident)
                    ins.then_inc(hidden_turned, 1)

            pe.wait_ge(consts_loaded, 16)
            pe.wait_ge(gains_loaded, 16 * R_LOADS)
            pe.transpose(bank[7][:, 0:NG], slab[0:NG, S_RAW:S_RAW + P], ident[0:NG, 0:NG]).then_inc(gains_turned, 1)

            def gate_rows(l, banks):
                for i, b in enumerate(banks):
                    if b in banks[:i]:
                        pe.wait_ge(ada_stored, 5 * l + 2 + banks.index(b))
                    o = (2 + 3 * (i // 2)) * D + (i % 2) * COL
                    pe.matmul(bank[b][:, :], ones, big[:, o:o + COL], start=True, stop=True).then_inc(ada_summed, 1)

            jobs_done, idx_done = [0], [0]
            groups_done = 0
            ub = 0
            for l in LAYERS:
                m = l % DEPTH
                widths = groups(width(l))
                if 0 < l <= DEPTH:
                    pe.wait_ge(ada_stored, 5 * l - (4 if l < DEPTH else 0))
                turn_rows()
                if 0 < l < DEPTH:
                    gate_rows(l - 1, GATE_BANKS[l - 1])
                    pe.wait_ge(ada_stored, 5 * l)
                pe.wait_ge(rows_lo_done, 2 * turned[0])
                ring.stage()

                def project(c, n, g):
                    pe.wait_ge(group_stored, FREE_BANKS + TT * (groups_done + c - 1))
                    up([bank[4 + 2 * g], bank[5 + 2 * g]], lhs, TT, n)

                group_loop(pe, ring, widths[:-1], project)

                pe.wait_ge(rope_dve_done, l + 1)
                all_but_last = proj_evac(l) - TT
                pe.wait_ge(group_stored, all_but_last)
                ps = pairs(l)
                pool_pairs = (6, 10) if l < DEPTH else (7, 11)
                for i, (where, c) in enumerate(ps):
                    b = i // 2
                    if i in pool_pairs:
                        pe.wait_ge(rope_pool_done, 2 * l + 1 + pool_pairs.index(i))
                    if i % 2 == 0 and b >= 4:
                        pe.wait_ge(heads_stored, BANKS0[l] + b - 3)
                    for t in range(TT):
                        src = prj[:, t, c:c + P] if where == "big" else h[:, t, c:c + P]
                        o = (i % 2) * SEQ + t * P
                        ins = pe.transpose(bank[b % 4][:, o:o + P], src, ident)
                    if i % 2 or i == len(ps) - 1:
                        ins.then_inc(heads_turned, 1)
                pe.wait_ge(heads_stored, BANKS0[l] + (len(ps) + 1) // 2)

                if l >= DEPTH:
                    for i in range(I2):
                        n = idx_done[0] = idx_done[0] + 1
                        s = slice(HD * (i % 2), HD * (i % 2) + HD)
                        for t in range(TT):
                            ins = pe.matmul(bank[IX_BANKS[i]][:, t * SEQ:(t + 1) * SEQ], qkT[s, 4 + i // 2, t * P:(t + 1) * P],
                                            qkT[s, 6, :], start=True, stop=True)
                        ins.then_inc(index_ready, 1)

                js = jobs(l)
                j0 = jobs_done[0]
                for n in range(len(js) + 3):
                    if n == 2:
                        up([bank[b] for b in LAST_BANKS], lhs, TT, widths[-1])
                        groups_done += len(widths)
                        if l >= DEPTH:
                            pe.wait_ge(index_read, idx_done[0])
                    if n < len(js):
                        qp, kp, base, dims, _, _, _, _, _ = js[n]
                        b = SC_BANKS[n % 3]
                        if n >= 3:
                            pe.wait_ge(max_ready, j0 + n - 2)
                        s = slice(base, base + dims)
                        for t in range(TT):
                            ins = pe.matmul(bank[b][:, t * SEQ:(t + 1) * SEQ], qkT[s, qp, t * P:(t + 1) * P], qkT[s, kp, :],
                                            start=True, stop=True)
                        ins.then_inc(scores_ready, 1)
                    if 2 <= n <= len(js) + 1:
                        i = n - 2
                        b = (j0 + i) % 2
                        pe.wait_ge(probs_ready, TT * (j0 + i + 1))
                        if i == 1:
                            pe.wait_ge(group_stored, proj_evac(l))
                        if i >= 2:
                            pe.wait_ge(probs_stored, j0 + i - 1)
                        for t in range(TT):
                            for k in range(TT):
                                ins = pe.transpose(bank[2 + b][:, k * SEQ + t * P:k * SEQ + (t + 1) * P],
                                                   scr(X_P + b * COL + t * SEQ + k * P, P), ident)
                        ins.then_inc(probs_turned, 1)
                    if n >= 3:
                        i = n - 3
                        b = (j0 + i) % 2
                        vc = js[i][4]
                        pe.wait_ge(probs_stored, j0 + i + 1)
                        if i >= 2:
                            pe.wait_ge(head_output_done, TT * (j0 + i - 1))
                        for t in range(TT):
                            for k in range(TT):
                                ins = pe.matmul(bank[4 + b][:, t * HD:(t + 1) * HD],
                                                scr(X_PT + b * COL + k * SEQ + t * P, P), prj[:, k, vc:vc + HD],
                                                start=k == 0, stop=k == TT - 1)
                        ins.then_inc(weighted_ready, 1)
                jobs_done[0] += len(js)

                turn_rows()
                ring.stage()
                for c in range(D // COL):
                    up([bank[4 + 2 * c], bank[5 + 2 * c]], lhs, TT, COL, waits_rows=c == 0)
                turn_rows()

                J = steps(l)
                if l < MOE:
                    nd = 2 if l < DEPTH else 1
                    nf, wid = (4, F_UP) if l < DEPTH else (2, F_GATED)
                    a2 = X_ACT2
                    ring.stage(RAW, SPLIT if l < DEPTH else 3)

                    def step(j, first=False):
                        up([bank[0], bank[1]], lhs, TT, COL, waits_rows=isinstance(j, int) and j == 0)
                        if not (isinstance(j, int) and j == 0):
                            down(ub + TT * (j - 1), nd, TT, lambda t, c: bank[4 + 2 * t + c][:, :], first, False)
                        turn_hidden(ub + TT * j, TT, nf, a2, wid, [bank[2], bank[3]])

                    step(0)
                    step(1, True)
                    with pe.Fori(0, J - 2) as j:
                        ring.enter(j, 2 + nd)
                        step(j + 2)
                    ring.leave(J - 2)
                    down(ub + TT * (J - 1), nd, TT, lambda t, c: bank[4 + 2 * t + c][:, :], False, True)
                    ub += TT * J
                    if l < DEPTH:
                        pe.wait_ge(ada_used, NPIECE * 9 * (l + 1))
                        pe.wait_ge(activated, ub)
                        for i, v in enumerate(COLUMN_VECTORS):
                            for k in range(KC):
                                o = v * D + k * P
                                ins = pe.matmul(bank[0][:, KC * i + k:KC * i + k + 1], big[:, o:o + P], ones[:, 0:1],
                                                start=True, stop=True)
                        ins.then_inc(ada_summed, 1)
                        if l == DEPTH - 1:
                            gate_rows(l, GATE_BANKS[l])
                        if l == DEPTH - 1:
                            xns[0] += TT
                    continue

                pe.wait_ge(rows_lo_done, 2 * turned[0])
                for k in range(KC):
                    ins = product(bank[6][0:NE, 0:SEQ], wr_hi[:, k, :], wr_lo[:, k, :], hT_hi[:, k, :], hT_lo[:, k, :],
                                  k == 0, k == KC - 1)
                ins.then_inc(logits_by_expert_ready, 1)
                pe.wait_ge(logits_by_expert_stored, 1)
                for t in range(TT):
                    ins = pe.transpose(bank[4][:, t * NE:(t + 1) * NE], lgT[:, t * P:(t + 1) * P], ident[0:NE, 0:NE])
                ins.then_inc(logits_ready, 1)
                pe.wait_ge(selected, 2)
                sel = rt[:, 5]
                pe.matmul(bank[5][:, 0:NE], before, sel[:, 0, :], start=True, stop=True)
                pe.matmul(bank[5][:, NE:2 * NE], ones, sel[:, 0, :], start=True, stop=False)
                pe.matmul(bank[5][:, NE:2 * NE], before, sel[:, 1, :], start=False, stop=True)
                pe.matmul(bank[5][:, 2 * NE:3 * NE], ones, sel[:, 0, :], start=True, stop=False)
                pe.matmul(bank[5][:, 2 * NE:3 * NE], ones, sel[:, 1, :], start=False, stop=True).then_inc(counts_ready, 1)

                def gather(n):
                    pe.wait_ge(list_ready, 4 * n + 4)
                    if isinstance(n, int) and n % NE == 0:
                        pe.wait_ge(output_added, 4 * n + 1)
                    else:
                        pe.wait_ge(output_added, 4 * n - 3)
                    if not (isinstance(n, int) and n == 0):
                        pe.wait_ge(list_stored, n)
                    for k in range(KC):
                        for t in range(TT):
                            ins = pe.matmul(bank[4 + k // 4][:, (k % 4) * P:(k % 4 + 1) * P], h[:, t, k * P:(k + 1) * P],
                                            scr(X_G + t * P, P), start=t == 0, stop=t == TT - 1)
                    ins.then_inc(gathered, 1)
                    for t in range(TT):
                        ins = pe.transpose(bank[6][:, t * P:(t + 1) * P], scr(X_GW + t * P, P), ident)
                    ins.then_inc(list_turned, 1)

                def scatter(p, n):
                    pe.wait_ge(output_stored, 2 * n + 2)
                    pe.wait_ge(list_stored, n + 1)
                    pe.wait_ge(gathered_scaled, KC * (n + 1))
                    for t in range(TT):
                        for c in range(2):
                            ins = pe.matmul(bank[4 + 2 * t + c][:, :], scr(X_GT[p] + t * P, P), scr(X_YE + c * COL, COL),
                                            start=True, stop=True)
                    ins.then_inc(scattered, 1)

                def sums(n, j, first, last):
                    down(ub + n * MJ + j, 1, 1, lambda t, c: bank[2 + c][:, :], first, last)

                def experts(t0, n0):
                    def body(i, p, n, first, last):
                        ring.t, ring.i, ring.split = t0 + i * (2 * MT) + MT * p - (not first), 0 if first else 2, 3
                        pe.wait_ge(gathered_lo_done, n + 1)

                        def rows_up(j):
                            up([bank[0]], lambda k, t: lhs_listed(k + KC * p, t), 1, COL)

                        def turn(j):
                            turn_hidden(ub + n * MJ + j, 1, 2, X_MACT2, F_GATED, [bank[1]])

                        rows_up(0)
                        if not first:
                            sums(n - 1, MJ - 1, False, True)
                        turn(0)
                        rows_up(1)
                        if not first:
                            scatter(1 - p, n - 1)
                        sums(n, 0, True, False)
                        turn(1)
                        if not last:
                            gather(n + 1)
                        with pe.Fori(0, MJ - 2) as j:
                            ring.enter(j, 3)
                            rows_up(j + 2)
                            sums(n, j + 1, False, False)
                            turn(j + 2)
                        ring.leave(MJ - 2)

                    gather(n0)
                    each_expert(pe, n0, body)
                    sums(n0 + NE - 1, MJ - 1, False, True)
                    scatter(1, n0 + NE - 1)

                t0 = ring.t
                experts(t0, 0)
                pe.wait_ge(fullest_counted, 1)
                full = pe.value_load(flag[0:1, 0:1], min_val=0, max_val=SEQ)
                with pe.If(full > P):
                    experts(t0 + NE * MT, NE)

_INS = ["x", "norm1", "w_in", "q_norm", "k_norm", "out_norm_a", "out_norm_b", "w_out", "norm2", "w_mlp_in",
        "w_mlp_out", "final_norm", "c_2", "positions_2", "w_in_2", "w_out_2", "diff_lambda_2", "diff_subln_2",
        "w_ada_2", "b_ada_2", "g_attn_2", "g_ffn_2", "w_ff_gate_2", "w_ff_up_2", "w_ff_down_2", "w_router_2",
        "w_exp_gate_2", "w_exp_up_2", "w_exp_down_2", "g_final_2"]


def kernel(**inputs):
    import concourse.bacc as _bacc
    from concourse.bass_utils import run_bass_kernel_spmd as _run

    nc = _bacc.Bacc("TRN2", target_bir_lowering=False, num_devices=1)
    arrays = {f"in_{n}": np.ascontiguousarray(inputs[n]) for n in _INS}
    arrays["in_consts"] = constants()
    A = {n[3:]: nc.dram_tensor(n, a.shape, mybir.dt.from_np(a.dtype), kind="ExternalInput").ap()
         for n, a in arrays.items()}
    out = nc.dram_tensor("out_0", (1, SEQ, D), F32, kind="ExternalOutput").ap()
    build(nc, A, out)
    r = _run(nc, [arrays], core_ids=[0])
    return r.results[0]["out_0"]
```
